# Optimizing a Trainium2 kernel written in Bass

```python
import functools
import jax
import jax.numpy as jnp
from jax import lax
import numpy as np

D_MODEL = 1024
BATCH = 1
SEQ = 512
DEPTH = 2

GRID_W = 64
CTX_LEN = 256
EPS = 1e-6

N_BRANCH = 4
BR_W = 512
CONV_K = 31
RET_HEADS = 4
RET_DIM = BR_W // RET_HEADS
MLSTM_HEADS = 4
MLSTM_DIM = BR_W // MLSTM_HEADS
MLSTM_CONV_K = 3
MLSTM_GATES = 4 * MLSTM_HEADS
ATTN_HEADS = 8
ATTN_KV_HEADS = 2
ATTN_DIM = BR_W // ATTN_HEADS
WINDOW = 128
BLOCK = 128
CHUNK = 128
ROPE_BASE = 10000.0
NEG_INIT = -1e30
PEER_HEADS = 8
PEER_KEYS = 128
PEER_EXPERTS = PEER_KEYS * PEER_KEYS
PEER_QDIM = 256
PEER_TOPK = 16
PEER_TOKENS = 128

CONV_IN = 2 * BR_W
RET_IN = 4 * BR_W
MLSTM_IN = 4 * BR_W + MLSTM_GATES
ATTN_IN = ATTN_HEADS * ATTN_DIM + 2 * ATTN_KV_HEADS * ATTN_DIM
GATE_IN = N_BRANCH * D_MODEL
IN_SPLITS = (CONV_IN, RET_IN, MLSTM_IN, ATTN_IN, GATE_IN)
P_IN = CONV_IN + RET_IN + MLSTM_IN + ATTN_IN + GATE_IN

kernel_name = "hybrid_gated_dit_peer_block"

def split_cols(a, sizes):
    cuts = [int(s) for s in np.cumsum(sizes)[:-1]]
    return jnp.split(a, cuts, axis=-1)

def heads(a, n):
    return a.reshape(a.shape[:-1] + (n, a.shape[-1] // n))

def rmsnorm(x, g):
    xf = x.astype(jnp.float32)
    y = xf * lax.rsqrt(jnp.mean(xf * xf, axis=-1, keepdims=True) + EPS)
    return (y * g.astype(jnp.float32)).astype(x.dtype)

def _standardize(x):
    xf = x.astype(jnp.float32)
    xc = xf - jnp.mean(xf, axis=-1, keepdims=True)
    return xc * lax.rsqrt(jnp.mean(xc * xc, axis=-1, keepdims=True) + EPS)

def layernorm(x, g, b):
    return (_standardize(x) * g.astype(jnp.float32) + b.astype(jnp.float32)).astype(x.dtype)

def head_norm(y):
    z = _standardize(y)
    return z.reshape(z.shape[:-2] + (-1,))

def modulate(x, g, shift, scale):
    return rmsnorm(x, g) * (1.0 + scale) + shift

def axial_rope(x, rows, cols):
    d = x.shape[-1]
    nf = d // 4
    freqs = ROPE_BASE ** (-jnp.arange(nf, dtype=jnp.float32) / nf)

    def rot(xh, pos):
        ang = pos.astype(jnp.float32)[:, None] * freqs[None, :]
        cos = jnp.cos(ang)[None, :, None, :]
        sin = jnp.sin(ang)[None, :, None, :]
        x1, x2 = xh[..., :nf], xh[..., nf:]
        return jnp.concatenate([x1 * cos - x2 * sin, x2 * cos + x1 * sin], axis=-1)

    xf = x.astype(jnp.float32)
    out = jnp.concatenate([rot(xf[..., : d // 2], rows), rot(xf[..., d // 2:], cols)], axis=-1)
    return out.astype(x.dtype)

def depthwise_conv(x, w, b):
    k = w.shape[0]
    y = lax.conv_general_dilated(
        x, w[:, None, :].astype(x.dtype), window_strides=(1,),
        padding=[((k - 1) // 2, k // 2)],
        dimension_numbers=('NWC', 'WIO', 'NWC'),
        feature_group_count=x.shape[-1])
    return y + b.astype(x.dtype)

def retention_scan(q, k, v, s0, log_gamma):
    bsz, t, h, d = q.shape
    nc, L = t // CHUNK, CHUNK
    idx = jnp.arange(L, dtype=jnp.float32)
    diff = idx[:, None] - idx[None, :]
    lower = diff >= 0
    dmat = jnp.where(lower, jnp.exp(jnp.where(lower, diff, 0.0)[None] * log_gamma[:, None, None]), 0.0)
    q_dec = jnp.exp((idx + 1.0)[None, :] * log_gamma[:, None])
    k_dec = jnp.exp((L - 1.0 - idx)[None, :] * log_gamma[:, None])
    c_dec = jnp.exp(L * log_gamma)
    chunks = lambda a: a.reshape(bsz, nc, L, h, d).transpose(1, 0, 3, 2, 4)

    def step(s, inp):
        qc, kc, vc = inp
        att = jnp.einsum('bhid,bhjd->bhij', qc, kc) * dmat
        o = jnp.einsum('bhij,bhjd->bhid', att, vc) + q_dec[..., None] * jnp.einsum('bhid,bhde->bhie', qc, s)
        s = c_dec[:, None, None] * s + jnp.einsum('bhjd,bhje->bhde', kc * k_dec[..., None], vc)
        return s, o

    s, o = lax.scan(step, s0, (chunks(q), chunks(k), chunks(v)))
    return o.transpose(1, 0, 3, 2, 4).reshape(bsz, t, h, d), s

def mlstm_scan(q, k, v, log_i, log_f, state0):
    bsz, t, h, d = q.shape
    nc, L = t // CHUNK, CHUNK
    seq_chunks = lambda a: a.reshape(bsz, nc, L, h, d).transpose(1, 0, 3, 2, 4)
    gate_chunks = lambda a: a.reshape(bsz, nc, L, h).transpose(1, 0, 3, 2)
    tril = jnp.tril(jnp.ones((L, L), dtype=bool))

    def step(carry, inp):
        cmat, nvec, m = carry
        qc, kc, vc, ic, fc = inp
        b = jnp.cumsum(fc, axis=-1)
        logw = jnp.where(tril, b[..., :, None] - b[..., None, :] + ic[..., None, :], -jnp.inf)
        inter = b + m[..., None]
        m_t = jnp.maximum(inter, jnp.max(logw, axis=-1))
        s = jnp.einsum('bhid,bhjd->bhij', qc, kc) * jnp.exp(logw - m_t[..., None])
        w_prev = jnp.exp(inter - m_t)
        num = jnp.einsum('bhij,bhjd->bhid', s, vc) + w_prev[..., None] * jnp.einsum('bhid,bhde->bhie', qc, cmat)
        den = jnp.sum(s, axis=-1) + w_prev * jnp.einsum('bhid,bhd->bhi', qc, nvec)
        hc = num / jnp.maximum(jnp.abs(den), jnp.exp(-m_t))[..., None]
        b_end = b[..., -1]
        log_wk = b_end[..., None] - b + ic
        m_new = jnp.maximum(b_end + m, jnp.max(log_wk, axis=-1))
        decay = jnp.exp(b_end + m - m_new)
        kw = kc * jnp.exp(log_wk - m_new[..., None])[..., None]
        cmat = decay[..., None, None] * cmat + jnp.einsum('bhjd,bhje->bhde', kw, vc)
        nvec = decay[..., None] * nvec + jnp.sum(kw, axis=2)
        return (cmat, nvec, m_new), hc

    state, hs = lax.scan(step, state0, (seq_chunks(q), seq_chunks(k), seq_chunks(v),
                                        gate_chunks(log_i), gate_chunks(log_f)))
    return hs.transpose(1, 0, 3, 2, 4).reshape(bsz, t, h, d), state

def run_bidir(scan_f, scan_b, ctx_f, lat_f, ctx_b, lat_b, state0):
    flip = lambda arrs: tuple(jnp.flip(a, axis=1) for a in arrs)
    oc_f, st_f = scan_f(*ctx_f, state0)
    ol_f, _ = scan_f(*lat_f, st_f)
    oc_b, st_b = scan_b(*flip(ctx_b), state0)
    ol_b, _ = scan_b(*flip(lat_b), st_b)
    return oc_f + jnp.flip(oc_b, axis=1), ol_f + jnp.flip(ol_b, axis=1)

def softmax_with_sink(s, sink):
    sk = jnp.broadcast_to(sink[None, :, :, None, None], s.shape[:-1] + (1,))
    return jax.nn.softmax(jnp.concatenate([s, sk], axis=-1), axis=-1)[..., :-1]

def window_attention(q, k, v, k_ctx, v_ctx, sink):
    dt = q.dtype
    bsz, s_len, hq, d = q.shape
    hkv = k.shape[2]
    g = hq // hkv
    nb = s_len // BLOCK
    scale = d ** -0.5
    sink_l = sink.astype(jnp.float32).reshape(hkv, g)
    qb = q.reshape(bsz, nb, BLOCK, hkv, g, d).transpose(1, 0, 2, 3, 4, 5)

    def band(a):
        ap = jnp.pad(a, ((0, 0), (BLOCK, BLOCK), (0, 0), (0, 0))).reshape(bsz, nb + 2, BLOCK, hkv, d)
        return jnp.concatenate([ap[:, :-2], ap[:, 1:-1], ap[:, 2:]], axis=2).transpose(1, 0, 2, 3, 4)

    kb, vb = band(k), band(v)
    blk = jnp.arange(nb)[:, None, None]
    qpos = blk * BLOCK + jnp.arange(BLOCK)[None, :, None]
    kpos = (blk - 1) * BLOCK + jnp.arange(3 * BLOCK)[None, None, :]
    mask = (jnp.abs(qpos - kpos) <= WINDOW) & (kpos >= 0) & (kpos < s_len)
    n_loc = 3 * BLOCK

    def block(args):
        qi, ki, vi, mi = args
        s_loc = jnp.einsum('bqhgd,bkhd->bhgqk', qi, ki).astype(jnp.float32) * scale
        s_loc = jnp.where(mi[None, None, None], s_loc, -jnp.inf)
        s_ctx = jnp.einsum('bqhgd,bkhd->bhgqk', qi, k_ctx).astype(jnp.float32) * scale
        p = softmax_with_sink(jnp.concatenate([s_loc, s_ctx], axis=-1), sink_l)
        return (jnp.einsum('bhgqk,bkhd->bqhgd', p[..., :n_loc].astype(dt), vi)
                + jnp.einsum('bhgqk,bkhd->bqhgd', p[..., n_loc:].astype(dt), v_ctx))

    o = lax.map(block, (qb, kb, vb, mask))
    return o.transpose(1, 0, 2, 3, 4, 5).reshape(bsz, s_len, hq * d)

def context_attention(q, k, v, sink):
    dt = q.dtype
    bsz, n, hq, d = q.shape
    hkv = k.shape[2]
    g = hq // hkv
    s = jnp.einsum('bqhgd,bkhd->bhgqk', q.reshape(bsz, n, hkv, g, d), k).astype(jnp.float32) * d ** -0.5
    p = softmax_with_sink(s, sink.astype(jnp.float32).reshape(hkv, g)).astype(dt)
    return jnp.einsum('bhgqk,bkhd->bqhgd', p, v).reshape(bsz, n, hq * d)

def merge(ys, gates_pre, w_branch, w_out):
    gates = jnp.split(gates_pre, N_BRANCH, axis=-1)
    acc = jax.nn.sigmoid(gates[0]) * (ys[0] @ w_branch[0])
    for i in range(1, N_BRANCH):
        acc = acc + jax.nn.sigmoid(gates[i]) * (ys[i] @ w_branch[i])
    return acc @ w_out

def token_mixer(h, hc, rows, cols, w_in, conv_w, conv_b, conv_ln_g, conv_ln_b, ret_decay,
                mlstm_conv_w, mlstm_conv_b, mlstm_gate_b, attn_sink, w_branch, w_out, with_ctx_out):
    dt = h.dtype
    bsz = h.shape[0]
    conv_l, ret_l, mls_l, att_l, gate_l = split_cols(h @ w_in, IN_SPLITS)
    conv_c, ret_c, mls_c, att_c, gate_c = split_cols(hc @ w_in, IN_SPLITS)

    def conformer_conv(u):
        a, g = jnp.split(u, 2, axis=-1)
        y = depthwise_conv(a * jax.nn.sigmoid(g), conv_w, conv_b)
        return jax.nn.silu(layernorm(y, conv_ln_g, conv_ln_b))

    def ret_inputs(u, rotate):
        q, k, v, g = jnp.split(u, 4, axis=-1)
        q, k, v = heads(q, RET_HEADS), heads(k, RET_HEADS), heads(v, RET_HEADS)
        if rotate:
            q, k = axial_rope(q, rows, cols), axial_rope(k, rows, cols)
        return (q.astype(jnp.float32), k.astype(jnp.float32) * RET_DIM ** -0.5, v.astype(jnp.float32)), g

    ret_in_l, ret_g_l = ret_inputs(ret_l, True)
    ret_in_c, ret_g_c = ret_inputs(ret_c, False)
    log_gamma = jax.nn.log_sigmoid(ret_decay.astype(jnp.float32))
    s0 = jnp.zeros((bsz, RET_HEADS, RET_DIM, RET_DIM), jnp.float32)
    ret_y_c, ret_y_l = run_bidir(functools.partial(retention_scan, log_gamma=log_gamma[0]),
                                 functools.partial(retention_scan, log_gamma=log_gamma[1]),
                                 ret_in_c, ret_in_l, ret_in_c, ret_in_l, s0)

    def ret_out(y, g):
        return head_norm(y).astype(dt) * jax.nn.silu(g)

    def mlstm_inputs(u):
        qk, v, o, gates = split_cols(u, (2 * BR_W, BR_W, BR_W, MLSTM_GATES))
        qk = jax.nn.silu(depthwise_conv(qk, mlstm_conv_w, mlstm_conv_b))
        q, k = jnp.split(qk, 2, axis=-1)
        q, k, v = (heads(a, MLSTM_HEADS).astype(jnp.float32) for a in (q, k, v))
        k = k * MLSTM_DIM ** -0.5
        gi_f, gf_f, gi_b, gf_b = jnp.split(
            gates.astype(jnp.float32) + mlstm_gate_b.reshape(-1).astype(jnp.float32), 4, axis=-1)
        fwd = (q, k, v, gi_f, jax.nn.log_sigmoid(gf_f))
        bwd = (q, k, v, gi_b, jax.nn.log_sigmoid(gf_b))
        return fwd, bwd, o

    mls_f_l, mls_b_l, mls_o_l = mlstm_inputs(mls_l)
    mls_f_c, mls_b_c, mls_o_c = mlstm_inputs(mls_c)
    m_state0 = (jnp.zeros((bsz, MLSTM_HEADS, MLSTM_DIM, MLSTM_DIM), jnp.float32),
                jnp.zeros((bsz, MLSTM_HEADS, MLSTM_DIM), jnp.float32),
                jnp.full((bsz, MLSTM_HEADS), NEG_INIT, jnp.float32))
    mls_y_c, mls_y_l = run_bidir(mlstm_scan, mlstm_scan, mls_f_c, mls_f_l, mls_b_c, mls_b_l, m_state0)

    def mlstm_out(y, o):
        return head_norm(y).astype(dt) * jax.nn.sigmoid(o)

    def attn_inputs(u):
        q, k, v = split_cols(u, (ATTN_HEADS * ATTN_DIM, ATTN_KV_HEADS * ATTN_DIM, ATTN_KV_HEADS * ATTN_DIM))
        return heads(q, ATTN_HEADS), heads(k, ATTN_KV_HEADS), heads(v, ATTN_KV_HEADS)

    q_l, k_l, v_l = attn_inputs(att_l)
    q_c, k_c, v_c = attn_inputs(att_c)
    q_l, k_l = axial_rope(q_l, rows, cols), axial_rope(k_l, rows, cols)
    att_y_l = window_attention(q_l, k_l, v_l, k_c, v_c, attn_sink)

    out_l = merge((conformer_conv(conv_l), ret_out(ret_y_l, ret_g_l), mlstm_out(mls_y_l, mls_o_l), att_y_l),
                  gate_l, w_branch, w_out)
    if not with_ctx_out:
        return out_l, None
    att_y_c = context_attention(q_c, k_c, v_c, attn_sink)
    out_c = merge((conformer_conv(conv_c), ret_out(ret_y_c, ret_g_c), mlstm_out(mls_y_c, mls_o_c), att_y_c),
                  gate_c, w_branch, w_out)
    return out_l, out_c

def peer_ffn(h, wq, keys, u, v):
    dt = h.dtype
    bsz, t, d = h.shape
    half = PEER_QDIM // 2
    tokens = h.reshape(-1, PEER_TOKENS, d)
    keys32 = keys.astype(jnp.float32)

    def block(xb):
        q = (xb @ wq).astype(jnp.float32).reshape(-1, PEER_HEADS, 2, half)
        s = jnp.einsum('nhcd,ckd->nhck', q, keys32)
        sv, si = lax.top_k(s, PEER_TOPK)
        cand = sv[:, :, 0, :, None] + sv[:, :, 1, None, :]
        cv, ci = lax.top_k(cand.reshape(cand.shape[:2] + (-1,)), PEER_TOPK)
        i1 = jnp.take_along_axis(si[:, :, 0], ci // PEER_TOPK, axis=-1)
        i2 = jnp.take_along_axis(si[:, :, 1], ci % PEER_TOPK, axis=-1)
        expert = i1 * PEER_KEYS + i2
        gate = jax.nn.softmax(cv, axis=-1)
        u_sel = jnp.take(u, expert, axis=0)
        v_sel = jnp.take(v, expert, axis=0)
        act = jax.nn.gelu(jnp.einsum('nd,nhkd->nhk', xb, u_sel).astype(jnp.float32), approximate=False)
        return jnp.einsum('nhk,nhkd->nd', (gate * act).astype(dt), v_sel)

    return lax.map(block, tokens).reshape(bsz, t, d)

def setup_inputs(seed: int = 0) -> dict:
    key = jax.random.key(seed)
    ks = jax.random.split(key, 26)
    nrm = lambda k, shape, s: jax.random.normal(k, shape, jnp.float32) * s
    D = D_MODEL
    ret_init = jnp.log(2.0 ** (5.0 + jnp.arange(RET_HEADS, dtype=jnp.float32)) - 1.0)
    f_init = jnp.linspace(3.0, 6.0, MLSTM_HEADS, dtype=jnp.float32)
    z_init = jnp.zeros((MLSTM_HEADS,), jnp.float32)
    gate_init = jnp.stack([z_init, f_init, z_init, f_init])
    return {
        "x": nrm(ks[0], (BATCH, SEQ, D), 1.0),
        "c": nrm(ks[1], (BATCH, D), 1.0),
        "ctx": nrm(ks[2], (BATCH, CTX_LEN, D), 1.0),
        "c_ctx": nrm(ks[3], (D,), 1.0),
        "mod_w": nrm(ks[4], (DEPTH, D, 6 * D), D ** -0.5),
        "mod_b": nrm(ks[5], (DEPTH, 6 * D), 0.02),
        "norm1_g": 1.0 + nrm(ks[6], (DEPTH, D), 0.02),
        "norm2_g": 1.0 + nrm(ks[7], (DEPTH, D), 0.02),
        "w_in": nrm(ks[8], (DEPTH, D, P_IN), D ** -0.5),
        "conv_w": nrm(ks[9], (DEPTH, CONV_K, BR_W), CONV_K ** -0.5),
        "conv_b": nrm(ks[10], (DEPTH, BR_W), 0.02),
        "conv_ln_g": 1.0 + nrm(ks[11], (DEPTH, BR_W), 0.02),
        "conv_ln_b": nrm(ks[12], (DEPTH, BR_W), 0.02),
        "ret_decay": ret_init + nrm(ks[13], (DEPTH, 2, RET_HEADS), 0.1),
        "mlstm_conv_w": nrm(ks[14], (DEPTH, MLSTM_CONV_K, 2 * BR_W), MLSTM_CONV_K ** -0.5),
        "mlstm_conv_b": nrm(ks[15], (DEPTH, 2 * BR_W), 0.02),
        "mlstm_gate_b": gate_init + nrm(ks[16], (DEPTH, 4, MLSTM_HEADS), 0.1),
        "attn_sink": nrm(ks[17], (DEPTH, ATTN_HEADS), 0.5),
        "w_branch": nrm(ks[18], (DEPTH, N_BRANCH, BR_W, D), BR_W ** -0.5),
        "w_out": nrm(ks[19], (DEPTH, D, D), D ** -0.5),
        "peer_wq": nrm(ks[20], (DEPTH, D, PEER_HEADS * PEER_QDIM), D ** -0.5),
        "peer_keys": nrm(ks[21], (DEPTH, 2, PEER_KEYS, PEER_QDIM // 2), (PEER_QDIM // 2) ** -0.5),
        "peer_u": nrm(ks[22], (DEPTH, PEER_EXPERTS, D), D ** -0.5),
        "peer_v": nrm(ks[23], (DEPTH, PEER_EXPERTS, D), PEER_HEADS ** -0.5),
        "final_g": 1.0 + nrm(ks[24], (D,), 0.02),
    }

def reference(x, c, ctx, c_ctx, mod_w, mod_b, norm1_g, norm2_g, w_in, conv_w, conv_b, conv_ln_g, conv_ln_b,
              ret_decay, mlstm_conv_w, mlstm_conv_b, mlstm_gate_b, attn_sink, w_branch, w_out,
              peer_wq, peer_keys, peer_u, peer_v, final_g):
    n_rows = x.shape[1] // GRID_W
    rows = jnp.repeat(jnp.arange(n_rows, dtype=jnp.int32), GRID_W)
    cols = jnp.tile(jnp.arange(GRID_W, dtype=jnp.int32), n_rows)
    s_lat = jax.nn.silu(c)
    s_ctx = jax.nn.silu(c_ctx)
    for l in range(DEPTH):
        last = l == DEPTH - 1
        mod_l = (s_lat @ mod_w[l] + mod_b[l])[:, None, :]
        mod_c = (s_ctx @ mod_w[l] + mod_b[l])[None, None, :]
        sh1, sc1, ga1, sh2, sc2, ga2 = jnp.split(mod_l, 6, axis=-1)
        csh1, csc1, cga1, csh2, csc2, cga2 = jnp.split(mod_c, 6, axis=-1)
        o_lat, o_ctx = token_mixer(
            modulate(x, norm1_g[l], sh1, sc1), modulate(ctx, norm1_g[l], csh1, csc1), rows, cols,
            w_in[l], conv_w[l], conv_b[l], conv_ln_g[l], conv_ln_b[l], ret_decay[l],
            mlstm_conv_w[l], mlstm_conv_b[l], mlstm_gate_b[l], attn_sink[l], w_branch[l], w_out[l],
            not last)
        x = x + ga1 * o_lat
        x = x + ga2 * peer_ffn(modulate(x, norm2_g[l], sh2, sc2), peer_wq[l], peer_keys[l], peer_u[l], peer_v[l])
        if not last:
            ctx = ctx + cga1 * o_ctx
            ctx = ctx + cga2 * peer_ffn(modulate(ctx, norm2_g[l], csh2, csc2),
                                        peer_wq[l], peer_keys[l], peer_u[l], peer_v[l])
    return rmsnorm(x, final_g)


_drawn_inputs = setup_inputs


def setup_inputs(seed=0):
    import zlib

    import numpy as np

    out = dict(_drawn_inputs(seed))
    spreads = {}
    factors = {'conv_b': 3.284,
     'conv_ln_g': 3.452,
     'conv_ln_b': 3.807,
     'mlstm_conv_b': 30.029,
     'attn_sink': 21.691,
     'final_g': 8.129,
     'norm2_g': 2.744}
    for name, (base, spread) in spreads.items():
        noise = np.random.default_rng([zlib.crc32(name.encode()), seed]).standard_normal(out[name].shape)
        drawn = base * np.exp(spread * noise) if base else spread * noise
        out[name] = jnp.asarray(drawn.astype(out[name].dtype))
    for name, factor in factors.items():
        out[name] = (out[name] * factor).astype(out[name].dtype)
    return out
```

```python
from contextlib import ExitStack

import numpy as np
import concourse.bass as bass
from concourse import mybir

P = 128
D = 1024
KD = D // P
CTX, LAT = 256, 512
TOK = CTX + LAT
NB = TOK // P
CB = CTX // P
DEPTH = 2
GRID_W = 64
BR = 512
BB = BR // P
NH = 4
TAPS = 31
AH, AD, AKV = 8, 64, 2
EPS = 1e-6
NEG = -1e30
HEADS, TOPK, KEYS = 8, 16, 128
EXPERTS = KEYS * KEYS
SLOTS = HEADS * TOPK
P_IN = 10000
C_CONV_A, C_CONV_G = 0, 512
C_RQ, C_RK, C_RV, C_RG = 1024, 1536, 2048, 2560
C_MQ, C_MK, C_MV, C_MO, C_MG = 3072, 3584, 4096, 4608, 5120
C_AQ, C_AK = 5136, 5648
C_GATE = 5904
W = 256
RING = 4
CPAD = TOK + 4 * (TAPS // 2)
MPAD = TOK + 4
BANKS = 6
URING, VRING, DRING = 8, 8, 8

F32 = mybir.dt.float32
U32 = mybir.dt.uint32
ALU = mybir.AluOpType
ACT = mybir.ActivationFunctionType
AX = mybir.AxisListType.X

SEG_CTX, SEG_LAT = (0, CTX), (CTX, LAT)


def out_segs(l):
    return [SEG_CTX, SEG_LAT] if l < DEPTH - 1 else [SEG_LAT]


def out_blocks(l):
    return list(range(NB)) if l < DEPTH - 1 else list(range(CB, NB))


ALL_SEGS = [SEG_CTX, SEG_LAT]

CONST = {}


def const_table():
    parts, at = [], 0

    def put(name, a):
        nonlocal at
        a = np.broadcast_to(np.asarray(a, np.float32), (P, a.shape[-1]))
        CONST[name] = (at, a.shape[-1])
        parts.append(a)
        at += a.shape[-1]

    i = np.arange(P)
    put("ident", np.eye(P))
    for name, dim in (("R", P), ("A", AD)):
        nf = dim // 4
        freqs = np.float32(10000.0) ** (-np.arange(nf, dtype=np.float32) / np.float32(nf))
        d = i % dim
        first = (d % (2 * nf)) < nf
        pos = np.where((d < dim // 2)[:, None], (np.arange(LAT) // GRID_W)[None], (np.arange(LAT) % GRID_W)[None])
        ang = pos.astype(np.float32) * freqs[d % nf][:, None].astype(np.float32)
        put("cos" + name, np.cos(ang))
        put("sin" + name, np.sin(ang))
        perm = np.zeros((P, P))
        for p in range(P):
            perm[p + nf if first[p] else p - nf, p] = -1.0 if first[p] else 1.0
        put("perm" + name, perm)
    put("until", (i[:, None] <= i[None]) * 1.0)
    put("since", (i[:, None] >= i[None]) * 1.0)
    put("ahead", np.maximum(i[None] - i[:, None], 0))
    put("behind", np.maximum(i[:, None] - i[None], 0))
    put("maskprev", np.where(i[None] >= i[:, None], 0.0, NEG))
    put("masknext", np.where(i[None] <= i[:, None], 0.0, NEG))
    put("ones", np.ones((P, P)))
    put("mean512", np.full((P, P), 1.0 / BR))
    put("mean128", np.full((P, P), 1.0 / P))
    put("iota16", np.arange(TOPK)[None])
    put("rowup", (i + 1.0)[None])
    put("rowdown", (float(P) - i)[None])
    put("coldown", (P - 1.0 - i)[:, None])
    put("colup", (i * 1.0)[:, None])
    return np.concatenate(parts, axis=1)


const_table()
NCONST = sum(n for _, n in CONST.values())

PAR, _at = {}, 0
for _n, _w in (("n1g", KD), ("conv_w", BB * TAPS), ("conv_b", BB), ("ln_g", BB), ("ln_b", BB),
               ("mconv_w", 8 * 3), ("mconv_b", 8)):
    PAR[_n] = (_at, _w)
    _at += _w
NPAR = _at


def scan_order(d):
    return list(range(NB)) if d == 0 else list(range(CB - 1, -1, -1)) + list(range(NB - 1, CB - 1, -1))


def pad_at(t0):
    h = TAPS // 2
    return h if t0 == 0 else h + CTX + 2 * h


def mpad_at(t0):
    return 1 if t0 == 0 else 1 + CTX + 2


def chunk_slice(d, c):
    if d == 0:
        return slice(c * P, (c + 1) * P)
    return slice((c + 1) * P - 1, c * P - 1 if c else None, -1)


def gslot(l, j, i, m, t0):
    segs = out_segs(l)
    return (((j * 4 + i) * 2 + m) * len(segs) + [s[0] for s in segs].index(t0)) % 4


def local_blocks(t):
    return [] if t < CB else [j for j in (t - 1, t, t + 1) if CB <= j < NB]


def peer_calls(l):
    return [(0, CB, 0), (CB, NB - CB, CB)] if l == 0 else [(CB, NB - CB, NB + (l - 1) * (NB - CB))]


class Flow:

    def __init__(self, nc, ctx, known):
        self.nc, self.ctx, self.known = nc, ctx, known
        self.sems, self.count, self.marks = {}, {}, {}

    def sem(self, name):
        if name not in self.sems:
            self.sems[name] = self.ctx.enter_context(self.nc.semaphore(name))
            self.count[name] = 0
        return self.sems[name]

    def done(self, ins, sem, step=None, by=1):
        ins.then_inc(self.sem(sem), by)
        self.count[sem] += by
        if step is not None:
            self.marks[step] = (sem, self.count[sem])
        return ins

    def at(self, *step):
        sem, value = self.known[step] if self.known else ("first_building", 1)
        return self.sem(sem), value

    def mark(self, step, sem):
        self.sem(sem)
        self.marks[step] = (sem, self.count[sem])


def build(nc, ins, out, known):
    ctx = ExitStack()
    with ctx:
        fl = Flow(nc, ctx, known)
        at = fl.at
        arena = ctx.enter_context(nc.sbuf_tensor("arena", [P, 53100], F32))
        top = [0]

        def take(n):
            a = arena[:, top[0]:top[0] + n]
            top[0] += n
            assert top[0] <= 53100, top[0]
            return a

        banks = [ctx.enter_context(nc.psum_tensor(f"bank{i}", [P, 512], F32)) for i in range(8)]

        X = take(NB * D)
        HT = take(KD * TOK)
        YS = take(4 * BB * TOK)
        WR = take(RING * KD * W)
        CT = take(NCONST)
        PR = take(NPAR)
        SM = take(460)
        WK0 = top[0]
        WKN = 53100 - WK0
        WK = arena[:, WK0:53100]

        Xb = X.rearrange("p (b d) -> p b d", b=NB)
        HTk = HT.rearrange("p (k t) -> p k t", k=KD)
        YSb = YS.rearrange("p (b t) -> p b t", b=4 * BB)
        WRr = WR.rearrange("p (r n) -> p r n", r=RING)

        def const(name):
            at, n = CONST[name]
            return CT[:, at:at + n]

        def par(name):
            at, n = PAR[name]
            return PR[:, at:at + n]

        sm_at = [0]

        def small(n):
            a = SM[:, sm_at[0]:sm_at[0] + n]
            sm_at[0] += n
            assert sm_at[0] <= 460
            return a

        SIL = small(KD * 2)
        SC1, SH1 = small(2 * KD), small(2 * KD)
        LG, KDEC, CDEC = small(8), small(8), small(8)
        SINK = small(AH)
        GB = small(2)
        SSQ, RSQ, RSB = small(NB), small(NB), small(NB)
        T8 = [small(8) for _ in range(3)]
        AW = [small(8) for _ in range(6)]
        KEYT = small(2 * KEYS)

        ident = const("ident")

        def work(*sizes):
            at, got = 0, []
            for n in sizes:
                got.append(WK[:, at:at + n])
                at += n
            assert at <= WKN, (at, WKN)
            return got

        def blocks4(a, b=BB):
            return a.rearrange("p (b t) -> p b t", b=b)

        def conv_work():
            cp, y, sg, sq, rs = work(BB * CPAD, BB * TOK, 2 * TOK, BB * TOK, TOK)
            return blocks4(cp), blocks4(y), blocks4(sg, 2), blocks4(sq), rs

        def ret_work():
            q, k, v_, raw, dec, dtmp, qdec, att, qd, kd = work(BB * TOK, BB * TOK, NB * BR, 2 * LAT, BR, BR, 2 * BR,
                                                               BR, 2 * BR, BR)
            st = YS[:, 2 * BB * TOK:4 * BB * TOK]
            return dict(Q=blocks4(q), K=blocks4(k), V=blocks4(v_, NB), raw=blocks4(raw, 2), dec=blocks4(dec),
                        dtmp=blocks4(dtmp), qdec=qdec.rearrange("p (d h i) -> p d h i", d=2, h=NH), att=blocks4(att),
                        qd=qd.rearrange("p (d h i) -> p d h i", d=2, h=NH), kd=blocks4(kd),
                        kt=blocks4(YS[:, BB * TOK:2 * BB * TOK], NB),
                        S=st.rearrange("p (n h e) -> p n h e", n=2 * NB, h=NH),
                        sq=blocks4(st[:, 0:BB * TOK]), rs=blocks4(st[:, BB * TOK:]), g=blocks4(k))

        def mlstm_work():
            q, k, v_, pad, c_, n_, cols, m0, bc = work(BB * TOK, BB * TOK, NB * BR, 2 * MPAD, 2 * BR, 2 * NH, NB * P, 8,
                                                       2 * 3 * BR)
            ys = YS[:, 2 * BB * TOK:4 * BB * TOK]
            row = [ys[:, x * TOK:(x + 1) * TOK] for x in range(8)]
            t = [blocks4(ys[:, BB * TOK + x * BR:BB * TOK + (x + 1) * BR]) for x in range(5)]
            return dict(Q=blocks4(q), K=blocks4(k), V=blocks4(v_, NB), pad=blocks4(pad, 2),
                        C=c_.rearrange("p (x h e) -> p x h e", x=2, h=NH), N=blocks4(n_, 2), cols=blocks4(cols, NB),
                        m0=m0, bc=blocks4(bc, 2), em=bc[:, 0:TOK], gw=blocks4(bc[:, TOK:TOK + KD * P], KD),
                        **dict(zip(("i", "f", "b", "mt", "t", "a", "m", "wp"), row)),
                        **dict(zip(("e", "s", "qw", "nb", "kw"), t)),
                        den=ys[:, BB * TOK + 5 * BR:BB * TOK + 6 * BR],
                        sq=blocks4(v_), rs=blocks4(bc), g=blocks4(k), Kf=k)

        def attn_work():
            q, k, v_, raw, s_, p_, pt, y = work(BB * TOK, TOK, NB * P, 2 * LAT, 2 * 5 * P, 2 * 5 * P, 2 * 5 * P, 2 * BR)
            return dict(Q=blocks4(q), K=k, V=blocks4(v_, NB), raw=blocks4(raw, 2), S=blocks4(s_, 2), P=blocks4(p_, 2),
                        PT=blocks4(pt, 2), Y=blocks4(y, 2))

        def merge_work():
            acc, gs, prd, ga, tmp = work(KD * TOK, 4 * LAT, LAT, 2 * D, 2 * W)
            return blocks4(acc, KD), blocks4(gs, 4), prd, ga, tmp

        def route_work():
            (h2, idx, gate, ga, s_, s2, sv, si, sif, cand, cand2, cv, ci, cu, cf, i1, i2, ce, cs) = work(
                NB * D, NB * SLOTS, NB * SLOTS, 2 * D, 2 * HEADS * KEYS, KEYS, 256, 256, 256, 256, 256,
                SLOTS, SLOTS, SLOTS, SLOTS, SLOTS, SLOTS, SLOTS, HEADS)
            return dict(idx=blocks4(idx.bitcast(U32), NB), gate=blocks4(gate, NB), s=blocks4(s_, 16), s2=s2,
                        sv=blocks4(sv, 16), si=si.bitcast(U32), si3=blocks4(si.bitcast(U32), 16), siff=sif,
                        sif=blocks4(sif, 16), cand=cand, cand2=cand2, cv=blocks4(cv, HEADS), cif=ci.bitcast(U32),
                        ci=blocks4(ci.bitcast(U32), HEADS), cu=cu.bitcast(U32), cf=cf, i1=i1, i2=i2,
                        ce=blocks4(ce, HEADS), csum=cs, oh=blocks4(HT[:, 0:SLOTS * TOPK], SLOTS))

        def peer_work():
            h2, idx, gate, ga, hb, ib, gb, dots, ac, w_, y, dg = work(
                NB * D, NB * SLOTS, NB * SLOTS, 2 * D, D, SLOTS, SLOTS, SLOTS, SLOTS, SLOTS, D, DRING * P)
            ring = [YS[:, x * D:(x + 1) * D] for x in range(12)] + [HT[:, x * D:(x + 1) * D] for x in range(6)]
            return dict(H2=h2, idx=idx.bitcast(U32), gate=gate, ga=ga, hb=hb, idxb=ib.bitcast(U32), gateb=gb, dots=dots,
                        act=ac, w=w_, y=y, diag=blocks4(dg, DRING), u=ring[:URING], v=ring[URING:URING + VRING])

        w_in = ins["w_in"]
        modr = ins["mod_rows"]
        rowsd = ins["mlstm_rows"]

        def w_view(a, k):
            return a.rearrange("(k p) n -> p k n", p=P)

        PLAN = []

        def plan(name, parts):
            PLAN.append((name, parts))

        def whole(src, k=KD):
            return [(lambda w: w[:, 0:k * W].rearrange("p (k n) -> p k n", k=k), src)]

        for l in range(DEPTH):
            for c in range(6 * D // W):
                plan(("mod", l, c), whole(w_view(ins["mod_w"][l], KD)[:, :, c * W:(c + 1) * W]))
        for l in range(DEPTH):
            v = w_view(w_in[l], KD)

            def cols(c0):
                return whole(v[:, :, c0:c0 + W])

            for h in range(2):
                plan(("conv_g", l, h), cols(C_CONV_G + h * W))
                plan(("conv_a", l, h), cols(C_CONV_A + h * W))
            for tag, c0 in (("rk", C_RK), ("rv", C_RV), ("rq", C_RQ), ("rg", C_RG),
                            ("mgate", None), ("mq", C_MQ), ("mk", C_MK), ("mv", C_MV), ("mo", C_MO)):
                if tag == "mgate":
                    plan((tag, l, 0), [(lambda w: w[:, 0:KD * 16].rearrange("p (k n) -> p k n", k=KD),
                                        v[:, :, C_MG:C_MG + 16])])
                    continue
                for h in range(2):
                    plan((tag, l, h), cols(c0 + h * W))
            plan(("akv", l, 0), cols(C_AK))
            for h in range(2):
                plan(("aq", l, h), [
                    ((lambda w, b=b, g=g: w[:, 0:KD * W].rearrange("p (k n) -> p k n", k=KD)
                      [:, :, b * P + g * AD:b * P + (g + 1) * AD]),
                     v[:, :, C_AQ + (g * 4 + 2 * h + b) * AD:C_AQ + (g * 4 + 2 * h + b + 1) * AD])
                    for b in range(2) for g in range(2)])
            for j in range(D // W):
                for i in range(4):
                    plan(("gate", l, j, i), cols(C_GATE + i * D + j * W))
                    plan(("branch", l, j, i), whole(w_view(ins["w_branch"][l, i], BB)[:, :, j * W:(j + 1) * W], BB))
            for j in range(D // W):
                plan(("out", l, j), whole(w_view(ins["w_out"][l], KD)[:, :, j * W:(j + 1) * W]))
            for j in range(HEADS * 256 // W):
                plan(("wq", l, j), whole(w_view(ins["peer_wq"][l], KD)[:, :, j * W:(j + 1) * W]))
        SLOT = {name: n for n, (name, _) in enumerate(PLAN)}

        stage_names = ["mod"]
        for l in range(DEPTH):
            stage_names += [(s, l) for s in ("norm", "conv", "ret", "mlstm", "attn", "merge", "out", "peernorm",
                                             "peerq", "route", "peer")]
        stage_names.append("final")
        ENG = ("tensor", "vector", "scalar", "gpsimd")

        class Engine:

            def __init__(self, eng, name):
                self.eng, self.name, self.sem, self.first = eng, name, None, True

            def stage(self, s):
                if self.sem is not None:
                    self.finish()
                n = stage_names.index(s)
                label = s if isinstance(s, str) else f"{s[0]}{s[1]}"
                self.stg, self.sem = s, f"{label}_{self.name}"
                fl.sem(self.sem)
                for other in ENG if n else ():
                    self.eng.wait_ge(*at("end", other, stage_names[n - 1]))

            def finish(self):
                fl.mark(("end", self.name, self.stg), self.sem)
                if self.stg[0] == "peer" and self.name == "vector":
                    b0, nb, base = peer_calls(self.stg[1])[-1]
                    fl.sem("residual_added")
                    fl.marks[("end", self.name, self.stg)] = ("residual_added", base + nb + 1)

            def step(self, *step):
                fl.count[self.sem] += 1
                if step:
                    fl.marks[step] = (self.sem, fl.count[self.sem])
                return fl.sem(self.sem), 1

            def latest(self):
                return fl.sem(self.sem), fl.count[self.sem]

        AW_EPS = small(1)
        block = ctx.enter_context(nc.Block())
        banks_of = {} if known is None else known["banks"]
        order = []

        def bank_of(name):
            return banks[banks_of[name]]

        @block.tensor
        def _(eng):
            pe = Engine(eng, "tensor")
            mm = nc.tensor.matmul

            def bank(name):
                g = len(order)
                order.append(name)
                banks_of[name] = g % BANKS
                if g >= BANKS:
                    eng.wait_ge(*at("read", order[g - BANKS]))
                return banks[g % BANKS]

            def weight(name, k=KD):
                n = SLOT[name]
                eng.wait_ge(*at("loaded", name))
                return WRr[:, n % RING, 0:k * W].rearrange("p (k n) -> p k n", k=k)

            def used(name):
                fl.mark(("used", name), pe.sem)

            def project(tag, l, h, segs):
                w = weight((tag, l, h))
                for m in range(2):
                    for t0, n in segs:
                        b = bank((tag, l, 2 * h + m, t0))
                        for k in range(KD):
                            i = mm(b[:, 0:n], w[:, k, m * P:(m + 1) * P], HTk[:, k, t0:t0 + n],
                                   start=(k == 0), stop=(k == KD - 1))
                        i.then_inc(*pe.step("full", (tag, l, 2 * h + m, t0)))
                used((tag, l, h))

            def project_tok(tag, l, h, c0, n):
                w = weight((tag, l, h))
                for t in range(NB):
                    b = bank((tag + "_tok", l, h, t))
                    for k in range(KD):
                        i = mm(b[:, 0:n], HTk[:, k, t * P:(t + 1) * P], w[:, k, c0:c0 + n],
                               start=(k == 0), stop=(k == KD - 1))
                    i.then_inc(*pe.step("full", (tag + "_tok", l, h, t)))

            def rotate(tag, l, ms, perm, src):
                for m in ms:
                    b = bank((tag + "_rot", l, m))
                    eng.wait_ge(*at(tag + "_raw", l, m))
                    mm(b[:, :], const(perm), src(m), start=True, stop=True).then_inc(*pe.step("full", (tag + "_rot", l, m)))

            def norm_sums(tag, l, groups, y, sq, mean):
                for what, src in (("mean", y), ("var", sq)):
                    for t0, n in out_segs(l):
                        for g, blocks in enumerate(groups):
                            b = bank((tag, what, l, g, t0))
                            eng.wait_ge(*at(tag + "_" + what, l, g, t0))
                            for j, m in enumerate(blocks):
                                i = mm(b[:, 0:n], const(mean), src(m, t0, n), start=(j == 0), stop=(j == len(blocks) - 1))
                            i.then_inc(*pe.step("full", (tag, what, l, g, t0)))

            pe.stage("mod")
            eng.wait_ge(*at("params"))
            eng.wait_ge(*at("silu_c"))
            for l in range(DEPTH):
                for c in range(6 * D // W):
                    w = weight(("mod", l, c))
                    b = bank(("mod", l, c))
                    for k in range(KD):
                        i = mm(b[0:2, 0:W], SIL[:, 2 * k:2 * k + 2], w[:, k, :], start=(k == 0), stop=(k == KD - 1))
                    i.then_inc(*pe.step("full", ("mod", l, c)))
                    used(("mod", l, c))

            for l in range(DEPTH):
                pe.stage(("norm", l))
                xn = work(D, D)
                for t in range(NB):
                    for half in range(2):
                        b = bank(("xT", l, t, half))
                        eng.wait_ge(*at("xn", l, t))
                        for k in range(4):
                            i = nc.tensor.transpose(b[:, k * P:(k + 1) * P],
                                                    xn[t % 2][:, (half * 4 + k) * P:(half * 4 + k + 1) * P], ident)
                        i.then_inc(*pe.step("full", ("xT", l, t, half)))

                pe.stage(("conv", l))
                CP, Y, SG, SQ, RS = conv_work()
                for h in range(2):
                    project("conv_g", l, h, out_segs(l))
                    project("conv_a", l, h, out_segs(l))
                norm_sums("conv", l, [range(BB)], lambda m, t0, n: Y[:, m, t0:t0 + n],
                          lambda m, t0, n: SQ[:, m, t0:t0 + n], "mean512")

                pe.stage(("ret", l))
                R = ret_work()
                for h in range(2):
                    project("rk", l, h, ALL_SEGS)
                    rotate("rk", l, (2 * h, 2 * h + 1), "permR", lambda m: R["raw"][:, m % 2, :])
                for h in range(2):
                    project_tok("rv", l, h, 0, W)
                    used(("rv", l, h))
                for h in range(2):
                    project("rq", l, h, out_segs(l))
                    rotate("rq", l, (2 * h, 2 * h + 1), "permR", lambda m: R["raw"][:, m % 2, :])
                for c in range(NB):
                    b = bank(("rkT", l, c))
                    eng.wait_ge(*at("rk_ready", l))
                    for h in range(NH):
                        i = nc.tensor.transpose(b[:, h * P:(h + 1) * P], R["K"][:, h, c * P:(c + 1) * P], ident)
                    i.then_inc(*pe.step("full", ("rkT", l, c)))
                for d, chunks in ((0, scan_order(0)), (1, scan_order(1))):
                    for c in chunks[:-1]:
                        b = bank(("rS", l, d, c))
                        eng.wait_ge(*at("rkd", l, d, c))
                        for h in range(NH):
                            i = mm(b[:, h * P:(h + 1) * P], R["kd"][:, h, :], R["V"][:, c, h * P:(h + 1) * P],
                                   start=True, stop=True)
                        i.then_inc(*pe.step("full", ("rS", l, d, c)))
                for c in out_blocks(l):
                    b = bank(("rkq", l, c))
                    eng.wait_ge(*at("rq_ready", l))
                    for h in range(NH):
                        i = mm(b[:, h * P:(h + 1) * P], R["K"][:, h, c * P:(c + 1) * P], R["Q"][:, h, c * P:(c + 1) * P],
                               start=True, stop=True)
                    i.then_inc(*pe.step("full", ("rkq", l, c)))
                    b = bank(("ro", l, c))
                    eng.wait_ge(*at("ratt", l, c))
                    dirs = [d for d in range(2) if scan_order(d)[0] != c]
                    for h in range(NH):
                        i = mm(b[:, h * P:(h + 1) * P], R["V"][:, c, h * P:(h + 1) * P], R["att"][:, h, :],
                               start=True, stop=not dirs)
                        for d in dirs:
                            i = mm(b[:, h * P:(h + 1) * P], R["S"][:, d * NB + c, h, :], R["qd"][:, d, h, :],
                                   start=False, stop=d == dirs[-1])
                    i.then_inc(*pe.step("full", ("ro", l, c)))
                norm_sums("ret", l, [[h] for h in range(NH)], lambda m, t0, n: YSb[:, BB + m, t0:t0 + n],
                          lambda m, t0, n: R["sq"][:, m, t0:t0 + n], "mean128")
                for h in range(2):
                    project("rg", l, h, out_segs(l))

                pe.stage(("mlstm", l))
                M = mlstm_work()
                eng.wait_ge(*at("gw", l))
                for t0, n in ALL_SEGS:
                    b = bank(("mgate", l, t0))
                    for k in range(KD):
                        i = mm(b[:, 0:n], M["gw"][:, k, :], HTk[:, k, t0:t0 + n], start=(k == 0), stop=(k == KD - 1))
                    i.then_inc(*pe.step("full", ("mgate", l, t0)))
                for h in range(2):
                    project("mq", l, h, out_segs(l))
                for h in range(2):
                    project("mk", l, h, ALL_SEGS)
                for h in range(2):
                    project_tok("mv", l, h, 0, W)
                    used(("mv", l, h))
                for c in range(NB):
                    b = bank(("mcols", l, c))
                    eng.wait_ge(*at("mrows", l))
                    nc.tensor.transpose(b[:, 0:P], M["a"][:, c * P:(c + 1) * P], ident).then_inc(*pe.step("full", ("mcols", l, c)))
                for d in range(2):
                    for n_, c in enumerate(scan_order(d)):
                        if c in out_blocks(l):
                            b = bank(("mkq", l, d, c))
                            eng.wait_ge(*at("mqk_ready", l))
                            for h in range(NH):
                                i = mm(b[:, h * P:(h + 1) * P], M["K"][:, h, c * P:(c + 1) * P],
                                       M["Q"][:, h, c * P:(c + 1) * P], start=True, stop=True)
                            i.then_inc(*pe.step("full", ("mkq", l, d, c)))
                            b = bank(("mnum", l, d, c))
                            eng.wait_ge(*at("ms", l, d, c))
                            for h in range(NH):
                                i = mm(b[:, h * P:(h + 1) * P], M["V"][:, c, h * P:(h + 1) * P], M["s"][:, h, :],
                                       start=True, stop=not n_)
                                if n_:
                                    i = mm(b[:, h * P:(h + 1) * P], M["C"][:, n_ % 2, h, :], M["qw"][:, h, :],
                                           start=False, stop=True)
                            i.then_inc(*pe.step("full", ("mnum", l, d, c)))
                            b = bank(("mden", l, d, c))
                            for h in range(NH):
                                i = mm(b[:, h * P:(h + 1) * P], const("ones"), M["s"][:, h, :], start=True, stop=not n_)
                                if n_:
                                    i = mm(b[:, h * P:(h + 1) * P], M["nb"][:, h, :], M["qw"][:, h, :],
                                           start=False, stop=True)
                            i.then_inc(*pe.step("full", ("mden", l, d, c)))
                        if n_ < NB - 1:
                            b = bank(("mkT", l, d, c))
                            eng.wait_ge(*at("mqk_ready", l))
                            for h in range(NH):
                                i = nc.tensor.transpose(b[:, h * P:(h + 1) * P], M["K"][:, h, c * P:(c + 1) * P], ident)
                            i.then_inc(*pe.step("full", ("mkT", l, d, c)))
                            b = bank(("mC", l, d, c))
                            eng.wait_ge(*at("mkw", l, d, c))
                            for h in range(NH):
                                i = mm(b[:, h * P:(h + 1) * P], M["kw"][:, h, :], M["V"][:, c, h * P:(h + 1) * P],
                                       start=True, stop=True)
                            i.then_inc(*pe.step("full", ("mC", l, d, c)))
                            b = bank(("mn", l, d, c))
                            for h in range(NH):
                                i = mm(b[:, h:h + 1], M["kw"][:, h, :], const("ones")[:, 0:1], start=True, stop=True)
                            i.then_inc(*pe.step("full", ("mn", l, d, c)))
                norm_sums("mls", l, [[h] for h in range(NH)], lambda m, t0, n: YSb[:, 2 * BB + m, t0:t0 + n],
                          lambda m, t0, n: M["sq"][:, m, t0:t0 + n], "mean128")
                for h in range(2):
                    project("mo", l, h, out_segs(l))

                pe.stage(("attn", l))
                A = attn_work()
                w = weight(("akv", l, 0))
                for t0, n in ALL_SEGS:
                    b = bank(("ak", l, 0, t0))
                    for k in range(KD):
                        i = mm(b[:, 0:n], w[:, k, 0:P], HTk[:, k, t0:t0 + n], start=(k == 0), stop=(k == KD - 1))
                    i.then_inc(*pe.step("full", ("ak", l, 0, t0)))
                rotate("ak", l, (0,), "permA", lambda m: A["raw"][:, 0, :])
                project_tok("akv", l, 0, P, P)
                used(("akv", l, 0))
                for h in range(2):
                    project("aq", l, h, out_segs(l))
                    rotate("aq", l, (2 * h, 2 * h + 1), "permA", lambda m: A["raw"][:, m % 2, :])
                for t in out_blocks(l):
                    local = local_blocks(t)
                    for h in range(AH):
                        g, fb = h // 4, h % 4
                        lo = g * AD
                        q = A["Q"][lo:lo + AD, fb, t * P:(t + 1) * P]
                        eng.wait_ge(*at("aq_ready", l))
                        if local:
                            b = bank(("aloc", l, t, h))
                            i = mm(b[:, 0:P * len(local)], q, A["K"][lo:lo + AD, local[0] * P:(local[-1] + 1) * P],
                                   start=True, stop=True)
                            i.then_inc(*pe.step("full", ("aloc", l, t, h)))
                        b = bank(("actx", l, t, h))
                        i = mm(b[:, 0:CTX], q, A["K"][lo:lo + AD, 0:CTX], start=True, stop=True)
                        i.then_inc(*pe.step("full", ("actx", l, t, h)))

                        def back(t, h, local):
                            kb = local + [0, 1]
                            for part, js in (("apl", list(range(len(local)))), ("apc", [len(local), len(local) + 1])):
                                if not js:
                                    continue
                                b = bank((part, l, t, h))
                                eng.wait_ge(*at("ap", l, t, h))
                                for x, j in enumerate(js):
                                    i = nc.tensor.transpose(b[:, x * P:(x + 1) * P],
                                                            A["P"][:, h % 2, j * P:(j + 1) * P], ident)
                                i.then_inc(*pe.step("full", (part, l, t, h)))
                            b = bank(("ay", l, t, h))
                            eng.wait_ge(*at("apt", l, t, h))
                            gg = h // 4
                            for x, j in enumerate(kb):
                                i = mm(b[:, 0:AD], A["PT"][:, h % 2, x * P:(x + 1) * P],
                                       A["V"][:, j, gg * AD:(gg + 1) * AD], start=(x == 0), stop=(x == len(kb) - 1))
                            i.then_inc(*pe.step("full", ("ay", l, t, h)))

                        if h:
                            back(t, h - 1, local)
                    back(t, AH - 1, local)
                    b = bank(("ayT", l, t))
                    eng.wait_ge(*at("ayn", l, t))
                    for m in range(BB):
                        i = nc.tensor.transpose(b[:, m * P:(m + 1) * P], A["Y"][:, t % 2, m * P:(m + 1) * P], ident)
                    i.then_inc(*pe.step("full", ("ayT", l, t)))

                pe.stage(("merge", l))
                for j in range(D // W):
                    for i_ in range(4):
                        wg = weight(("gate", l, j, i_))
                        wb = weight(("branch", l, j, i_), BB)
                        for m in range(2):
                            for t0, n in out_segs(l):
                                b = bank(("gate", l, j, i_, m, t0))
                                for k in range(KD):
                                    i = mm(b[:, 0:n], wg[:, k, m * P:(m + 1) * P], HTk[:, k, t0:t0 + n],
                                           start=(k == 0), stop=(k == KD - 1))
                                i.then_inc(*pe.step("full", ("gate", l, j, i_, m, t0)))
                                b = bank(("branch", l, j, i_, m, t0))
                                for k in range(BB):
                                    i = mm(b[:, 0:n], wb[:, k, m * P:(m + 1) * P], YSb[:, i_ * BB + k, t0:t0 + n],
                                           start=(k == 0), stop=(k == BB - 1))
                                i.then_inc(*pe.step("full", ("branch", l, j, i_, m, t0)))
                        used(("gate", l, j, i_))
                        used(("branch", l, j, i_))

                pe.stage(("out", l))
                ACC = merge_work()[0]
                for j in range(D // W):
                    w = weight(("out", l, j))
                    for t in out_blocks(l):
                        b = bank(("out", l, j, t))
                        for k in range(KD):
                            i = mm(b[:, 0:W], ACC[:, k, t * P:(t + 1) * P], w[:, k, :], start=(k == 0), stop=(k == KD - 1))
                        i.then_inc(*pe.step("full", ("out", l, j, t)))
                    used(("out", l, j))

                pe.stage(("peernorm", l))
                H2 = work(NB * D)[0].rearrange("p (b d) -> p b d", b=NB)
                for t in out_blocks(l):
                    for half in range(2):
                        b = bank(("hT", l, t, half))
                        eng.wait_ge(*at("h2", l, t))
                        for k in range(4):
                            i = nc.tensor.transpose(b[:, k * P:(k + 1) * P],
                                                    H2[:, t, (half * 4 + k) * P:(half * 4 + k + 1) * P], ident)
                        i.then_inc(*pe.step("full", ("hT", l, t, half)))

                pe.stage(("peerq", l))
                for h in range(HEADS * 256 // W):
                    project("wq", l, h, out_segs(l))

                pe.stage(("route", l))
                for t in out_blocks(l):
                    for g in range(4):
                        b = bank(("score", l, t, g))
                        for x in range(4):
                            hc = 4 * g + x
                            i = mm(b[:, x * KEYS:(x + 1) * KEYS], YSb[:, hc, t * P:(t + 1) * P],
                                   KEYT[:, (hc % 2) * KEYS:(hc % 2 + 1) * KEYS], start=True, stop=True)
                        i.then_inc(*pe.step("full", ("score", l, t, g)))

                pe.stage(("peer", l))
                G = peer_work()
                for b0, nb, base in peer_calls(l):
                    with eng.Fori(0, nb) as i:
                        for n in range(SLOTS):
                            if n == 0:
                                eng.wait_ge(fl.sem("residual_added"), i + base + 1)
                            eng.wait_ge(fl.sem(f"v_landed{n % VRING}"), (i + base) * (16 * SLOTS // VRING) + 16 * (n // VRING + 1))
                            eng.wait_ge(fl.sem("diagonal_ready"), (i + base) * SLOTS + n + 1)
                            mm(banks[6][:, :], G["diag"][:, n % DRING, :], G["v"][n % VRING][:, 0:512],
                               start=(n == 0), stop=(n == SLOTS - 1))
                            mm(banks[7][:, :], G["diag"][:, n % DRING, :], G["v"][n % VRING][:, 512:1024],
                               start=(n == 0), stop=(n == SLOTS - 1)).then_inc(fl.sem("v_summed"), 1)
            pe.stage("final")
            pe.finish()

        @block.vector
        def _(eng):
            dv = Engine(eng, "vector")
            v = nc.vector

            def normalise(tag, l, groups, y, sq, rs):
                for t0, n in out_segs(l):
                    for g, blocks in enumerate(groups):
                        eng.wait_ge(*at("full", (tag, "mean", l, g, t0)))
                        b = bank_of((tag, "mean", l, g, t0))
                        for m in blocks:
                            v.tensor_tensor(y(m, t0, n), y(m, t0, n), b[:, 0:n], ALU.subtract).then_inc(*dv.step())
                            eng.wait_ge(*dv.latest())
                        fl.mark(("read", (tag, "mean", l, g, t0)), dv.sem)
                        fl.mark((tag + "_centred", l, g, t0), dv.sem)
                for t0, n in out_segs(l):
                    for g, blocks in enumerate(groups):
                        eng.wait_ge(*at(tag + "_root", l, g, t0))
                        v.reciprocal(rs(g, t0, n), rs(g, t0, n)).then_inc(*dv.step())
                        eng.wait_ge(*dv.latest())
                        for m in blocks:
                            v.tensor_tensor(y(m, t0, n), y(m, t0, n), rs(g, t0, n), ALU.mult).then_inc(*dv.step())
                            eng.wait_ge(*dv.latest())
                        fl.mark((tag + "_normed", l, g, t0), dv.sem)

            def rope(tag, l, nb, cos, sin, raw, dst):
                for m in range(nb):
                    eng.wait_ge(*at("full", (tag + "_rot", l, m)))
                    b = bank_of((tag + "_rot", l, m))
                    v.tensor_tensor(dst(m), raw(m), const(cos), ALU.mult).then_inc(*dv.step())
                    eng.wait_ge(*dv.latest())
                    v.tensor_tensor(raw(m), b[:, :], const(sin), ALU.mult).then_inc(*dv.step("read", (tag + "_rot", l, m)))
                    eng.wait_ge(*dv.latest())
                    v.tensor_tensor(dst(m), dst(m), raw(m), ALU.add).then_inc(*dv.step(tag + "_roped", l, m))
                    eng.wait_ge(*dv.latest())
                fl.mark((tag + "_ready", l), dv.sem)

            dv.stage("mod")
            MR, MB = work(6 * D, 6 * D)
            eng.wait_ge(*at("params"))
            for l in range(DEPTH):
                eng.wait_ge(*at("mod_b", l))
                if l:
                    eng.wait_ge(*at("mod_stored", l - 1))
                for c in range(6 * D // W):
                    eng.wait_ge(*at("full", ("mod", l, c)))
                    b = bank_of(("mod", l, c))
                    v.tensor_tensor(MR[0:2, c * W:(c + 1) * W], b[0:2, 0:W], MB[0:2, c * W:(c + 1) * W], ALU.add).then_inc(*dv.step("read", ("mod", l, c)))
                fl.mark(("mod_rows", l), dv.sem)

            for l in range(DEPTH):
                dv.stage(("norm", l))
                xn = work(D, D)
                eng.wait_ge(*at("layer", l))
                for s in range(2):
                    v.scalar_tensor_tensor(SC1[:, s * KD:(s + 1) * KD], SC1[:, s * KD:(s + 1) * KD], 1.0,
                                                 par("n1g"), ALU.add, ALU.mult).then_inc(*dv.step())
                    eng.wait_ge(*dv.latest())
                fl.mark(("sc1", l), dv.sem)
                v.scalar_tensor_tensor(T8[0], LG, -1.0, LG, ALU.mult, ALU.max).then_inc(*dv.step("rabs", l))
                eng.wait_ge(*dv.latest())
                v.tensor_scalar(LG, LG, 0.0, None, ALU.min).then_inc(*dv.step())
                eng.wait_ge(*dv.latest())
                eng.wait_ge(*at("rln", l))
                v.tensor_tensor(LG, LG, T8[2], ALU.subtract).then_inc(*dv.step("lg", l))
                eng.wait_ge(*dv.latest())
                for t in range(NB):
                    eng.wait_ge(*at("ssq", l, t))
                    v.tensor_scalar(RSQ[:, t:t + 1], SSQ[:, t:t + 1], 1.0 / D, EPS, ALU.mult, ALU.add).then_inc(*dv.step())
                    eng.wait_ge(*dv.latest())
                    v.reciprocal(RSQ[:, t:t + 1], RSQ[:, t:t + 1]).then_inc(*dv.step("rsq", l, t))
                    eng.wait_ge(*dv.latest())
                    eng.wait_ge(*at("rs", l, t))
                    if t >= 2:
                        eng.wait_ge(*at("full", ("xT", l, t - 2, 1)))
                    v.tensor_scalar(xn[t % 2], Xb[:, t, :], RSB[:, t:t + 1], None, ALU.mult).then_inc(*dv.step("xn", l, t))
                    eng.wait_ge(*dv.latest())
                    eng.wait_ge(*at("full", ("xT", l, t, 1)))
                    b = bank_of(("xT", l, t, 1))
                    s = 0 if t >= CB else 1
                    for k in range(4):
                        kk = 4 + k
                        i = v.tensor_scalar(HTk[:, kk, t * P:(t + 1) * P], b[:, k * P:(k + 1) * P],
                                            SC1[:, s * KD + kk:s * KD + kk + 1], SH1[:, s * KD + kk:s * KD + kk + 1],
                                            ALU.mult, ALU.add)
                        i.then_inc(*dv.step())
                    fl.mark(("read", ("xT", l, t, 1)), dv.sem)

                dv.stage(("conv", l))
                CP, Y, SG, SQ, RS = conv_work()
                v.memset(CP, 0.0).then_inc(*dv.step())
                eng.wait_ge(*dv.latest())

                def glu(h):
                    for m in range(2):
                        for t0, n in out_segs(l):
                            o = pad_at(t0)
                            eng.wait_ge(*at("conv_sg", l, h, m, t0))
                            eng.wait_ge(*at("full", ("conv_a", l, 2 * h + m, t0)))
                            b = bank_of(("conv_a", l, 2 * h + m, t0))
                            v.tensor_tensor(CP[:, 2 * h + m, o:o + n], b[:, 0:n], SG[:, m, t0:t0 + n], ALU.mult).then_inc(*dv.step("read", ("conv_a", l, 2 * h + m, t0)))
                            eng.wait_ge(*dv.latest())
                    fl.mark(("conv_glu", l, h), dv.sem)

                def taps(h):
                    cw, cb = par("conv_w"), par("conv_b")
                    for m in (2 * h, 2 * h + 1):
                        for t0, n in out_segs(l):
                            o = pad_at(t0) - TAPS // 2
                            dst = Y[:, m, t0:t0 + n]
                            v.tensor_scalar(dst, CP[:, m, o:o + n], cw[:, m * TAPS:m * TAPS + 1], cb[:, m:m + 1],
                                                  ALU.mult, ALU.add).then_inc(*dv.step())
                            eng.wait_ge(*dv.latest())
                            for j in range(1, TAPS):
                                v.scalar_tensor_tensor(dst, CP[:, m, o + j:o + j + n],
                                                             cw[:, m * TAPS + j:m * TAPS + j + 1], dst, ALU.mult, ALU.add).then_inc(*dv.step())
                                eng.wait_ge(*dv.latest())
                glu(0)
                glu(1)
                taps(0)
                taps(1)
                for t0, n in out_segs(l):
                    fl.mark(("conv_mean", l, 0, t0), dv.sem)
                normalise("conv", l, [range(BB)], lambda m, t0, n: Y[:, m, t0:t0 + n],
                          SQ, lambda g, t0, n: RS[:, t0:t0 + n])

                dv.stage(("ret", l))
                R = ret_work()
                for h in range(NH):
                    eng.wait_ge(*at("rdec", l, h))
                    v.tensor_tensor(R["dec"][:, h, :], R["dec"][:, h, :], const("until"), ALU.mult).then_inc(*dv.step())
                    eng.wait_ge(*dv.latest())
                    v.tensor_tensor(R["dtmp"][:, h, :], R["dtmp"][:, h, :], const("since"), ALU.mult).then_inc(*dv.step())
                    eng.wait_ge(*dv.latest())
                    v.tensor_tensor(R["dec"][:, h, :], R["dec"][:, h, :], R["dtmp"][:, h, :], ALU.add).then_inc(*dv.step())
                    eng.wait_ge(*dv.latest())
                rope("rk", l, BB, "cosR", "sinR", lambda m: R["raw"][:, m % 2, :], lambda m: R["K"][:, m, CTX:])
                for h in range(2):
                    for t in range(NB):
                        eng.wait_ge(*at("full", ("rv_tok", l, h, t)))
                        b = bank_of(("rv_tok", l, h, t))
                        v.tensor_copy(R["V"][:, t, h * W:(h + 1) * W], b[:, 0:W]).then_inc(*dv.step("read", ("rv_tok", l, h, t)))
                rope("rq", l, BB, "cosR", "sinR", lambda m: R["raw"][:, m % 2, :], lambda m: R["Q"][:, m, CTX:])
                for c in range(NB):
                    eng.wait_ge(*at("full", ("rkT", l, c)))
                    b = bank_of(("rkT", l, c))
                    v.tensor_copy(R["kt"][:, c, :], b[:, :]).then_inc(*dv.step("read", ("rkT", l, c)))
                    eng.wait_ge(*dv.latest())

                def ret_out(c):
                    eng.wait_ge(*at("full", ("ro", l, c)))
                    b = bank_of(("ro", l, c))
                    v.tensor_copy(YSb[:, BB:2 * BB, c * P:(c + 1) * P], blocks4(b[:, :])).then_inc(*dv.step("read", ("ro", l, c)))
                    eng.wait_ge(*dv.latest())

                prev = None
                for d in range(2):
                    chunks = scan_order(d)
                    for n_, c in enumerate(chunks[:-1]):
                        if prev:
                            eng.wait_ge(*at("full", prev))
                        v.tensor_tensor(R["kd"], R["kt"][:, c, :].rearrange("p (h j) -> p h j", h=NH),
                                              KDEC[:, d * 4:d * 4 + 4].unsqueeze(2).to_broadcast([P, NH, P]), ALU.mult).then_inc(*dv.step("rkd", l, d, c))
                        eng.wait_ge(*dv.latest())
                        prev = ("rS", l, d, c)
                        eng.wait_ge(*at("full", prev))
                        b = bank_of(prev)
                        new = R["S"][:, d * NB + chunks[n_ + 1], :, :]
                        if n_ == 0:
                            v.tensor_copy(new.rearrange("p h e -> p (h e)"), b[:, :]).then_inc(*dv.step("read", prev))
                            eng.wait_ge(*dv.latest())
                        else:
                            old = R["S"][:, d * NB + c, :, :]
                            v.tensor_tensor(new, old, CDEC[:, d * 4:d * 4 + 4].unsqueeze(2).to_broadcast([P, NH, P]),
                                                  ALU.mult).then_inc(*dv.step())
                            eng.wait_ge(*dv.latest())
                            v.tensor_tensor(new.rearrange("p h e -> p (h e)"), new.rearrange("p h e -> p (h e)"),
                                                 b[:, :], ALU.add).then_inc(*dv.step("read", prev))
                            eng.wait_ge(*dv.latest())
                for x, c in enumerate(out_blocks(l)):
                    if x:
                        eng.wait_ge(*at("full", ("ro", l, out_blocks(l)[x - 1])))
                    eng.wait_ge(*at("full", ("rkq", l, c)))
                    b = bank_of(("rkq", l, c))
                    v.tensor_tensor(R["att"].rearrange("p h i -> p (h i)"), b[:, :],
                                         R["dec"].rearrange("p h i -> p (h i)"), ALU.mult).then_inc(*dv.step("read", ("rkq", l, c)))
                    eng.wait_ge(*dv.latest())
                    for d in range(2):
                        v.tensor_tensor(R["qd"][:, d, :, :], R["Q"][:, :, c * P:(c + 1) * P], R["qdec"][:, d, :, :],
                                              ALU.mult).then_inc(*dv.step())
                        eng.wait_ge(*dv.latest())
                    fl.mark(("ratt", l, c), dv.sem)
                    if x:
                        ret_out(out_blocks(l)[x - 1])
                ret_out(out_blocks(l)[-1])
                for t0, n in out_segs(l):
                    for g in range(NH):
                        fl.mark(("ret_mean", l, g, t0), dv.sem)
                normalise("ret", l, [[h] for h in range(NH)], lambda m, t0, n: YSb[:, BB + m, t0:t0 + n],
                          None, lambda g, t0, n: R["rs"][:, g, t0:t0 + n])
                for m in range(BB):
                    for t0, n in out_segs(l):
                        eng.wait_ge(*at("rgate", l, m, t0))
                        y = YSb[:, BB + m, t0:t0 + n]
                        v.tensor_tensor(y, y, R["g"][:, m, t0:t0 + n], ALU.mult).then_inc(*dv.step())

                dv.stage(("mlstm", l))
                M = mlstm_work()
                v.memset(M["gw"], 0.0).then_inc(*dv.step())
                eng.wait_ge(*dv.latest())
                eng.wait_ge(*at("loaded", ("mgate", l, 0)))
                src = WRr[:, SLOT[("mgate", l, 0)] % RING, 0:KD * 16].rearrange("p (k n) -> p k n", k=KD)
                for qd, kind in enumerate((0, 2, 1, 3)):
                    v.tensor_copy(M["gw"][:, :, 32 * qd:32 * qd + 4], src[:, :, 4 * kind:4 * kind + 4]).then_inc(*dv.step())
                fl.mark(("gw", l), dv.sem)
                fl.mark(("used", ("mgate", l, 0)), dv.sem)
                eng.wait_ge(*at("gate_bias", l))
                I, F_, B, A_, MM, MT, WP, EM, T = (M[x] for x in ("i", "f", "b", "a", "m", "mt", "wp", "em", "t"))
                for t0, n in ALL_SEGS:
                    eng.wait_ge(*at("full", ("mgate", l, t0)))
                    b = bank_of(("mgate", l, t0))
                    v.tensor_scalar(I[0:64, t0:t0 + n], b[0:64, 0:n], GB[0:64, 0:1], None, ALU.add).then_inc(*dv.step())
                    eng.wait_ge(*dv.latest())
                    v.tensor_scalar(F_[0:64, t0:t0 + n], b[64:128, 0:n], GB[64:128, 1:2], None, ALU.add).then_inc(*dv.step("read", ("mgate", l, t0)))
                    eng.wait_ge(*dv.latest())
                v.scalar_tensor_tensor(T[0:64, :], F_[0:64, :], -1.0, F_[0:64, :], ALU.mult, ALU.max).then_inc(*dv.step("mabs", l))
                eng.wait_ge(*dv.latest())
                v.tensor_scalar(F_[0:64, :], F_[0:64, :], 0.0, None, ALU.min).then_inc(*dv.step())
                eng.wait_ge(*dv.latest())
                eng.wait_ge(*at("mln", l))
                v.tensor_tensor(F_[0:64, :], F_[0:64, :], T[0:64, :], ALU.subtract).then_inc(*dv.step())
                eng.wait_ge(*dv.latest())
                for d in range(2):
                    q = slice(32 * d, 32 * d + 32)
                    for c in range(NB):
                        s = chunk_slice(d, c)
                        v.tensor_tensor_scan(B[q, s], const("ones")[q, :], F_[q, s], 0.0, ALU.mult, ALU.add).then_inc(*dv.step())
                        eng.wait_ge(*dv.latest())
                v.tensor_tensor(A_[0:64, :], I[0:64, :], B[0:64, :], ALU.subtract).then_inc(*dv.step())
                eng.wait_ge(*dv.latest())
                m0 = M["m0"]
                v.memset(m0, NEG).then_inc(*dv.step())
                eng.wait_ge(*dv.latest())
                for d in range(2):
                    q = slice(32 * d, 32 * d + 32)
                    for n_, c in enumerate(scan_order(d)):
                        s = chunk_slice(d, c)
                        e = (c + 1) * P - 1 if d == 0 else c * P
                        mi = m0[q, n_:n_ + 1]
                        v.tensor_tensor_scan(MM[q, s], A_[q, s], A_[q, s], mi, ALU.max, ALU.max).then_inc(*dv.step())
                        eng.wait_ge(*dv.latest())
                        if n_ < NB - 1:
                            v.tensor_tensor(m0[q, n_ + 1:n_ + 2], MM[q, e:e + 1], B[q, e:e + 1], ALU.add).then_inc(*dv.step())
                            eng.wait_ge(*dv.latest())
                        v.tensor_scalar(WP[q, s], MM[q, s], mi, -1.0, ALU.subtract, ALU.mult).then_inc(*dv.step())
                        eng.wait_ge(*dv.latest())
                        v.tensor_scalar(T[q, s], A_[q, s], MM[q, e:e + 1], None, ALU.subtract).then_inc(*dv.step())
                        eng.wait_ge(*dv.latest())
                v.tensor_tensor(MT[0:64, :], B[0:64, :], MM[0:64, :], ALU.add).then_inc(*dv.step("mrowlogs", l))
                eng.wait_ge(*dv.latest())
                order_qk = [("mq", m) for m in range(BB)] + [("mk", m) for m in range(BB)]
                v.memset(M["pad"], 0.0).then_inc(*dv.step("mpad0", l))
                eng.wait_ge(*dv.latest())
                for x, (tag, m) in enumerate(order_qk):
                    cw, cb = par("mconv_w"), par("mconv_b")
                    ch = m + (BB if tag == "mk" else 0)
                    for t0, n in (out_segs(l) if tag == "mq" else ALL_SEGS):
                        o = mpad_at(t0) - 1
                        pad = M["pad"][:, x % 2, :]
                        dst = M["Q" if tag == "mq" else "K"][:, m, t0:t0 + n]
                        eng.wait_ge(*at("mpad", l, tag, m, t0))
                        v.tensor_scalar(dst, pad[:, o:o + n], cw[:, 3 * ch:3 * ch + 1], cb[:, ch:ch + 1],
                                              ALU.mult, ALU.add).then_inc(*dv.step())
                        eng.wait_ge(*dv.latest())
                        for j in (1, 2):
                            v.scalar_tensor_tensor(dst, pad[:, o + j:o + j + n], cw[:, 3 * ch + j:3 * ch + j + 1],
                                                         dst, ALU.mult, ALU.add).then_inc(*dv.step())
                            eng.wait_ge(*dv.latest())
                        fl.mark(("mconv", l, tag, m, t0), dv.sem)
                eng.wait_ge(*at("msilu", l))
                v.tensor_scalar(M["Kf"], M["Kf"], float(P) ** -0.5, None, ALU.mult).then_inc(*dv.step("mqk_ready", l))
                eng.wait_ge(*dv.latest())
                for h in range(2):
                    for t in range(NB):
                        eng.wait_ge(*at("full", ("mv_tok", l, h, t)))
                        b = bank_of(("mv_tok", l, h, t))
                        v.tensor_copy(M["V"][:, t, h * W:(h + 1) * W], b[:, 0:W]).then_inc(*dv.step("read", ("mv_tok", l, h, t)))
                for c in range(NB):
                    eng.wait_ge(*at("full", ("mcols", l, c)))
                    b = bank_of(("mcols", l, c))
                    v.tensor_copy(M["cols"][:, c, :], b[:, 0:P]).then_inc(*dv.step("read", ("mcols", l, c)))
                    eng.wait_ge(*dv.latest())
                h4 = lambda a: a.rearrange("p (h i) -> p h i", h=NH)
                for d in range(2):
                    for n_, c in enumerate(scan_order(d)):
                        bc = M["bc"][:, n_ % 2, :]
                        eng.wait_ge(*at("mbc", l, d, c))
                        if c in out_blocks(l):
                            acol = M["cols"][:, c, 32 * d:32 * d + 4].unsqueeze(2).to_broadcast([P, NH, P])
                            v.tensor_tensor(M["e"], h4(bc[:, 0:512]), acol, ALU.subtract).then_inc(*dv.step("mlogw", l, d, c))
                            eng.wait_ge(*dv.latest())
                            if n_:
                                v.tensor_tensor(M["qw"], M["Q"][:, :, c * P:(c + 1) * P], h4(bc[:, 512:1024]), ALU.mult).then_inc(*dv.step())
                                eng.wait_ge(*dv.latest())
                                v.tensor_copy(M["nb"], M["N"][:, n_ % 2, :].unsqueeze(2).to_broadcast([P, NH, P])).then_inc(*dv.step())
                                eng.wait_ge(*dv.latest())
                            eng.wait_ge(*at("mexp", l, d, c))
                            mask = const("until" if d == 0 else "since").unsqueeze(1).to_broadcast([P, NH, P])
                            v.scalar_tensor_tensor(M["e"], M["e"], 1.0, mask, ALU.min, ALU.mult).then_inc(*dv.step())
                            eng.wait_ge(*dv.latest())
                            eng.wait_ge(*at("full", ("mkq", l, d, c)))
                            b = bank_of(("mkq", l, d, c))
                            v.tensor_tensor(M["s"].rearrange("p h i -> p (h i)"), M["e"].rearrange("p h i -> p (h i)"),
                                                 b[:, :], ALU.mult).then_inc(*dv.step("read", ("mkq", l, d, c)))
                            eng.wait_ge(*dv.latest())
                            fl.mark(("ms", l, d, c), dv.sem)
                            eng.wait_ge(*at("full", ("mden", l, d, c)))
                            b = bank_of(("mden", l, d, c))
                            v.scalar_tensor_tensor(M["den"], b[:, :], -1.0, bc[:, 1024:1536], ALU.mult, ALU.max).then_inc(*dv.step())
                            eng.wait_ge(*dv.latest())
                            v.tensor_tensor(M["den"], b[:, :], M["den"], ALU.max).then_inc(*dv.step())
                            eng.wait_ge(*dv.latest())
                            fl.mark(("read", ("mden", l, d, c)), dv.sem)
                            v.reciprocal(M["den"], M["den"]).then_inc(*dv.step())
                            eng.wait_ge(*dv.latest())
                            eng.wait_ge(*at("full", ("mnum", l, d, c)))
                            b = bank_of(("mnum", l, d, c))
                            y = YSb[:, 2 * BB:3 * BB, c * P:(c + 1) * P]
                            if d == 0:
                                v.tensor_tensor(y, h4(b[:, :]), h4(M["den"]), ALU.mult).then_inc(*dv.step("read", ("mnum", l, d, c)))
                                eng.wait_ge(*dv.latest())
                            else:
                                v.tensor_tensor(M["den"], b[:, :], M["den"], ALU.mult).then_inc(*dv.step("read", ("mnum", l, d, c)))
                                eng.wait_ge(*dv.latest())
                                v.tensor_tensor(y, y, h4(M["den"]), ALU.add).then_inc(*dv.step())
                                eng.wait_ge(*dv.latest())
                        if n_ < NB - 1:
                            wcol = M["cols"][:, c, 64 + 32 * d:64 + 32 * d + 4].unsqueeze(2).to_broadcast([P, NH, P])
                            eng.wait_ge(*at("full", ("mkT", l, d, c)))
                            b = bank_of(("mkT", l, d, c))
                            v.tensor_tensor(M["kw"], h4(b[:, :]), wcol, ALU.mult).then_inc(*dv.step("read", ("mkT", l, d, c)))
                            eng.wait_ge(*dv.latest())
                            fl.mark(("mkw", l, d, c), dv.sem)
                            new, nn = M["C"][:, (n_ + 1) % 2, :, :], M["N"][:, (n_ + 1) % 2, :]
                            eng.wait_ge(*at("full", ("mC", l, d, c)))
                            b = bank_of(("mC", l, d, c))
                            if n_ == 0:
                                v.tensor_copy(new.rearrange("p h e -> p (h e)"), b[:, :]).then_inc(*dv.step("read", ("mC", l, d, c)))
                                eng.wait_ge(*dv.latest())
                                eng.wait_ge(*at("full", ("mn", l, d, c)))
                                b = bank_of(("mn", l, d, c))
                                v.tensor_copy(nn, b[:, 0:4]).then_inc(*dv.step("read", ("mn", l, d, c)))
                                eng.wait_ge(*dv.latest())
                            else:
                                e = P - 1 if d == 0 else 0
                                dec = h4(bc[:, 512:1024])[:, :, e:e + 1]
                                old, on = M["C"][:, n_ % 2, :, :], M["N"][:, n_ % 2, :]
                                v.tensor_tensor(new, old, dec.to_broadcast([P, NH, P]), ALU.mult).then_inc(*dv.step())
                                eng.wait_ge(*dv.latest())
                                v.tensor_tensor(nn.unsqueeze(2), on.unsqueeze(2), dec, ALU.mult).then_inc(*dv.step())
                                eng.wait_ge(*dv.latest())
                                v.tensor_tensor(new.rearrange("p h e -> p (h e)"), new.rearrange("p h e -> p (h e)"),
                                                     b[:, :], ALU.add).then_inc(*dv.step("read", ("mC", l, d, c)))
                                eng.wait_ge(*dv.latest())
                                eng.wait_ge(*at("full", ("mn", l, d, c)))
                                b = bank_of(("mn", l, d, c))
                                v.tensor_tensor(nn, nn, b[:, 0:4], ALU.add).then_inc(*dv.step("read", ("mn", l, d, c)))
                                eng.wait_ge(*dv.latest())
                        fl.mark(("mbc_used", l, d, c), dv.sem)
                for t0, n in out_segs(l):
                    for g in range(NH):
                        fl.mark(("mls_mean", l, g, t0), dv.sem)
                normalise("mls", l, [[h] for h in range(NH)], lambda m, t0, n: YSb[:, 2 * BB + m, t0:t0 + n],
                          None, lambda g, t0, n: M["rs"][:, g, t0:t0 + n])
                for m in range(BB):
                    for t0, n in out_segs(l):
                        eng.wait_ge(*at("mogate", l, m, t0))
                        y = YSb[:, 2 * BB + m, t0:t0 + n]
                        v.tensor_tensor(y, y, M["g"][:, m, t0:t0 + n], ALU.mult).then_inc(*dv.step())

                dv.stage(("attn", l))
                A = attn_work()
                rope("ak", l, 1, "cosA", "sinA", lambda m: A["raw"][:, 0, :], lambda m: A["K"][:, CTX:])
                for t in range(NB):
                    eng.wait_ge(*at("full", ("akv_tok", l, 0, t)))
                    b = bank_of(("akv_tok", l, 0, t))
                    v.tensor_copy(A["V"][:, t, :], b[:, 0:P]).then_inc(*dv.step("read", ("akv_tok", l, 0, t)))
                rope("aq", l, BB, "cosA", "sinA", lambda m: A["raw"][:, m % 2, :], lambda m: A["Q"][:, m, CTX:])
                MX, NM, SE, DN, RC, SUM = AW
                for t in out_blocks(l):
                    local = local_blocks(t)
                    nl = len(local) * P
                    if t - 2 in out_blocks(l):
                        eng.wait_ge(*at("full", ("ayT", l, t - 2)))

                    def back(h):
                        eng.wait_ge(*at("aexp", l, t, h))
                        v.tensor_tensor(DN[:, h:h + 1], SUM[:, h:h + 1], SE[:, h:h + 1], ALU.add).then_inc(*dv.step())
                        eng.wait_ge(*dv.latest())
                        v.reciprocal(RC[:, h:h + 1], DN[:, h:h + 1]).then_inc(*dv.step())
                        eng.wait_ge(*dv.latest())
                        eng.wait_ge(*at("full", ("apc", l, t, h)))
                        b = bank_of(("apc", l, t, h))
                        v.tensor_copy(A["PT"][:, h % 2, nl:nl + CTX], b[:, 0:CTX]).then_inc(*dv.step("read", ("apc", l, t, h)))
                        eng.wait_ge(*dv.latest())
                        if local:
                            eng.wait_ge(*at("apl_moved", l, t, h))
                        v.tensor_copy(DN[:, h:h + 1], RC[:, h:h + 1]).then_inc(*dv.step("apt", l, t, h))
                        eng.wait_ge(*dv.latest())
                        eng.wait_ge(*at("full", ("ay", l, t, h)))
                        b = bank_of(("ay", l, t, h))
                        v.tensor_scalar(A["Y"][:, t % 2, h * AD:(h + 1) * AD], b[:, 0:AD], RC[:, h:h + 1], None,
                                             ALU.mult).then_inc(*dv.step("read", ("ay", l, t, h)))
                        eng.wait_ge(*dv.latest())

                    for h in range(AH):
                        S = A["S"][:, h % 2, :]
                        if local:
                            eng.wait_ge(*at("full", ("aloc", l, t, h)))
                            b = bank_of(("aloc", l, t, h))
                            for x, j in enumerate(local):
                                o = slice(x * P, (x + 1) * P)
                                if j == t:
                                    i = v.tensor_scalar(S[:, o], b[:, o], AD ** -0.5, None, ALU.mult)
                                else:
                                    mask = const("maskprev" if j < t else "masknext")
                                    i = v.scalar_tensor_tensor(S[:, o], b[:, o], AD ** -0.5, mask, ALU.mult, ALU.add)
                                i.then_inc(*dv.step())
                            fl.mark(("read", ("aloc", l, t, h)), dv.sem)
                        eng.wait_ge(*at("full", ("actx", l, t, h)))
                        b = bank_of(("actx", l, t, h))
                        v.tensor_scalar(S[:, nl:nl + CTX], b[:, 0:CTX], AD ** -0.5, None, ALU.mult).then_inc(*dv.step("read", ("actx", l, t, h)))
                        eng.wait_ge(*dv.latest())
                        v.tensor_reduce(MX[:, h:h + 1], S[:, 0:nl + CTX], AX, ALU.max).then_inc(*dv.step())
                        eng.wait_ge(*dv.latest())
                        v.tensor_scalar(NM[:, h:h + 1], MX[:, h:h + 1], SINK[:, h:h + 1], -1.0, ALU.max, ALU.mult).then_inc(*dv.step("anm", l, t, h))
                        eng.wait_ge(*dv.latest())
                        if h:
                            back(h - 1)
                    back(AH - 1)
                    fl.mark(("ayn", l, t), dv.sem)

                dv.stage(("merge", l))
                ACC, GS, PRD, _, _ = merge_work()
                for j in range(D // W):
                    for i_ in range(4):
                        for m in range(2):
                            for t0, n in out_segs(l):
                                eng.wait_ge(*at("gsig", l, j, i_, m, t0))
                                eng.wait_ge(*at("full", ("branch", l, j, i_, m, t0)))
                                b = bank_of(("branch", l, j, i_, m, t0))
                                acc = ACC[:, 2 * j + m, t0:t0 + n]
                                g = GS[:, gslot(l, j, i_, m, t0), 0:n]
                                if i_ == 0:
                                    v.tensor_tensor(acc, b[:, 0:n], g, ALU.mult).then_inc(*dv.step("read", ("branch", l, j, i_, m, t0)))
                                    eng.wait_ge(*dv.latest())
                                else:
                                    v.tensor_tensor(PRD[:, 0:n], b[:, 0:n], g, ALU.mult).then_inc(*dv.step("read", ("branch", l, j, i_, m, t0)))
                                    eng.wait_ge(*dv.latest())
                                    v.tensor_tensor(acc, acc, PRD[:, 0:n], ALU.add).then_inc(*dv.step())
                                    eng.wait_ge(*dv.latest())

                dv.stage(("out", l))
                GA, TMP = merge_work()[3:]
                for j in range(D // W):
                    for t in out_blocks(l):
                        eng.wait_ge(*at("full", ("out", l, j, t)))
                        b = bank_of(("out", l, j, t))
                        s = 0 if t >= CB else 1
                        eng.wait_ge(*at("ga1", l))
                        tmp = TMP[:, (t % 2) * W:(t % 2 + 1) * W]
                        v.tensor_tensor(tmp, b[:, 0:W], GA[:, s * D + j * W:s * D + (j + 1) * W], ALU.mult).then_inc(*dv.step("read", ("out", l, j, t)))
                        eng.wait_ge(*dv.latest())
                        x = Xb[:, t, j * W:(j + 1) * W]
                        v.tensor_tensor(x, x, tmp, ALU.add).then_inc(*dv.step())
                        eng.wait_ge(*dv.latest())

                dv.stage(("peernorm", l))
                H2w, SC2, SH2, G2 = work(NB * D, 2 * D, 2 * D, D)
                H2 = H2w.rearrange("p (b d) -> p b d", b=NB)
                eng.wait_ge(*at("mod2", l))
                for s in range(2):
                    sc = SC2[:, s * D:(s + 1) * D]
                    v.scalar_tensor_tensor(sc, sc, 1.0, G2, ALU.add, ALU.mult).then_inc(*dv.step())
                    eng.wait_ge(*dv.latest())
                for t in out_blocks(l):
                    s = 0 if t >= CB else 1
                    eng.wait_ge(*at("ssq2", l, t))
                    v.tensor_scalar(RSQ[:, t:t + 1], SSQ[:, t:t + 1], 1.0 / D, EPS, ALU.mult, ALU.add).then_inc(*dv.step())
                    eng.wait_ge(*dv.latest())
                    v.reciprocal(RSQ[:, t:t + 1], RSQ[:, t:t + 1]).then_inc(*dv.step("rsq2", l, t))
                    eng.wait_ge(*dv.latest())
                    eng.wait_ge(*at("rs2", l, t))
                    v.scalar_tensor_tensor(H2[:, t, :], Xb[:, t, :], RSB[:, t:t + 1], SC2[:, s * D:(s + 1) * D],
                                                 ALU.mult, ALU.mult).then_inc(*dv.step())
                    eng.wait_ge(*dv.latest())
                    v.tensor_tensor(H2[:, t, :], H2[:, t, :], SH2[:, s * D:(s + 1) * D], ALU.add).then_inc(*dv.step("h2", l, t))
                    eng.wait_ge(*dv.latest())
                    eng.wait_ge(*at("full", ("hT", l, t, 1)))
                    b = bank_of(("hT", l, t, 1))
                    v.tensor_copy(HTk[:, 4:8, t * P:(t + 1) * P], b[:, :].rearrange("p (k i) -> p k i", k=4)).then_inc(*dv.step("read", ("hT", l, t, 1)))

                dv.stage(("peerq", l))
                for h in range(HEADS * 256 // W):
                    for m in range(2):
                        for t0, n in out_segs(l):
                            if m:
                                eng.wait_ge(*at("full", ("wq", l, 2 * h + m, t0)))
                                b = bank_of(("wq", l, 2 * h + m, t0))
                                v.tensor_copy(YSb[:, 2 * h + m, t0:t0 + n], b[:, 0:n]).then_inc(*dv.step("read", ("wq", l, 2 * h + m, t0)))

                dv.stage(("route", l))
                R_ = route_work()
                S, SV, SI, SIF, CAND, CV, CI = (R_[x] for x in ("s", "sv", "si3", "sif", "cand", "cv", "ci"))
                for t in out_blocks(l):
                    for hc in range(2 * HEADS):
                        if hc % 4 == 0:
                            eng.wait_ge(*at("scored", l, t, hc // 4))
                        s, s2 = S[:, hc, :], R_["s2"]
                        v.max(SV[:, hc, 0:8], s).then_inc(*dv.step())
                        eng.wait_ge(*dv.latest())
                        v.max_index(SI[:, hc, 0:8], SV[:, hc, 0:8], s).then_inc(*dv.step())
                        v.match_replace(s2, SV[:, hc, 0:8], s, -3e38).then_inc(*dv.step())
                        eng.wait_ge(*dv.latest())
                        v.max(SV[:, hc, 8:16], s2).then_inc(*dv.step())
                        eng.wait_ge(*dv.latest())
                        v.max_index(SI[:, hc, 8:16], SV[:, hc, 8:16], s2).then_inc(*dv.step())
                        eng.wait_ge(*dv.latest())
                    fl.mark(("route_read", l, t), dv.sem)
                    v.tensor_copy(R_["siff"], R_["si"]).then_inc(*dv.step())
                    eng.wait_ge(*dv.latest())
                    for h in range(HEADS):
                        a = SV[:, 2 * h, :].unsqueeze(2).to_broadcast([P, TOPK, TOPK])
                        b_ = SV[:, 2 * h + 1, :].unsqueeze(1).to_broadcast([P, TOPK, TOPK])
                        v.tensor_tensor(CAND.rearrange("p (a b) -> p a b", a=TOPK), a, b_, ALU.add).then_inc(*dv.step())
                        eng.wait_ge(*dv.latest())
                        v.max(CV[:, h, 0:8], CAND).then_inc(*dv.step())
                        eng.wait_ge(*dv.latest())
                        v.max_index(CI[:, h, 0:8], CV[:, h, 0:8], CAND).then_inc(*dv.step())
                        v.match_replace(R_["cand2"], CV[:, h, 0:8], CAND, -3e38).then_inc(*dv.step())
                        eng.wait_ge(*dv.latest())
                        v.max(CV[:, h, 8:16], R_["cand2"]).then_inc(*dv.step())
                        eng.wait_ge(*dv.latest())
                        v.max_index(CI[:, h, 8:16], CV[:, h, 8:16], R_["cand2"]).then_inc(*dv.step())
                        eng.wait_ge(*dv.latest())
                    CIf = R_["cif"]
                    OH = R_["oh"]
                    io = const("iota16").unsqueeze(1).to_broadcast([P, SLOTS, TOPK])
                    for x, (op, imm) in enumerate(((ALU.logical_shift_right, 4), (ALU.bitwise_and, 15))):
                        v.tensor_scalar(R_["cu"], CIf, imm, None, op).then_inc(*dv.step())
                        eng.wait_ge(*dv.latest())
                        v.tensor_copy(R_["cf"], R_["cu"]).then_inc(*dv.step())
                        eng.wait_ge(*dv.latest())
                        v.tensor_tensor(OH, R_["cf"].unsqueeze(2).to_broadcast([P, SLOTS, TOPK]), io, ALU.is_equal).then_inc(*dv.step())
                        eng.wait_ge(*dv.latest())
                        for h in range(HEADS):
                            pick = SIF[:, 2 * h + x, :].unsqueeze(1).to_broadcast([P, TOPK, TOPK])
                            o = OH[:, h * TOPK:(h + 1) * TOPK, :]
                            v.tensor_tensor(o, o, pick, ALU.mult).then_inc(*dv.step())
                            if h == HEADS - 1:
                                eng.wait_ge(*dv.latest())
                        v.tensor_reduce(R_["i1" if x == 0 else "i2"], OH, AX, ALU.add).then_inc(*dv.step())
                        eng.wait_ge(*dv.latest())
                    v.scalar_tensor_tensor(R_["i2"], R_["i1"], float(KEYS), R_["i2"], ALU.mult, ALU.add).then_inc(*dv.step())
                    eng.wait_ge(*dv.latest())
                    v.tensor_scalar(R_["idx"][:, t, :], R_["i2"], float(l * EXPERTS), None, ALU.add).then_inc(*dv.step())
                    eng.wait_ge(*dv.latest())
                    v.tensor_tensor(R_["ce"], CV, CV[:, :, 0:1].to_broadcast([P, HEADS, TOPK]), ALU.subtract).then_inc(*dv.step("cdiff", l, t))
                    eng.wait_ge(*dv.latest())
                    eng.wait_ge(*at("cexp", l, t))
                    v.tensor_reduce(R_["csum"], R_["ce"], AX, ALU.add).then_inc(*dv.step())
                    eng.wait_ge(*dv.latest())
                    v.reciprocal(R_["csum"], R_["csum"]).then_inc(*dv.step())
                    eng.wait_ge(*dv.latest())
                    v.tensor_tensor(R_["gate"][:, t, :].rearrange("p (h k) -> p h k", h=HEADS), R_["ce"],
                                          R_["csum"].unsqueeze(2).to_broadcast([P, HEADS, TOPK]), ALU.mult).then_inc(*dv.step())
                    eng.wait_ge(*dv.latest())

                dv.stage(("peer", l))
                G = peer_work()
                eng.wait_ge(*at("ga2", l))
                for b0, nb, base in peer_calls(l):
                    s = 0 if b0 >= CB else 1
                    with eng.Fori(0, nb) as i:
                        it = i + base
                        v.tensor_copy(G["idxb"], G["idx"][:, bass.ds(i * SLOTS + b0 * SLOTS, SLOTS)])\
                            .then_inc(fl.sem("indices_staged"), 1)
                        v.tensor_copy(G["gateb"], G["gate"][:, bass.ds(i * SLOTS + b0 * SLOTS, SLOTS)])\
                            .then_inc(fl.sem("block_staged"), 1)
                        v.tensor_copy(G["hb"], G["H2"][:, bass.ds(i * D + b0 * D, D)]).then_inc(fl.sem("block_staged"), 1)
                        eng.wait_ge(fl.sem("block_staged"), (it + 1) * 2)

                        def weigh(h):
                            hs = slice(h * TOPK, (h + 1) * TOPK)
                            eng.wait_ge(fl.sem("gelu_done"), it * HEADS + h + 1)
                            v.tensor_tensor(G["w"][:, hs], G["gateb"][:, hs], G["act"][:, hs], ALU.mult)\
                                .then_inc(fl.sem("weights_ready"), 1)

                        for h in range(HEADS):
                            for k in range(TOPK):
                                n = h * TOPK + k
                                u = G["u"][n % URING]
                                eng.wait_ge(fl.sem(f"u_landed{n % URING}"), it * (16 * SLOTS // URING) + 16 * (n // URING + 1))
                                v.tensor_tensor_reduce(u, u, G["hb"], 1.0, 0.0, ALU.mult, ALU.add, G["dots"][:, n:n + 1])\
                                    .then_inc(fl.sem("dots_done"), 1)
                                if h and k == 3:
                                    weigh(h - 1)
                        weigh(HEADS - 1)
                        eng.wait_ge(fl.sem("v_summed"), (it + 1) * SLOTS + 1)
                        for half in range(2):
                            hs = slice(half * 512, half * 512 + 512)
                            v.tensor_tensor(G["y"][:, hs], banks[6 + half][:, :], G["ga"][:, s * D + half * 512:s * D + half * 512 + 512],
                                            ALU.mult).then_inc(fl.sem("y_scaled"), 1)
                        eng.wait_ge(fl.sem("y_scaled"), (it + 1) * 2)
                        xs = X[:, bass.ds(i * D + b0 * D, D)]
                        v.tensor_tensor(xs, xs, G["y"], ALU.add).then_inc(fl.sem("residual_added"), 1)
                        eng.wait_ge(fl.sem("residual_added"), it + 2)
            dv.stage("final")
            FG, O1, O2 = work(D, D, D)
            eng.wait_ge(*at("final_g"))
            for t in range(CB, NB):
                eng.wait_ge(*at("ssq2", DEPTH, t))
                v.tensor_scalar(RSQ[:, t:t + 1], SSQ[:, t:t + 1], 1.0 / D, EPS, ALU.mult, ALU.add).then_inc(*dv.step())
                eng.wait_ge(*dv.latest())
                v.reciprocal(RSQ[:, t:t + 1], RSQ[:, t:t + 1]).then_inc(*dv.step("rsq2", DEPTH, t))
                eng.wait_ge(*dv.latest())
                eng.wait_ge(*at("rs2", DEPTH, t))
                v.scalar_tensor_tensor(Xb[:, t, :], Xb[:, t, :], RSB[:, t:t + 1], FG, ALU.mult, ALU.mult).then_inc(*dv.step("result", t))
                eng.wait_ge(*dv.latest())
            dv.finish()

        @block.scalar
        def _(eng):
            sc = Engine(eng, "scalar")
            act = nc.scalar.activation

            def norm_side(tag, l, groups, y, sq, rs):
                for t0, n in out_segs(l):
                    for g, blocks in enumerate(groups):
                        eng.wait_ge(*at(tag + "_centred", l, g, t0))
                        for m in blocks:
                            act(sq(m, t0, n), y(m, t0, n), ACT.Square).then_inc(*sc.step())
                        fl.mark((tag + "_var", l, g, t0), sc.sem)
                for t0, n in out_segs(l):
                    for g, blocks in enumerate(groups):
                        eng.wait_ge(*at("full", (tag, "var", l, g, t0)))
                        b = bank_of((tag, "var", l, g, t0))
                        act(rs(g, t0, n), b[:, 0:n], ACT.Sqrt, bias=EPSC).then_inc(*sc.step(tag + "_root", l, g, t0))
                        fl.mark(("read", (tag, "var", l, g, t0)), sc.sem)

            EPSC = AW_EPS
            sc.stage("mod")
            eng.wait_ge(*at("eps"))
            eng.wait_ge(*at("params"))
            act(SIL, SIL, ACT.Silu).then_inc(*sc.step("silu_c"))
            eng.wait_ge(*sc.latest())

            for l in range(DEPTH):
                sc.stage(("norm", l))
                SQX = work(D, D, D)[2]
                eng.wait_ge(*at("rabs", l))
                act(T8[1], T8[0], ACT.Exp, scale=-1.0).then_inc(*sc.step())
                eng.wait_ge(*sc.latest())
                act(T8[2], T8[1], ACT.Ln, bias=1.0).then_inc(*sc.step("rln", l))
                eng.wait_ge(*sc.latest())
                eng.wait_ge(*at("lg", l))
                for d in range(2):
                    col = const("coldown" if d == 0 else "colup")
                    act(KDEC[:, 4 * d:4 * d + 4], LG[:, 4 * d:4 * d + 4], ACT.Exp, scale=col).then_inc(*sc.step())
                act(CDEC, LG, ACT.Exp, scale=float(P)).then_inc(*sc.step())
                for t in range(NB):
                    act(SQX, Xb[:, t, :], ACT.Square, accum_out=SSQ[:, t:t + 1]).then_inc(*sc.step("ssq", l, t))
                    eng.wait_ge(*sc.latest())
                for t in range(NB):
                    eng.wait_ge(*at("rsq", l, t))
                    act(RSB[:, t:t + 1], RSQ[:, t:t + 1], ACT.Sqrt).then_inc(*sc.step("rs", l, t))
                    eng.wait_ge(*sc.latest())
                    eng.wait_ge(*at("full", ("xT", l, t, 0)))
                    b = bank_of(("xT", l, t, 0))
                    s = 0 if t >= CB else 1
                    eng.wait_ge(*at("sc1", l))
                    for k in range(4):
                        act(HTk[:, k, t * P:(t + 1) * P], b[:, k * P:(k + 1) * P], ACT.Identity,
                                  bias=SH1[:, s * KD + k:s * KD + k + 1], scale=SC1[:, s * KD + k:s * KD + k + 1]).then_inc(*sc.step())
                    fl.mark(("read", ("xT", l, t, 0)), sc.sem)

                sc.stage(("conv", l))
                CP, Y, SG, SQ, RS = conv_work()
                for h in range(2):
                    for m in range(2):
                        for t0, n in out_segs(l):
                            if h:
                                eng.wait_ge(*at("conv_glu", l, 0))
                            eng.wait_ge(*at("full", ("conv_g", l, 2 * h + m, t0)))
                            b = bank_of(("conv_g", l, 2 * h + m, t0))
                            act(SG[:, m, t0:t0 + n], b[:, 0:n], ACT.Sigmoid).then_inc(*sc.step("conv_sg", l, h, m, t0))
                            fl.mark(("read", ("conv_g", l, 2 * h + m, t0)), sc.sem)
                norm_side("conv", l, [range(BB)], lambda m, t0, n: Y[:, m, t0:t0 + n],
                          lambda m, t0, n: SQ[:, m, t0:t0 + n],
                          lambda g, t0, n: RS[:, t0:t0 + n])
                for t0, n in out_segs(l):
                    eng.wait_ge(*at("conv_normed", l, 0, t0))
                    for m in range(BB):
                        act(YSb[:, m, t0:t0 + n], Y[:, m, t0:t0 + n], ACT.Silu, bias=par("ln_b")[:, m:m + 1],
                                  scale=par("ln_g")[:, m:m + 1]).then_inc(*sc.step())

                sc.stage(("ret", l))
                R = ret_work()
                for h in range(NH):
                    act(R["dec"][:, h, :], const("ahead"), ACT.Exp, scale=LG[:, h:h + 1]).then_inc(*sc.step())
                    act(R["dtmp"][:, h, :], const("behind"), ACT.Exp, scale=LG[:, 4 + h:5 + h]).then_inc(*sc.step("rdec", l, h))
                    for d in range(2):
                        act(R["qdec"][:, d, h, :], const("rowup" if d == 0 else "rowdown"), ACT.Exp,
                                  scale=LG[:, 4 * d + h:4 * d + h + 1]).then_inc(*sc.step())
                for tag, scale, dst in (("rk", float(P) ** -0.5, "K"), ("rq", 1.0, "Q")):
                    for m in range(BB):
                        for t0, n in (ALL_SEGS if tag == "rk" else out_segs(l)):
                            eng.wait_ge(*at("full", (tag, l, m, t0)))
                            b = bank_of((tag, l, m, t0))
                            if t0 == 0:
                                act(R[dst][:, m, 0:n], b[:, 0:n], ACT.Copy, scale=scale).then_inc(*sc.step("read", (tag, l, m, t0)))
                            else:
                                if m >= 2:
                                    eng.wait_ge(*at(tag + "_roped", l, m - 2))
                                elif tag == "rq":
                                    eng.wait_ge(*at("rk_roped", l, m + 2))
                                act(R["raw"][:, m % 2, :], b[:, 0:n], ACT.Copy, scale=scale).then_inc(*sc.step(tag + "_raw", l, m))
                                fl.mark(("read", (tag, l, m, t0)), sc.sem)
                norm_side("ret", l, [[h] for h in range(NH)], lambda m, t0, n: YSb[:, BB + m, t0:t0 + n],
                          lambda m, t0, n: R["sq"][:, m, t0:t0 + n],
                          lambda g, t0, n: R["rs"][:, g, t0:t0 + n])
                for m in range(BB):
                    for t0, n in out_segs(l):
                        eng.wait_ge(*at("full", ("rg", l, m, t0)))
                        b = bank_of(("rg", l, m, t0))
                        act(R["g"][:, m, t0:t0 + n], b[:, 0:n], ACT.Silu).then_inc(*sc.step("rgate", l, m, t0))
                        fl.mark(("read", ("rg", l, m, t0)), sc.sem)

                sc.stage(("mlstm", l))
                M = mlstm_work()
                T, A_, WP, MT, MM, EM = (M[x] for x in ("t", "a", "wp", "mt", "m", "em"))
                eng.wait_ge(*at("mabs", l))
                act(T[0:64, :], T[0:64, :], ACT.Exp, scale=-1.0).then_inc(*sc.step())
                eng.wait_ge(*sc.latest())
                act(T[0:64, :], T[0:64, :], ACT.Ln, bias=1.0).then_inc(*sc.step("mln", l))
                eng.wait_ge(*sc.latest())
                eng.wait_ge(*at("mrowlogs", l))
                act(WP[0:64, :], WP[0:64, :], ACT.Exp).then_inc(*sc.step())
                act(EM[0:64, :], MT[0:64, :], ACT.Exp, scale=-1.0).then_inc(*sc.step("mwrows", l))
                act(A_[64:128, :], T[0:64, :], ACT.Exp).then_inc(*sc.step("mrows", l))
                order_qk = [("mq", m) for m in range(BB)] + [("mk", m) for m in range(BB)]
                eng.wait_ge(*at("mpad0", l))
                for x, (tag, m) in enumerate(order_qk):
                    segs = out_segs(l) if tag == "mq" else ALL_SEGS
                    if x >= 2:
                        ptag, pm = order_qk[x - 2]
                        eng.wait_ge(*at("mconv", l, ptag, pm, SEG_LAT[0]))
                    for t0, n in segs:
                        eng.wait_ge(*at("full", (tag, l, m, t0)))
                        b = bank_of((tag, l, m, t0))
                        o = mpad_at(t0)
                        act(M["pad"][:, x % 2, o:o + n], b[:, 0:n], ACT.Copy).then_inc(*sc.step("mpad", l, tag, m, t0))
                        fl.mark(("read", (tag, l, m, t0)), sc.sem)
                for tag, m in order_qk:
                    for t0, n in (out_segs(l) if tag == "mq" else ALL_SEGS):
                        eng.wait_ge(*at("mconv", l, tag, m, t0))
                        dst = M["Q" if tag == "mq" else "K"][:, m, t0:t0 + n]
                        act(dst, dst, ACT.Silu).then_inc(*sc.step())
                fl.mark(("msilu", l), sc.sem)
                for d in range(2):
                    for c in scan_order(d):
                        if c in out_blocks(l):
                            eng.wait_ge(*at("mlogw", l, d, c))
                            act(M["e"], M["e"], ACT.Exp, scale=-1.0).then_inc(*sc.step("mexp", l, d, c))
                norm_side("mls", l, [[h] for h in range(NH)], lambda m, t0, n: YSb[:, 2 * BB + m, t0:t0 + n],
                          lambda m, t0, n: M["sq"][:, m, t0:t0 + n],
                          lambda g, t0, n: M["rs"][:, g, t0:t0 + n])
                for m in range(BB):
                    for t0, n in out_segs(l):
                        eng.wait_ge(*at("full", ("mo", l, m, t0)))
                        b = bank_of(("mo", l, m, t0))
                        act(M["g"][:, m, t0:t0 + n], b[:, 0:n], ACT.Sigmoid).then_inc(*sc.step("mogate", l, m, t0))
                        fl.mark(("read", ("mo", l, m, t0)), sc.sem)

                sc.stage(("attn", l))
                A = attn_work()
                for tag, nbk in (("ak", 1), ("aq", BB)):
                    for m in range(nbk):
                        for t0, n in (ALL_SEGS if tag == "ak" else out_segs(l)):
                            eng.wait_ge(*at("full", (tag, l, m, t0)))
                            b = bank_of((tag, l, m, t0))
                            if t0 == 0:
                                dst = A["K"][:, 0:n] if tag == "ak" else A["Q"][:, m, 0:n]
                                act(dst, b[:, 0:n], ACT.Copy).then_inc(*sc.step("read", (tag, l, m, t0)))
                            else:
                                if m >= 2:
                                    eng.wait_ge(*at("aq_roped", l, m - 2))
                                elif tag == "aq":
                                    eng.wait_ge(*at("ak_roped", l, 0))
                                act(A["raw"][:, m % 2, :], b[:, 0:n], ACT.Copy).then_inc(*sc.step(tag + "_raw", l, m))
                                fl.mark(("read", (tag, l, m, t0)), sc.sem)
                seq_th = [(t, h) for t in out_blocks(l) for h in range(AH)]
                MX, NM, SE, DN, RC, SUM = AW
                for t in out_blocks(l):
                    local = local_blocks(t)
                    nl = len(local) * P

                    def back(h):
                        if local:
                            if seq_th.index((t, h)) >= 2:
                                eng.wait_ge(*at("full", ("ay", l) + seq_th[seq_th.index((t, h)) - 2]))
                            eng.wait_ge(*at("full", ("apl", l, t, h)))
                            b = bank_of(("apl", l, t, h))
                            act(A["PT"][:, h % 2, 0:nl], b[:, 0:nl], ACT.Copy).then_inc(*sc.step("apl_moved", l, t, h))
                            fl.mark(("read", ("apl", l, t, h)), sc.sem)

                    for h in range(AH):
                        eng.wait_ge(*at("anm", l, t, h))
                        if seq_th.index((t, h)) >= 2:
                            eng.wait_ge(*at("full", ("apc", l) + seq_th[seq_th.index((t, h)) - 2]))
                        act(A["P"][:, h % 2, 0:nl + CTX], A["S"][:, h % 2, 0:nl + CTX], ACT.Exp, bias=NM[:, h:h + 1],
                                  accum_out=SUM[:, h:h + 1]).then_inc(*sc.step("ap", l, t, h))
                        act(SE[:, h:h + 1], SINK[:, h:h + 1], ACT.Exp, bias=NM[:, h:h + 1]).then_inc(*sc.step("aexp", l, t, h))
                        if h:
                            back(h - 1)
                    back(AH - 1)
                    eng.wait_ge(*at("full", ("ayT", l, t)))
                    b = bank_of(("ayT", l, t))
                    act(YSb[:, 3 * BB:4 * BB, t * P:(t + 1) * P], b[:, :].rearrange("p (m i) -> p m i", m=BB), ACT.Copy).then_inc(*sc.step("read", ("ayT", l, t)))

                sc.stage(("merge", l))
                GS = merge_work()[1]
                hist = []
                for j in range(D // W):
                    for i_ in range(4):
                        for m in range(2):
                            for t0, n in out_segs(l):
                                if len(hist) >= 4:
                                    eng.wait_ge(*at("read", ("branch",) + hist[-4]))
                                hist.append((l, j, i_, m, t0))
                                eng.wait_ge(*at("full", ("gate", l, j, i_, m, t0)))
                                b = bank_of(("gate", l, j, i_, m, t0))
                                act(GS[:, gslot(l, j, i_, m, t0), 0:n], b[:, 0:n], ACT.Sigmoid).then_inc(*sc.step("gsig", l, j, i_, m, t0))
                                fl.mark(("read", ("gate", l, j, i_, m, t0)), sc.sem)

                sc.stage(("out", l))
                sc.stage(("peernorm", l))
                SQX = YS[:, 0:D]
                for t in out_blocks(l):
                    act(SQX, Xb[:, t, :], ACT.Square, accum_out=SSQ[:, t:t + 1]).then_inc(*sc.step("ssq2", l, t))
                    eng.wait_ge(*sc.latest())
                for t in out_blocks(l):
                    eng.wait_ge(*at("rsq2", l, t))
                    act(RSB[:, t:t + 1], RSQ[:, t:t + 1], ACT.Sqrt).then_inc(*sc.step("rs2", l, t))
                    eng.wait_ge(*sc.latest())
                    eng.wait_ge(*at("full", ("hT", l, t, 0)))
                    b = bank_of(("hT", l, t, 0))
                    act(HTk[:, 0:4, t * P:(t + 1) * P], b[:, :].rearrange("p (k i) -> p k i", k=4), ACT.Copy).then_inc(*sc.step("read", ("hT", l, t, 0)))
                sc.stage(("peerq", l))
                for h in range(HEADS * 256 // W):
                    for t0, n in out_segs(l):
                        eng.wait_ge(*at("full", ("wq", l, 2 * h, t0)))
                        b = bank_of(("wq", l, 2 * h, t0))
                        act(YSb[:, 2 * h, t0:t0 + n], b[:, 0:n], ACT.Copy).then_inc(*sc.step("read", ("wq", l, 2 * h, t0)))
                sc.stage(("route", l))
                R_ = route_work()
                for x, t in enumerate(out_blocks(l)):
                    for g in range(4):
                        if x:
                            eng.wait_ge(*at("route_read", l, out_blocks(l)[x - 1]))
                        eng.wait_ge(*at("full", ("score", l, t, g)))
                        b = bank_of(("score", l, t, g))
                        act(R_["s"][:, 4 * g:4 * g + 4, :], b[:, :].rearrange("p (a k) -> p a k", a=4), ACT.Copy).then_inc(*sc.step("scored", l, t, g))
                        fl.mark(("read", ("score", l, t, g)), sc.sem)
                    eng.wait_ge(*at("cdiff", l, t))
                    act(R_["ce"], R_["ce"], ACT.Exp).then_inc(*sc.step("cexp", l, t))

                sc.stage(("peer", l))
                G = peer_work()
                for b0, nb, base in peer_calls(l):
                    with eng.Fori(0, nb) as i:
                        it = i + base

                        def gelu(h):
                            hs = slice(h * TOPK, (h + 1) * TOPK)
                            eng.wait_ge(fl.sem("dots_done"), it * SLOTS + (h + 1) * TOPK + 1)
                            act(G["act"][:, hs], G["dots"][:, hs], ACT.Gelu).then_inc(fl.sem("gelu_done"), 1)

                        def diagonals(h):
                            eng.wait_ge(fl.sem("weights_ready"), it * HEADS + h + 1)
                            for k in range(TOPK):
                                n = h * TOPK + k
                                if n >= DRING:
                                    eng.wait_ge(fl.sem("v_summed"), it * SLOTS + n - DRING + 2)
                                act(G["diag"][:, n % DRING, :], ident, ACT.Copy, scale=G["w"][:, n:n + 1])\
                                    .then_inc(fl.sem("diagonal_ready"), 1)

                        gelu(0)
                        for h in range(HEADS):
                            diagonals(h)
                            if h < HEADS - 1:
                                gelu(h + 1)
            sc.stage("final")
            SQX = YS[:, 0:D]
            for t in range(CB, NB):
                act(SQX, Xb[:, t, :], ACT.Square, accum_out=SSQ[:, t:t + 1]).then_inc(*sc.step("ssq2", DEPTH, t))
                eng.wait_ge(*sc.latest())
            for t in range(CB, NB):
                eng.wait_ge(*at("rsq2", DEPTH, t))
                act(RSB[:, t:t + 1], RSQ[:, t:t + 1], ACT.Sqrt).then_inc(*sc.step("rs2", DEPTH, t))
                eng.wait_ge(*sc.latest())
            sc.finish()

        @block.gpsimd
        def _(eng):
            po = Engine(eng, "gpsimd")
            po.stage("mod")
            for name in ("dots_done", "v_summed", "residual_added"):
                eng.sem_inc(fl.sem(name), 1)
            fl.done(nc.gpsimd.memset(AW_EPS, EPS), "eps_set", ("eps",))
            fl.done(nc.gpsimd.memset(GB, 0.0), "gb_zero", ("gb_zero",))
            MR, MB = work(6 * D, 6 * D)

            def dma(dst, src, sem, step=None):
                fl.done(eng.dma_start(dst, src), sem, step, by=16)

            for l in range(DEPTH):
                if l:
                    eng.wait_ge(*at("mod_rows", l - 1))
                dma(MB[0:2, :], ins["mod_b"][l:l + 1, :].to_broadcast([2, 6 * D]), "mod_bias_loaded", ("mod_b", l))
                eng.wait_ge(*at("mod_rows", l))
                dma(modr[l], MR[0:2, :], "mod_rows_stored", ("mod_stored", l))
            eng.wait_ge(*at("mod_stored", DEPTH - 1))
            eng.sem_inc(*po.step())
            for l in range(DEPTH):
                po.stage(("norm", l))
                po.stage(("conv", l))
                po.stage(("ret", l))
                po.stage(("mlstm", l))
                M = mlstm_work()
                if l == 0:
                    eng.wait_ge(*at("gb_zero"))
                for x, (kind, p0) in enumerate(((0, 0), (2, 32))):
                    dma(GB[p0:p0 + 4, 0:1], ins["mlstm_gate_b"][l, kind].rearrange("(h o) -> h o", o=1), "gate_bias_loaded")
                    dma(GB[64 + p0:64 + p0 + 4, 1:2], ins["mlstm_gate_b"][l, kind + 1].rearrange("(h o) -> h o", o=1),
                        "gate_bias_loaded")
                fl.mark(("gate_bias", l), "gate_bias_loaded")
                eng.wait_ge(*at("mwrows", l))
                for d in range(2):
                    for kind, rows in enumerate((M["m"], M["wp"], M["em"])):
                        dma(rowsd[d, :, kind].rearrange("c (h i) -> h c i", h=NH),
                            rows[32 * d:32 * d + 4, :].rearrange("h (c i) -> h c i", c=NB), "rows_stored")
                fl.mark(("rows_stored", l), "rows_stored")
                eng.wait_ge(*at("rows_stored", l))
                seq = [(d, c) for d in range(2) for c in scan_order(d)]
                for x, (d, c) in enumerate(seq):
                    if x >= 2:
                        eng.wait_ge(*at("mbc_used", l, *seq[x - 2]))
                    else:
                        eng.wait_ge(*at("mrows", l))
                        for cc in range(NB):
                            eng.wait_ge(*at("full", ("mcols", l, cc)))
                    n_ = x % NB
                    dma(M["bc"][:, n_ % 2, :], rowsd[d:d + 1, c].rearrange("o k n -> o (k n)").partition_broadcast(P)
                        .rearrange("p o n -> p (o n)"),
                        f"row_copies_loaded{n_ % 2}", ("mbc", l, d, c))
                po.stage(("attn", l))
                po.stage(("merge", l))
                po.stage(("out", l))
                po.stage(("peernorm", l))
                po.stage(("peerq", l))
                po.stage(("route", l))
                po.stage(("peer", l))
                G = peer_work()
                utab = ins["peer_u"]
                vtab = ins["peer_v"]
                for b0, nb, base in peer_calls(l):
                    with eng.Fori(0, nb) as i:
                        it = i + base
                        eng.wait_ge(fl.sem("indices_staged"), it + 1)
                        eng.wait_ge(fl.sem("dots_done"), it * SLOTS + 1)
                        eng.wait_ge(fl.sem("v_summed"), it * SLOTS + 1)
                        eng.sem_inc(fl.sem("gathers_allowed"), 1)
                        for h in range(HEADS + 1):
                            for k in range(TOPK):
                                n = h * TOPK + k
                                if h < HEADS:
                                    if n >= URING:
                                        eng.wait_ge(fl.sem("dots_done"), it * SLOTS + n - URING + 2)
                                        eng.sem_inc(fl.sem("gathers_allowed"), 1)
                                    eng.indirect_dma_start(G["u"][n % URING], None, utab,
                                                           bass.IndirectOffsetOnAxis(G["idxb"][:, n:n + 1], 0))\
                                        .then_inc(fl.sem(f"u_landed{n % URING}"), 16)
                                if h:
                                    n -= TOPK
                                    if n >= VRING:
                                        eng.wait_ge(fl.sem("v_summed"), it * SLOTS + n - VRING + 2)
                                        eng.sem_inc(fl.sem("gathers_allowed"), 1)
                                    eng.indirect_dma_start(G["v"][n % VRING], None, vtab,
                                                           bass.IndirectOffsetOnAxis(G["idxb"][:, n:n + 1], 0))\
                                        .then_inc(fl.sem(f"v_landed{n % VRING}"), 16)
            po.stage("final")
            po.finish()

        @block.sync
        def _(eng):
            def dma(dst, src, sem, step=None, slow=False):
                fl.done(eng.dma_start(dst, src, allow_slow_non_contiguous=slow), sem, step, by=16)

            dma(CT, ins["consts"], "params_loaded")
            dma(Xb[:, 0:CB, :], ins["ctx"][0].rearrange("(b p) d -> p b d", p=P), "params_loaded")
            dma(Xb[:, CB:NB, :], ins["x"][0].rearrange("(b p) d -> p b d", p=P), "params_loaded")
            dma(SIL, ins["cvec"], "params_loaded")
            fl.mark(("params",), "params_loaded")

            def layer_vectors(l):
                if l:
                    for e in ENG:
                        eng.wait_ge(*at("end", e, ("route", l - 1)))
                eng.wait_ge(*at("mod_stored", l))
                if l == 0:
                    eng.wait_ge(*at("mod_stored", 0))
                dma(PR, ins["params"][l], "layer_loaded")
                dma(LG, ins["ret_decay"][l].rearrange("(o d) h -> o (d h)", o=1).to_broadcast([P, 8]), "layer_loaded")
                dma(SINK, ins["attn_sink"][l:l + 1, :].to_broadcast([P, AH]), "layer_loaded")
                dma(KEYT, ins["keysT"][l], "layer_loaded")
                for s in range(2):
                    for dst, part in ((SH1, 0), (SC1, 1)):
                        dma(dst[:, s * KD:(s + 1) * KD], modr[l, s, part * D:(part + 1) * D].rearrange("(k p) -> p k", p=P),
                            "layer_loaded", slow=True)
                fl.mark(("layer", l), "layer_loaded")

            for n, (name, parts) in enumerate(PLAN):
                if n >= RING:
                    eng.wait_ge(*at("used", PLAN[n - RING][0]))
                for dst, src in parts:
                    dma(dst(WRr[:, n % RING, :]), src, f"weights_loaded{n % RING}")
                fl.mark(("loaded", name), f"weights_loaded{n % RING}")
                l = name[1]
                if name[0] == "mod" and l == DEPTH - 1 and name[2] == 6 * D // W - 1:
                    layer_vectors(0)
                if name == ("branch", l, 0, 3):
                    for e in ENG:
                        eng.wait_ge(*at("end", e, ("attn", l)))
                    GA = merge_work()[3]
                    for s in range(2):
                        dma(GA[:, s * D:(s + 1) * D], modr[l, s:s + 1, 2 * D:3 * D].to_broadcast([P, D]), "ga1_loaded")
                    fl.mark(("ga1", l), "ga1_loaded")
                if name == ("out", l, D // W - 1):
                    for e in ENG:
                        eng.wait_ge(*at("end", e, ("out", l)))
                    _, SC2, SH2, G2 = work(NB * D, 2 * D, 2 * D, D)
                    for s in range(2):
                        dma(SC2[:, s * D:(s + 1) * D], modr[l, s:s + 1, 4 * D:5 * D].to_broadcast([P, D]), "mod2_loaded")
                        dma(SH2[:, s * D:(s + 1) * D], modr[l, s:s + 1, 3 * D:4 * D].to_broadcast([P, D]), "mod2_loaded")
                    dma(G2, ins["norm2_g"][l:l + 1, :].to_broadcast([P, D]), "mod2_loaded")
                    fl.mark(("mod2", l), "mod2_loaded")
                if name == ("wq", l, HEADS * 256 // W - 1):
                    for e in ENG:
                        eng.wait_ge(*at("end", e, ("route", l)))
                    G = peer_work()
                    for s in range(2):
                        dma(G["ga"][:, s * D:(s + 1) * D], modr[l, s:s + 1, 5 * D:6 * D].to_broadcast([P, D]), "ga2_loaded")
                    fl.mark(("ga2", l), "ga2_loaded")
                    if l + 1 < DEPTH:
                        layer_vectors(l + 1)
            for e in ENG:
                eng.wait_ge(*at("end", e, ("peer", DEPTH - 1)))
            dma(work(D)[0], ins["final_g"].rearrange("(o d) -> o d", o=1).to_broadcast([P, D]), "final_g_loaded", ("final_g",))
            for t in range(CB, NB):
                eng.wait_ge(*at("result", t))
                dma(out[0, (t - CB) * P:(t - CB + 1) * P, :], Xb[:, t, :], "result_stored")
            fl.mark(("stored",), "result_stored")
            if known is not None:
                eng.wait_ge(fl.sem("result_stored"), fl.count["result_stored"])
        fl.marks["banks"] = dict(banks_of)
        return fl.marks


def program(nc, ins, out, known):
    scratch = {"mod_rows": nc.dram_tensor("mod_rows", (DEPTH, 2, 6 * D), F32).ap(),
               "mlstm_rows": nc.dram_tensor("mlstm_rows", (2, NB, 3, BR), F32).ap()}
    return build(nc, {**ins, **scratch}, out, known)


def _arrays(i):
    def chan(a):
        a = np.atleast_2d(a)
        return a.T.reshape(-1, P, a.shape[0]).transpose(1, 0, 2).reshape(P, -1)

    f = {k: np.ascontiguousarray(v) for k, v in i.items()}
    params = np.stack([np.concatenate([chan(f["norm1_g"][l]), chan(f["conv_w"][l]), chan(f["conv_b"][l]),
                                       chan(f["conv_ln_g"][l]), chan(f["conv_ln_b"][l]), chan(f["mlstm_conv_w"][l]),
                                       chan(f["mlstm_conv_b"][l])], axis=1) for l in range(DEPTH)])
    a = {k: f[k] for k in ("x", "ctx", "mod_w", "mod_b", "w_in", "ret_decay", "mlstm_gate_b", "attn_sink", "w_branch",
                           "w_out", "peer_wq", "norm2_g", "final_g")}
    a["cvec"] = chan(np.stack([f["c"][0], f["c_ctx"]]))
    a["params"] = params
    a["keysT"] = f["peer_keys"].transpose(0, 3, 1, 2).reshape(DEPTH, P, 2 * KEYS)
    a["peer_u"] = f["peer_u"].reshape(DEPTH * EXPERTS, D)
    a["peer_v"] = f["peer_v"].reshape(DEPTH * EXPERTS, D)
    a["consts"] = const_table()
    return {k: np.ascontiguousarray(v) for k, v in a.items()}


def kernel(**inputs):
    import concourse.bacc as bacc
    from concourse.bass_utils import run_bass_kernel_spmd as run

    arrays = _arrays(inputs)
    known = None
    for _ in range(2):
        nc = bacc.Bacc("TRN2", target_bir_lowering=False, num_devices=1)
        ins = {k: nc.dram_tensor(f"in_{k}", a.shape, F32, kind="ExternalInput").ap() for k, a in arrays.items()}
        out = nc.dram_tensor("out_0", (1, LAT, D), F32, kind="ExternalOutput").ap()
        known = program(nc, ins, out, known)
    r = run(nc, [{f"in_{k}": a for k, a in arrays.items()}], core_ids=[0])
    return r.results[0]["out_0"]
```

```python
from contextlib import ExitStack

import numpy as np
import concourse.bass as bass
from concourse import mybir

P = 128
D = 1024
KD = D // P
CTX, LAT = 256, 512
TOK = CTX + LAT
NB = TOK // P
CB = CTX // P
DEPTH = 2
GRID_W = 64
BR = 512
BB = BR // P
NH = 4
TAPS = 31
AH, AD, AKV = 8, 64, 2
EPS = 1e-6
NEG = -1e30
HEADS, TOPK, KEYS = 8, 16, 128
EXPERTS = KEYS * KEYS
SLOTS = HEADS * TOPK
NSCORE = 2 * HEADS * KEYS
P_IN = 10000
C_CONV_A, C_CONV_G = 0, 512
C_RQ, C_RK, C_RV, C_RG = 1024, 1536, 2048, 2560
C_MQ, C_MK, C_MV, C_MO, C_MG = 3072, 3584, 4096, 4608, 5120
C_AQ, C_AK = 5136, 5648
C_GATE = 5904
W = 256
RING = 4
CPAD = TOK + 4 * (TAPS // 2)
MPAD = TOK + 4
BANKS = 8
URING, VRING, DRING = 8, 8, 8

F32 = mybir.dt.float32
U32 = mybir.dt.uint32
ALU = mybir.AluOpType
ACT = mybir.ActivationFunctionType
AX = mybir.AxisListType.X

SEG_CTX, SEG_LAT = (0, CTX), (CTX, LAT)


def out_segs(l):
    return [SEG_CTX, SEG_LAT] if l < DEPTH - 1 else [SEG_LAT]


def out_blocks(l):
    return list(range(NB)) if l < DEPTH - 1 else list(range(CB, NB))


ALL_SEGS = [SEG_CTX, SEG_LAT]

CONST = {}


def const_table():
    parts, at = [], 0

    def put(name, a):
        nonlocal at
        a = np.broadcast_to(np.asarray(a, np.float32), (P, a.shape[-1]))
        CONST[name] = (at, a.shape[-1])
        parts.append(a)
        at += a.shape[-1]

    i = np.arange(P)
    put("ident", np.eye(P))
    for name, dim in (("R", P), ("A", AD)):
        nf = dim // 4
        freqs = np.float32(10000.0) ** (-np.arange(nf, dtype=np.float32) / np.float32(nf))
        d = i % dim
        first = (d % (2 * nf)) < nf
        pos = np.where((d < dim // 2)[:, None], (np.arange(LAT) // GRID_W)[None], (np.arange(LAT) % GRID_W)[None])
        ang = pos.astype(np.float32) * freqs[d % nf][:, None].astype(np.float32)
        put("cos" + name, np.cos(ang))
        put("sin" + name, np.sin(ang))
        perm = np.zeros((P, P))
        for p in range(P):
            perm[p + nf if first[p] else p - nf, p] = -1.0 if first[p] else 1.0
        put("perm" + name, perm)
    put("until", (i[:, None] <= i[None]) * 1.0)
    put("since", (i[:, None] >= i[None]) * 1.0)
    put("ahead", np.maximum(i[None] - i[:, None], 0))
    put("behind", np.maximum(i[:, None] - i[None], 0))
    put("maskprev", np.where(i[None] >= i[:, None], 0.0, NEG))
    put("masknext", np.where(i[None] <= i[:, None], 0.0, NEG))
    put("ones", np.ones((P, P)))
    put("mean512", np.full((P, P), 1.0 / BR))
    put("mean128", np.full((P, P), 1.0 / P))
    put("iota16", np.arange(TOPK)[None])
    put("rowup", (i + 1.0)[None])
    put("rowdown", (float(P) - i)[None])
    put("coldown", (P - 1.0 - i)[:, None])
    put("colup", (i * 1.0)[:, None])
    return np.concatenate(parts, axis=1)


const_table()
NCONST = sum(n for _, n in CONST.values())

PAR, _at = {}, 0
for _n, _w in (("n1g", KD), ("conv_w", BB * TAPS), ("conv_b", BB), ("ln_g", BB), ("ln_b", BB),
               ("mconv_w", 8 * 3), ("mconv_b", 8)):
    PAR[_n] = (_at, _w)
    _at += _w
NPAR = _at


def scan_order(d):
    return list(range(NB)) if d == 0 else list(range(CB - 1, -1, -1)) + list(range(NB - 1, CB - 1, -1))


def pad_at(t0):
    h = TAPS // 2
    return h if t0 == 0 else h + CTX + 2 * h


def mpad_at(t0):
    return 1 if t0 == 0 else 1 + CTX + 2


def chunk_slice(d, c):
    if d == 0:
        return slice(c * P, (c + 1) * P)
    return slice((c + 1) * P - 1, c * P - 1 if c else None, -1)


def gslot(l, j, i, m, t0):
    segs = out_segs(l)
    return (((j * 4 + i) * 2 + m) * len(segs) + [s[0] for s in segs].index(t0)) % 4


def local_blocks(t):
    return [] if t < CB else [j for j in (t - 1, t, t + 1) if CB <= j < NB]


def peer_calls(l):
    return [(0, CB, 0), (CB, NB - CB, CB)] if l == 0 else [(CB, NB - CB, NB + (l - 1) * (NB - CB))]


def q_segs(l, part):
    if l == 0:
        return [[SEG_CTX], [SEG_LAT]][part]
    return [[(CTX, P)], [(CTX + P, LAT - P)]][part]


def routed(l, it):
    return it + l


class Flow:

    def __init__(self, nc, ctx, known):
        self.nc, self.ctx, self.known = nc, ctx, known
        self.sems, self.count, self.marks = {}, {}, {}

    def sem(self, name):
        if name not in self.sems:
            self.sems[name] = self.ctx.enter_context(self.nc.semaphore(name))
            self.count[name] = 0
        return self.sems[name]

    def done(self, ins, sem, step=None, by=1):
        ins.then_inc(self.sem(sem), by)
        self.count[sem] += by
        if step is not None:
            self.marks[step] = (sem, self.count[sem])
        return ins

    def at(self, *step):
        sem, value = self.known[step] if self.known else ("first_building", 1)
        return self.sem(sem), value

    def mark(self, step, sem):
        self.sem(sem)
        self.marks[step] = (sem, self.count[sem])


def build(nc, ins, out, known):
    ctx = ExitStack()
    with ctx:
        fl = Flow(nc, ctx, known)
        at = fl.at
        arena = ctx.enter_context(nc.sbuf_tensor("arena", [P, 53100], F32))
        top = [0]

        def take(n):
            a = arena[:, top[0]:top[0] + n]
            top[0] += n
            assert top[0] <= 53100, top[0]
            return a

        banks = [ctx.enter_context(nc.psum_tensor(f"bank{i}", [P, 512], F32)) for i in range(8)]

        X = take(NB * D)
        YS = take(4 * BB * TOK)
        HT = take(KD * TOK)
        WR = take(RING * KD * W)
        CT = take(NCONST)
        PR = take(NPAR)
        SM = take(460)
        WK0 = top[0]
        WKN = 53100 - WK0
        WK = arena[:, WK0:53100]

        ST0 = (NB * D + 4 * BB * TOK + KD * TOK + RING * KD * W) - (NB - 1) * NSCORE
        STORE = arena[:, ST0:ST0 + NB * NSCORE]
        assert NCONST >= NSCORE

        Xb = X.rearrange("p (b d) -> p b d", b=NB)
        HTk = HT.rearrange("p (k t) -> p k t", k=KD)
        YSb = YS.rearrange("p (b t) -> p b t", b=4 * BB)
        WRr = WR.rearrange("p (r n) -> p r n", r=RING)

        def const(name):
            at, n = CONST[name]
            return CT[:, at:at + n]

        def par(name):
            at, n = PAR[name]
            return PR[:, at:at + n]

        sm_at = [0]

        def small(n):
            a = SM[:, sm_at[0]:sm_at[0] + n]
            sm_at[0] += n
            assert sm_at[0] <= 460
            return a

        SIL = small(KD * 2)
        SC1, SH1 = small(2 * KD), small(2 * KD)
        LG, KDEC, CDEC = small(8), small(8), small(8)
        SINK = small(AH)
        GB = small(2)
        SSQ, RSQ, RSB = small(NB), small(NB), small(NB)
        T8 = [small(8) for _ in range(3)]
        AW = [small(8) for _ in range(6)]
        KEYT = small(2 * KEYS)

        ident = const("ident")

        def work(*sizes):
            at, got = 0, []
            for n in sizes:
                got.append(WK[:, at:at + n])
                at += n
            assert at <= WKN, (at, WKN)
            return got

        def blocks4(a, b=BB):
            return a.rearrange("p (b t) -> p b t", b=b)

        def conv_work():
            at_sg = BB * CPAD
            return (blocks4(X[:, 0:BB * CPAD]), blocks4(YS[:, 0:BB * TOK]), blocks4(X[:, at_sg:at_sg + 2 * TOK], 2),
                    blocks4(X[:, 0:BB * TOK]), X[:, at_sg + 2 * TOK:at_sg + 3 * TOK])

        def ret_work():
            q, k, v_, raw, dec, dtmp, qdec, att, qd, kd = work(BB * TOK, BB * TOK, NB * BR, 2 * LAT, BR, BR, 2 * BR,
                                                               BR, 2 * BR, BR)
            st = YS[:, 2 * BB * TOK:4 * BB * TOK]
            return dict(Q=blocks4(q), K=blocks4(k), V=blocks4(v_, NB), raw=blocks4(raw, 2), dec=blocks4(dec),
                        dtmp=blocks4(dtmp), qdec=qdec.rearrange("p (d h i) -> p d h i", d=2, h=NH), att=blocks4(att),
                        qd=qd.rearrange("p (d h i) -> p d h i", d=2, h=NH), kd=blocks4(kd),
                        kt=blocks4(YS[:, BB * TOK:2 * BB * TOK], NB),
                        S=st.rearrange("p (n h e) -> p n h e", n=2 * NB, h=NH),
                        sq=blocks4(st[:, 0:BB * TOK]), rs=blocks4(st[:, BB * TOK:]), g=blocks4(k))

        def mlstm_work():
            q, k, v_, pad, c_, n_, cols, m0, bc = work(BB * TOK, BB * TOK, NB * BR, 2 * MPAD, 2 * BR, 2 * NH, NB * P, 8,
                                                       2 * 3 * BR)
            ys = YS[:, 2 * BB * TOK:4 * BB * TOK]
            row = [ys[:, x * TOK:(x + 1) * TOK] for x in range(8)]
            t = [[blocks4(a[:, x * BR:(x + 1) * BR]) for a in (ys[:, BB * TOK:], X)] for x in range(5)]
            c2, n2 = X[:, 6 * BR:8 * BR], X[:, 8 * BR:8 * BR + 2 * NH]
            return dict(Q=blocks4(q), K=blocks4(k), V=blocks4(v_, NB), pad=blocks4(pad, 2),
                        C=[a.rearrange("p (x h e) -> p x h e", x=2, h=NH) for a in (c_, c2)],
                        N=[blocks4(a, 2) for a in (n_, n2)], cols=blocks4(cols, NB),
                        m0=m0, bc=blocks4(bc, 2), em=bc[:, 0:TOK], gw=blocks4(bc[:, TOK:TOK + KD * P], KD),
                        **dict(zip(("i", "f", "b", "mt", "t", "a", "m", "wp"), row)),
                        **dict(zip(("e", "s", "qw", "nb", "kw"), t)),
                        den=[a[:, 5 * BR:6 * BR] for a in (ys[:, BB * TOK:], X)],
                        sq=blocks4(v_), rs=blocks4(bc), g=blocks4(k), Kf=k)

        def attn_work():
            q, k, v_, raw, s_, p_, pt, y = work(BB * TOK, TOK, NB * P, 2 * LAT, 2 * 5 * P, 2 * 5 * P, 2 * 5 * P, 2 * BR)
            return dict(Q=blocks4(q), K=k, V=blocks4(v_, NB), raw=blocks4(raw, 2), S=blocks4(s_, 2), P=blocks4(p_, 2),
                        PT=blocks4(pt, 2), Y=blocks4(y, 2))

        def merge_work():
            gs, prd, _, acc, ga, tmp = work(4 * LAT, LAT, NB * D - 5 * LAT, KD * TOK, 2 * D, 2 * W)
            return blocks4(acc, KD), blocks4(gs, 4), prd, ga, tmp

        def out_work():
            y = [YS[:, x * D:(x + 1) * D] for x in range(6)]
            return WK[:, 0:NB * D].rearrange("p (b d) -> p b d", b=NB), YS[:, 0:2 * D], YS[:, 2 * D:4 * D], y[4], y[5]

        def peer_work():
            (h2, ga, hb, iu, iv, gb, dots, ac, w_, dg, inx, gnx, s_, sv, si, sif, cand, cand2, cv, ci, cu, cf, i1, i2,
             ce, cs) = work(NB * D, 2 * D, D, SLOTS, SLOTS, SLOTS, SLOTS, SLOTS, SLOTS, DRING * P, SLOTS, SLOTS,
                            NSCORE, 256, 256, 256, 256, 256, SLOTS, SLOTS, SLOTS, SLOTS, SLOTS, SLOTS, SLOTS, HEADS)
            ring = [YS[:, x * D:(x + 1) * D] for x in range(12)] + [HT[:, x * D:(x + 1) * D] for x in range(4)]
            return dict(H2=h2, ga=ga, hb=hb, idxu=iu.bitcast(U32), idxv=iv.bitcast(U32), gateb=gb, dots=dots, act=ac,
                        w=w_, diag=blocks4(dg, DRING), u=ring[:URING], v=ring[URING:URING + VRING],
                        idx=inx.bitcast(U32), gate=gnx,
                        sf=s_, s=blocks4(s_, 16), oh=blocks4(s_, SLOTS), s2=[cand2[:, 0:KEYS], cand2[:, KEYS:]],
                        sv=blocks4(sv, 16), si=si.bitcast(U32), si3=blocks4(si.bitcast(U32), 16), siff=sif,
                        sif=blocks4(sif, 16), cand=cand, cand2=cand2, cv=blocks4(cv, HEADS), cif=ci.bitcast(U32),
                        ci=blocks4(ci.bitcast(U32), HEADS), cu=cu.bitcast(U32), cf=cf, i1=i1, i2=i2,
                        ce=blocks4(ce, HEADS), csum=cs)

        w_in = ins["w_in"]
        modr = ins["mod_rows"]
        rowsd = ins["mlstm_rows"]

        def w_view(a, k):
            return a.rearrange("(k p) n -> p k n", p=P)

        PLAN = []

        def plan(name, parts):
            PLAN.append((name, parts))

        def whole(src, k=KD):
            return [(lambda w: w[:, 0:k * W].rearrange("p (k n) -> p k n", k=k), src)]

        for l in range(DEPTH):
            for c in range(6 * D // W):
                plan(("mod", l, c), whole(w_view(ins["mod_w"][l], KD)[:, :, c * W:(c + 1) * W]))
        for l in range(DEPTH):
            v = w_view(w_in[l], KD)

            def cols(c0):
                return whole(v[:, :, c0:c0 + W])

            for h in range(2):
                plan(("conv_g", l, h), cols(C_CONV_G + h * W))
                plan(("conv_a", l, h), cols(C_CONV_A + h * W))
            for tag, c0 in (("rk", C_RK), ("rv", C_RV), ("rq", C_RQ), ("rg", C_RG),
                            ("mgate", None), ("mq", C_MQ), ("mk", C_MK), ("mv", C_MV), ("mo", C_MO)):
                if tag == "mgate":
                    plan((tag, l, 0), [(lambda w: w[:, 0:KD * 16].rearrange("p (k n) -> p k n", k=KD),
                                        v[:, :, C_MG:C_MG + 16])])
                    continue
                for h in range(2):
                    plan((tag, l, h), cols(c0 + h * W))
            plan(("akv", l, 0), cols(C_AK))
            for h in range(2):
                plan(("aq", l, h), [
                    ((lambda w, b=b, g=g: w[:, 0:KD * W].rearrange("p (k n) -> p k n", k=KD)
                      [:, :, b * P + g * AD:b * P + (g + 1) * AD]),
                     v[:, :, C_AQ + (g * 4 + 2 * h + b) * AD:C_AQ + (g * 4 + 2 * h + b + 1) * AD])
                    for b in range(2) for g in range(2)])
            for j in range(D // W):
                for i in range(4):
                    plan(("gate", l, j, i), cols(C_GATE + i * D + j * W))
                    plan(("branch", l, j, i), whole(w_view(ins["w_branch"][l, i], BB)[:, :, j * W:(j + 1) * W], BB))
            for j in range(D // W):
                plan(("out", l, j), whole(w_view(ins["w_out"][l], KD)[:, :, j * W:(j + 1) * W]))
            for part in range(2):
                for j in range(HEADS * 256 // W):
                    plan((f"wq{part}", l, j), whole(w_view(ins["peer_wq"][l], KD)[:, :, j * W:(j + 1) * W]))
        SLOT = {name: n for n, (name, _) in enumerate(PLAN)}

        stage_names = ["mod"]
        for l in range(DEPTH):
            stage_names += [(s, l) for s in ("norm", "ret", "mlstm", "attn", "merge", "out", "peerq", "route",
                                             "peer")]
        stage_names.append("final")
        ENG = ("tensor", "vector", "scalar", "gpsimd")

        class Engine:

            def __init__(self, eng, name):
                self.eng, self.name, self.sem, self.first = eng, name, None, True

            def stage(self, s):
                if self.sem is not None:
                    self.finish()
                n = stage_names.index(s)
                label = s if isinstance(s, str) else f"{s[0]}{s[1]}"
                self.stg, self.sem = s, f"{label}_{self.name}"
                fl.sem(self.sem)
                for other in ENG if n else ():
                    self.eng.wait_ge(*at("end", other, stage_names[n - 1]))

            def finish(self):
                fl.mark(("end", self.name, self.stg), self.sem)
                if self.stg[0] == "peerq" and self.name == "vector":
                    fl.sem("indices_staged")
                    fl.marks[("end", self.name, self.stg)] = ("indices_staged", routed(self.stg[1], peer_calls(self.stg[1])[0][2]) + 1)
                if self.stg[0] == "peer" and self.name == "vector":
                    b0, nb, base = peer_calls(self.stg[1])[-1]
                    fl.sem("residual_added")
                    fl.marks[("end", self.name, self.stg)] = ("residual_added", base + nb + 1)

            def step(self, *step):
                fl.count[self.sem] += 1
                if step:
                    fl.marks[step] = (self.sem, fl.count[self.sem])
                return fl.sem(self.sem), 1

            def latest(self, but=0):
                return fl.sem(self.sem), fl.count[self.sem] - but

        class Routing:

            def __init__(self, blocks_before):
                self.before, self.n = blocks_before * (known["route_steps"][1] if known else 1), 0

            def step(self):
                self.n += 1
                return fl.sem("route_steps"), 1

            def latest(self, but=0):
                return fl.sem("route_steps"), self.before + (self.n - but)

        AW_EPS = small(1)
        block = ctx.enter_context(nc.Block())
        banks_of = {} if known is None else known["banks"]
        order = []

        def bank_of(name):
            return banks[banks_of[name]]

        @block.tensor
        def _(eng):
            pe = Engine(eng, "tensor")
            mm = nc.tensor.matmul

            def bank(name):
                g = len(order)
                order.append(name)
                banks_of[name] = g % BANKS
                if g >= BANKS:
                    eng.wait_ge(*at("read", order[g - BANKS]))
                return banks[g % BANKS]

            def weight(name, k=KD):
                n = SLOT[name]
                eng.wait_ge(*at("loaded", name))
                return WRr[:, n % RING, 0:k * W].rearrange("p (k n) -> p k n", k=k)

            def used(name):
                fl.mark(("used", name), pe.sem)

            def project(tag, l, h, segs):
                w = weight((tag, l, h))
                for m in range(2):
                    for t0, n in segs:
                        b = bank((tag, l, 2 * h + m, t0))
                        for k in range(KD):
                            i = mm(b[:, 0:n], w[:, k, m * P:(m + 1) * P], HTk[:, k, t0:t0 + n],
                                   start=(k == 0), stop=(k == KD - 1))
                        i.then_inc(*pe.step("full", (tag, l, 2 * h + m, t0)))
                used((tag, l, h))

            def project_tok(tag, l, h, c0, n):
                w = weight((tag, l, h))
                for t in range(NB):
                    b = bank((tag + "_tok", l, h, t))
                    for k in range(KD):
                        i = mm(b[:, 0:n], HTk[:, k, t * P:(t + 1) * P], w[:, k, c0:c0 + n],
                               start=(k == 0), stop=(k == KD - 1))
                    i.then_inc(*pe.step("full", (tag + "_tok", l, h, t)))

            def rotate(tag, l, ms, perm, src):
                for m in ms:
                    b = bank((tag + "_rot", l, m))
                    eng.wait_ge(*at(tag + "_raw", l, m))
                    mm(b[:, :], const(perm), src(m), start=True, stop=True).then_inc(*pe.step("full", (tag + "_rot", l, m)))

            def norm_sums(tag, l, groups, y, sq, mean):
                for what, src in (("mean", y), ("var", sq)):
                    for t0, n in out_segs(l):
                        for g, blocks in enumerate(groups):
                            b = bank((tag, what, l, g, t0))
                            eng.wait_ge(*at(tag + "_" + what, l, g, t0))
                            for j, m in enumerate(blocks):
                                i = mm(b[:, 0:n], const(mean), src(m, t0, n), start=(j == 0), stop=(j == len(blocks) - 1))
                            i.then_inc(*pe.step("full", (tag, what, l, g, t0)))

            pe.stage("mod")
            eng.wait_ge(*at("params"))
            eng.wait_ge(*at("silu_c"))
            for l in range(DEPTH):
                for c in range(6 * D // W):
                    w = weight(("mod", l, c))
                    b = bank(("mod", l, c))
                    for k in range(KD):
                        i = mm(b[0:2, 0:W], SIL[:, 2 * k:2 * k + 2], w[:, k, :], start=(k == 0), stop=(k == KD - 1))
                    i.then_inc(*pe.step("full", ("mod", l, c)))
                    used(("mod", l, c))

            for l in range(DEPTH):
                pe.stage(("norm", l))
                xn = work(D, D)
                for t in range(NB):
                    for half in range(2):
                        b = bank(("xT", l, t, half))
                        eng.wait_ge(*at("xn", l, t))
                        for k in range(4):
                            i = nc.tensor.transpose(b[:, k * P:(k + 1) * P],
                                                    xn[t % 2][:, (half * 4 + k) * P:(half * 4 + k + 1) * P], ident)
                        i.then_inc(*pe.step("full", ("xT", l, t, half)))

                pe.stage(("ret", l))
                R = ret_work()
                CP, Y, SG, SQ, RS = conv_work()
                for h in range(2):
                    project("conv_g", l, h, out_segs(l))
                    project("conv_a", l, h, out_segs(l))
                for h in range(2):
                    project("rk", l, h, ALL_SEGS)
                    rotate("rk", l, (2 * h, 2 * h + 1), "permR", lambda m: R["raw"][:, m % 2, :])
                for h in range(2):
                    project_tok("rv", l, h, 0, W)
                    used(("rv", l, h))
                for h in range(2):
                    project("rq", l, h, out_segs(l))
                    rotate("rq", l, (2 * h, 2 * h + 1), "permR", lambda m: R["raw"][:, m % 2, :])
                norm_sums("conv", l, [range(BB)], lambda m, t0, n: Y[:, m, t0:t0 + n],
                          lambda m, t0, n: SQ[:, m, t0:t0 + n], "mean512")
                for c in range(NB):
                    b = bank(("rkT", l, c))
                    eng.wait_ge(*at("rk_ready", l))
                    for h in range(NH):
                        i = nc.tensor.transpose(b[:, h * P:(h + 1) * P], R["K"][:, h, c * P:(c + 1) * P], ident)
                    i.then_inc(*pe.step("full", ("rkT", l, c)))
                for d, chunks in ((0, scan_order(0)), (1, scan_order(1))):
                    for c in chunks[:-1]:
                        b = bank(("rS", l, d, c))
                        eng.wait_ge(*at("rkd", l, d, c))
                        for h in range(NH):
                            i = mm(b[:, h * P:(h + 1) * P], R["kd"][:, h, :], R["V"][:, c, h * P:(h + 1) * P],
                                   start=True, stop=True)
                        i.then_inc(*pe.step("full", ("rS", l, d, c)))
                for c in out_blocks(l):
                    b = bank(("rkq", l, c))
                    eng.wait_ge(*at("rq_ready", l))
                    for h in range(NH):
                        i = mm(b[:, h * P:(h + 1) * P], R["K"][:, h, c * P:(c + 1) * P], R["Q"][:, h, c * P:(c + 1) * P],
                               start=True, stop=True)
                    i.then_inc(*pe.step("full", ("rkq", l, c)))
                    b = bank(("ro", l, c))
                    eng.wait_ge(*at("ratt", l, c))
                    dirs = [d for d in range(2) if scan_order(d)[0] != c]
                    for h in range(NH):
                        i = mm(b[:, h * P:(h + 1) * P], R["V"][:, c, h * P:(h + 1) * P], R["att"][:, h, :],
                               start=True, stop=not dirs)
                        for d in dirs:
                            i = mm(b[:, h * P:(h + 1) * P], R["S"][:, d * NB + c, h, :], R["qd"][:, d, h, :],
                                   start=False, stop=d == dirs[-1])
                    i.then_inc(*pe.step("full", ("ro", l, c)))
                norm_sums("ret", l, [[h] for h in range(NH)], lambda m, t0, n: YSb[:, BB + m, t0:t0 + n],
                          lambda m, t0, n: R["sq"][:, m, t0:t0 + n], "mean128")
                for h in range(2):
                    project("rg", l, h, out_segs(l))

                pe.stage(("mlstm", l))
                M = mlstm_work()
                eng.wait_ge(*at("gw", l))
                for t0, n in ALL_SEGS:
                    b = bank(("mgate", l, t0))
                    for k in range(KD):
                        i = mm(b[:, 0:n], M["gw"][:, k, :], HTk[:, k, t0:t0 + n], start=(k == 0), stop=(k == KD - 1))
                    i.then_inc(*pe.step("full", ("mgate", l, t0)))
                for h in range(2):
                    project("mq", l, h, out_segs(l))
                for h in range(2):
                    project("mk", l, h, ALL_SEGS)
                for h in range(2):
                    project_tok("mv", l, h, 0, W)
                    used(("mv", l, h))
                for c in range(NB):
                    b = bank(("mcols", l, c))
                    eng.wait_ge(*at("mrows", l))
                    nc.tensor.transpose(b[:, 0:P], M["a"][:, c * P:(c + 1) * P], ident).then_inc(*pe.step("full", ("mcols", l, c)))
                for n_ in range(NB):
                    turn = [(d, scan_order(d)[n_]) for d in range(2)]
                    for d, c in turn:
                        if c in out_blocks(l):
                            b = bank(("mkq", l, d, c))
                            eng.wait_ge(*at("mqk_ready", l))
                            for h in range(NH):
                                i = mm(b[:, h * P:(h + 1) * P], M["K"][:, h, c * P:(c + 1) * P],
                                       M["Q"][:, h, c * P:(c + 1) * P], start=True, stop=True)
                            i.then_inc(*pe.step("full", ("mkq", l, d, c)))
                        if n_ < NB - 1:
                            b = bank(("mkT", l, d, c))
                            eng.wait_ge(*at("mqk_ready", l))
                            for h in range(NH):
                                i = nc.tensor.transpose(b[:, h * P:(h + 1) * P], M["K"][:, h, c * P:(c + 1) * P], ident)
                            i.then_inc(*pe.step("full", ("mkT", l, d, c)))
                    for d, c in turn:
                        if n_ < NB - 1:
                            b = bank(("mC", l, d, c))
                            eng.wait_ge(*at("mkw", l, d, c))
                            for h in range(NH):
                                i = mm(b[:, h * P:(h + 1) * P], M["kw"][d][:, h, :], M["V"][:, c, h * P:(h + 1) * P],
                                       start=True, stop=True)
                            i.then_inc(*pe.step("full", ("mC", l, d, c)))
                            b = bank(("mn", l, d, c))
                            for h in range(NH):
                                i = mm(b[:, h:h + 1], M["kw"][d][:, h, :], const("ones")[:, 0:1], start=True, stop=True)
                            i.then_inc(*pe.step("full", ("mn", l, d, c)))
                    for d, c in turn:
                        if c in out_blocks(l):
                            b = bank(("mnum", l, d, c))
                            eng.wait_ge(*at("ms", l, d, c))
                            for h in range(NH):
                                i = mm(b[:, h * P:(h + 1) * P], M["V"][:, c, h * P:(h + 1) * P], M["s"][d][:, h, :],
                                       start=True, stop=not n_)
                                if n_:
                                    i = mm(b[:, h * P:(h + 1) * P], M["C"][d][:, n_ % 2, h, :], M["qw"][d][:, h, :],
                                           start=False, stop=True)
                            i.then_inc(*pe.step("full", ("mnum", l, d, c)))
                            b = bank(("mden", l, d, c))
                            for h in range(NH):
                                i = mm(b[:, h * P:(h + 1) * P], const("ones"), M["s"][d][:, h, :], start=True, stop=not n_)
                                if n_:
                                    i = mm(b[:, h * P:(h + 1) * P], M["nb"][d][:, h, :], M["qw"][d][:, h, :],
                                           start=False, stop=True)
                            i.then_inc(*pe.step("full", ("mden", l, d, c)))
                norm_sums("mls", l, [[h] for h in range(NH)], lambda m, t0, n: YSb[:, 2 * BB + m, t0:t0 + n],
                          lambda m, t0, n: M["sq"][:, m, t0:t0 + n], "mean128")
                for h in range(2):
                    project("mo", l, h, out_segs(l))

                pe.stage(("attn", l))
                A = attn_work()
                w = weight(("akv", l, 0))
                for t0, n in ALL_SEGS:
                    b = bank(("ak", l, 0, t0))
                    for k in range(KD):
                        i = mm(b[:, 0:n], w[:, k, 0:P], HTk[:, k, t0:t0 + n], start=(k == 0), stop=(k == KD - 1))
                    i.then_inc(*pe.step("full", ("ak", l, 0, t0)))
                rotate("ak", l, (0,), "permA", lambda m: A["raw"][:, 0, :])
                project_tok("akv", l, 0, P, P)
                used(("akv", l, 0))
                for h in range(2):
                    project("aq", l, h, out_segs(l))
                    rotate("aq", l, (2 * h, 2 * h + 1), "permA", lambda m: A["raw"][:, m % 2, :])
                seq = [(t, h) for t in out_blocks(l) for h in range(AH)]

                def probs_back(t, h):
                    local = local_blocks(t)
                    eng.wait_ge(*at("ap", l, t, h))
                    for part, js in (("apl", list(range(len(local)))), ("apc", [len(local), len(local) + 1])):
                        if js:
                            b = bank((part, l, t, h))
                            for x, j in enumerate(js):
                                i = nc.tensor.transpose(b[:, x * P:(x + 1) * P], A["P"][:, h % 2, j * P:(j + 1) * P], ident)
                            i.then_inc(*pe.step("full", (part, l, t, h)))

                def values(t, h):
                    kb = local_blocks(t) + [0, 1]
                    b = bank(("ay", l, t, h))
                    eng.wait_ge(*at("apt", l, t, h))
                    if len(kb) > 2:
                        eng.wait_ge(*at("apl_moved", l, t, h))
                    g = h // 4
                    for x, j in enumerate(kb):
                        i = mm(b[:, 0:AD], A["PT"][:, h % 2, x * P:(x + 1) * P], A["V"][:, j, g * AD:(g + 1) * AD],
                               start=(x == 0), stop=(x == len(kb) - 1))
                    i.then_inc(*pe.step("full", ("ay", l, t, h)))
                    if h == AH - 1:
                        b = bank(("ayT", l, t))
                        eng.wait_ge(*at("ayn", l, t))
                        for m in range(BB):
                            i = nc.tensor.transpose(b[:, m * P:(m + 1) * P], A["Y"][:, t % 2, m * P:(m + 1) * P], ident)
                        i.then_inc(*pe.step("full", ("ayT", l, t)))

                for x_ in range(len(seq) + 2):
                    if x_ < len(seq):
                        t, h = seq[x_]
                        local = local_blocks(t)
                        g, fb = h // 4, h % 4
                        lo = g * AD
                        q = A["Q"][lo:lo + AD, fb, t * P:(t + 1) * P]
                        eng.wait_ge(*at("aq_ready", l))
                        if local:
                            b = bank(("aloc", l, t, h))
                            i = mm(b[:, 0:P * len(local)], q, A["K"][lo:lo + AD, local[0] * P:(local[-1] + 1) * P],
                                   start=True, stop=True)
                            i.then_inc(*pe.step("full", ("aloc", l, t, h)))
                        b = bank(("actx", l, t, h))
                        i = mm(b[:, 0:CTX], q, A["K"][lo:lo + AD, 0:CTX], start=True, stop=True)
                        i.then_inc(*pe.step("full", ("actx", l, t, h)))

                    if 1 <= x_ <= len(seq):
                        probs_back(*seq[x_ - 1])
                    if x_ >= 2:
                        values(*seq[x_ - 2])

                pe.stage(("merge", l))
                for j in range(D // W):
                    for i_ in range(4):
                        wg = weight(("gate", l, j, i_))
                        wb = weight(("branch", l, j, i_), BB)
                        for m in range(2):
                            for t0, n in out_segs(l):
                                b = bank(("gate", l, j, i_, m, t0))
                                for k in range(KD):
                                    i = mm(b[:, 0:n], wg[:, k, m * P:(m + 1) * P], HTk[:, k, t0:t0 + n],
                                           start=(k == 0), stop=(k == KD - 1))
                                i.then_inc(*pe.step("full", ("gate", l, j, i_, m, t0)))
                                b = bank(("branch", l, j, i_, m, t0))
                                for k in range(BB):
                                    i = mm(b[:, 0:n], wb[:, k, m * P:(m + 1) * P], YSb[:, i_ * BB + k, t0:t0 + n],
                                           start=(k == 0), stop=(k == BB - 1))
                                i.then_inc(*pe.step("full", ("branch", l, j, i_, m, t0)))
                        used(("gate", l, j, i_))
                        used(("branch", l, j, i_))

                pe.stage(("out", l))
                ACC = merge_work()[0]
                H2 = out_work()[0]

                def transposed(t):
                    for half in range(2):
                        b = bank(("hT", l, t, half))
                        eng.wait_ge(*at("h2", l, t))
                        for k in range(4):
                            i = nc.tensor.transpose(b[:, k * P:(k + 1) * P],
                                                    H2[:, t, (half * 4 + k) * P:(half * 4 + k + 1) * P], ident)
                        i.then_inc(*pe.step("full", ("hT", l, t, half)))

                for t in out_blocks(l):
                    for j in range(D // W):
                        w = weight(("out", l, j))
                        b = bank(("out", l, j, t))
                        for k in range(KD):
                            i = mm(b[:, 0:W], ACC[:, k, t * P:(t + 1) * P], w[:, k, :], start=(k == 0), stop=(k == KD - 1))
                        i.then_inc(*pe.step("full", ("out", l, j, t)))
                        if t == out_blocks(l)[-1]:
                            used(("out", l, j))
                    if t > out_blocks(l)[0]:
                        transposed(t - 1)
                transposed(NB - 1)

                def scores(t):
                    for g in range(4):
                        b = bank(("score", l, t, g))
                        for x in range(4):
                            hc = 4 * g + x
                            if t == out_blocks(l)[0]:
                                eng.wait_ge(*at("read", ("wq0", l, hc, q_segs(l, 0)[0][0])))
                            i = mm(b[:, x * KEYS:(x + 1) * KEYS], YSb[:, hc, t * P:(t + 1) * P],
                                   KEYT[:, (hc % 2) * KEYS:(hc % 2 + 1) * KEYS], start=True, stop=True)
                        i.then_inc(*pe.step("full", ("score", l, t, g)))

                pe.stage(("peerq", l))
                for part in range(2):
                    for h in range(HEADS * 256 // W):
                        project(f"wq{part}", l, h, q_segs(l, part))
                    if part == 0:
                        scores(out_blocks(l)[0])

                pe.stage(("route", l))
                for t in out_blocks(l)[1:]:
                    scores(t)

                pe.stage(("peer", l))
                G = peer_work()
                for b0, nb, base in peer_calls(l):
                    with eng.Fori(0, nb) as i:
                        for n in range(SLOTS):
                            if n == 0:
                                eng.wait_ge(fl.sem("residual_added"), i + base + 1)
                            eng.wait_ge(fl.sem(f"v_landed{n % VRING}"), (i + base) * (16 * SLOTS // VRING) + 16 * (n // VRING + 1))
                            eng.wait_ge(fl.sem("diagonal_ready"), (i + base) * SLOTS + n + 1)
                            mm(banks[6][:, :], G["diag"][:, n % DRING, :], G["v"][n % VRING][:, 0:512],
                               start=(n == 0), stop=(n == SLOTS - 1))
                            mm(banks[7][:, :], G["diag"][:, n % DRING, :], G["v"][n % VRING][:, 512:1024],
                               start=(n == 0), stop=(n == SLOTS - 1)).then_inc(fl.sem("v_summed"), 1)
            pe.stage("final")
            pe.finish()

        @block.vector
        def _(eng):
            dv = Engine(eng, "vector")
            v = nc.vector

            def normalise(tag, l, groups, y, sq, rs):
                for t0, n in out_segs(l):
                    for g, blocks in enumerate(groups):
                        eng.wait_ge(*at("full", (tag, "mean", l, g, t0)))
                        b = bank_of((tag, "mean", l, g, t0))
                        for m in blocks:
                            v.tensor_tensor(y(m, t0, n), y(m, t0, n), b[:, 0:n], ALU.subtract).then_inc(*dv.step())
                            eng.wait_ge(*dv.latest())
                        fl.mark(("read", (tag, "mean", l, g, t0)), dv.sem)
                        fl.mark((tag + "_centred", l, g, t0), dv.sem)
                for t0, n in out_segs(l):
                    for g, blocks in enumerate(groups):
                        eng.wait_ge(*at(tag + "_root", l, g, t0))
                        v.reciprocal(rs(g, t0, n), rs(g, t0, n)).then_inc(*dv.step())
                        eng.wait_ge(*dv.latest())
                        for m in blocks:
                            v.tensor_tensor(y(m, t0, n), y(m, t0, n), rs(g, t0, n), ALU.mult).then_inc(*dv.step())
                            eng.wait_ge(*dv.latest())
                        fl.mark((tag + "_normed", l, g, t0), dv.sem)

            def rope(tag, l, nb, cos, sin, raw, dst, between=lambda m: None):
                for m in range(nb):
                    eng.wait_ge(*at("full", (tag + "_rot", l, m)))
                    b = bank_of((tag + "_rot", l, m))
                    v.tensor_tensor(dst(m), raw(m), const(cos), ALU.mult).then_inc(*dv.step())
                    eng.wait_ge(*dv.latest())
                    v.tensor_tensor(raw(m), b[:, :], const(sin), ALU.mult).then_inc(*dv.step("read", (tag + "_rot", l, m)))
                    eng.wait_ge(*dv.latest())
                    v.tensor_tensor(dst(m), dst(m), raw(m), ALU.add).then_inc(*dv.step(tag + "_roped", l, m))
                    eng.wait_ge(*dv.latest())
                    between(m)
                fl.mark((tag + "_ready", l), dv.sem)

            dv.stage("mod")
            MR, MB = work(6 * D, 6 * D)
            eng.wait_ge(*at("params"))
            for l in range(DEPTH):
                eng.wait_ge(*at("mod_b", l))
                if l:
                    eng.wait_ge(*at("mod_stored", l - 1))
                for c in range(6 * D // W):
                    eng.wait_ge(*at("full", ("mod", l, c)))
                    b = bank_of(("mod", l, c))
                    v.tensor_tensor(MR[0:2, c * W:(c + 1) * W], b[0:2, 0:W], MB[0:2, c * W:(c + 1) * W], ALU.add).then_inc(*dv.step("read", ("mod", l, c)))
                fl.mark(("mod_rows", l), dv.sem)

            for l in range(DEPTH):
                dv.stage(("norm", l))
                xn = work(D, D)
                eng.wait_ge(*at("layer", l))
                for s in range(2):
                    v.scalar_tensor_tensor(SC1[:, s * KD:(s + 1) * KD], SC1[:, s * KD:(s + 1) * KD], 1.0,
                                                 par("n1g"), ALU.add, ALU.mult).then_inc(*dv.step())
                    eng.wait_ge(*dv.latest())
                fl.mark(("sc1", l), dv.sem)
                v.scalar_tensor_tensor(T8[0], LG, -1.0, LG, ALU.mult, ALU.max).then_inc(*dv.step("rabs", l))
                eng.wait_ge(*dv.latest())
                v.tensor_scalar(LG, LG, 0.0, None, ALU.min).then_inc(*dv.step())
                eng.wait_ge(*dv.latest())
                eng.wait_ge(*at("rln", l))
                v.tensor_tensor(LG, LG, T8[2], ALU.subtract).then_inc(*dv.step("lg", l))
                eng.wait_ge(*dv.latest())
                for t in range(NB):
                    eng.wait_ge(*at("ssq", l, t))
                    v.tensor_scalar(RSQ[:, t:t + 1], SSQ[:, t:t + 1], 1.0 / D, EPS, ALU.mult, ALU.add).then_inc(*dv.step())
                    eng.wait_ge(*dv.latest())
                    v.reciprocal(RSQ[:, t:t + 1], RSQ[:, t:t + 1]).then_inc(*dv.step("rsq", l, t))
                    eng.wait_ge(*dv.latest())
                    eng.wait_ge(*at("rs", l, t))
                    if t >= 2:
                        eng.wait_ge(*at("full", ("xT", l, t - 2, 1)))
                    v.tensor_scalar(xn[t % 2], Xb[:, t, :], RSB[:, t:t + 1], None, ALU.mult).then_inc(*dv.step("xn", l, t))
                    eng.wait_ge(*dv.latest())
                    eng.wait_ge(*at("full", ("xT", l, t, 1)))
                    b = bank_of(("xT", l, t, 1))
                    s = 0 if t >= CB else 1
                    for k in range(4):
                        kk = 4 + k
                        i = v.tensor_scalar(HTk[:, kk, t * P:(t + 1) * P], b[:, k * P:(k + 1) * P],
                                            SC1[:, s * KD + kk:s * KD + kk + 1], SH1[:, s * KD + kk:s * KD + kk + 1],
                                            ALU.mult, ALU.add)
                        i.then_inc(*dv.step())
                    fl.mark(("read", ("xT", l, t, 1)), dv.sem)

                dv.stage(("ret", l))
                R = ret_work()
                CP, Y, SG, SQ, RS = conv_work()
                if l:
                    eng.wait_ge(*at("x_parked", l))
                v.memset(CP, 0.0).then_inc(*dv.step())
                eng.wait_ge(*dv.latest())

                def glu(h):
                    for m in range(2):
                        for t0, n in out_segs(l):
                            o = pad_at(t0)
                            eng.wait_ge(*at("conv_sg", l, h, m, t0))
                            eng.wait_ge(*at("full", ("conv_a", l, 2 * h + m, t0)))
                            b = bank_of(("conv_a", l, 2 * h + m, t0))
                            v.tensor_tensor(CP[:, 2 * h + m, o:o + n], b[:, 0:n], SG[:, m, t0:t0 + n], ALU.mult).then_inc(*dv.step("read", ("conv_a", l, 2 * h + m, t0)))
                            eng.wait_ge(*dv.latest())
                    fl.mark(("conv_glu", l, h), dv.sem)

                def taps(h, t0, n):
                    cw, cb = par("conv_w"), par("conv_b")
                    o = pad_at(t0) - TAPS // 2
                    for j in range(TAPS):
                        for m in (2 * h, 2 * h + 1):
                            dst = Y[:, m, t0:t0 + n]
                            src = CP[:, m, o + j:o + j + n]
                            tap = cw[:, m * TAPS + j:m * TAPS + j + 1]
                            if j == 0:
                                v.tensor_scalar(dst, src, tap, cb[:, m:m + 1], ALU.mult, ALU.add).then_inc(*dv.step())
                            else:
                                eng.wait_ge(*dv.latest(1))
                                v.scalar_tensor_tensor(dst, src, tap, dst, ALU.mult, ALU.add).then_inc(*dv.step())
                    eng.wait_ge(*dv.latest())

                pieces = [(h, t0, n) for h in range(2) for t0, n in out_segs(l)]
                glu(0)
                glu(1)
                for h in range(NH):
                    eng.wait_ge(*at("rdec", l, h))
                    v.tensor_tensor(R["dec"][:, h, :], R["dec"][:, h, :], const("until"), ALU.mult).then_inc(*dv.step())
                    eng.wait_ge(*dv.latest())
                    v.tensor_tensor(R["dtmp"][:, h, :], R["dtmp"][:, h, :], const("since"), ALU.mult).then_inc(*dv.step())
                    eng.wait_ge(*dv.latest())
                    v.tensor_tensor(R["dec"][:, h, :], R["dec"][:, h, :], R["dtmp"][:, h, :], ALU.add).then_inc(*dv.step())
                    eng.wait_ge(*dv.latest())
                taps(*pieces[0])
                rope("rk", l, BB, "cosR", "sinR", lambda m: R["raw"][:, m % 2, :], lambda m: R["K"][:, m, CTX:],
                     lambda m: taps(*pieces[1]) if m == 1 else None)
                for h in range(2):
                    for t in range(NB):
                        eng.wait_ge(*at("full", ("rv_tok", l, h, t)))
                        b = bank_of(("rv_tok", l, h, t))
                        v.tensor_copy(R["V"][:, t, h * W:(h + 1) * W], b[:, 0:W]).then_inc(*dv.step("read", ("rv_tok", l, h, t)))
                for piece in pieces[2:]:
                    taps(*piece)
                for t0, n in out_segs(l):
                    fl.mark(("conv_mean", l, 0, t0), dv.sem)
                rope("rq", l, BB, "cosR", "sinR", lambda m: R["raw"][:, m % 2, :], lambda m: R["Q"][:, m, CTX:])
                normalise("conv", l, [range(BB)], lambda m, t0, n: Y[:, m, t0:t0 + n],
                          SQ, lambda g, t0, n: RS[:, t0:t0 + n])
                for c in range(NB):
                    eng.wait_ge(*at("full", ("rkT", l, c)))
                    b = bank_of(("rkT", l, c))
                    v.tensor_copy(R["kt"][:, c, :], b[:, :]).then_inc(*dv.step("read", ("rkT", l, c)))
                    eng.wait_ge(*dv.latest())

                def ret_out(c):
                    eng.wait_ge(*at("full", ("ro", l, c)))
                    b = bank_of(("ro", l, c))
                    v.tensor_copy(YSb[:, BB:2 * BB, c * P:(c + 1) * P], blocks4(b[:, :])).then_inc(*dv.step("read", ("ro", l, c)))
                    eng.wait_ge(*dv.latest())

                prev = None
                for d in range(2):
                    chunks = scan_order(d)
                    for n_, c in enumerate(chunks[:-1]):
                        if prev:
                            eng.wait_ge(*at("full", prev))
                        v.tensor_tensor(R["kd"], R["kt"][:, c, :].rearrange("p (h j) -> p h j", h=NH),
                                              KDEC[:, d * 4:d * 4 + 4].unsqueeze(2).to_broadcast([P, NH, P]), ALU.mult).then_inc(*dv.step("rkd", l, d, c))
                        eng.wait_ge(*dv.latest())
                        prev = ("rS", l, d, c)
                        eng.wait_ge(*at("full", prev))
                        b = bank_of(prev)
                        new = R["S"][:, d * NB + chunks[n_ + 1], :, :]
                        if n_ == 0:
                            v.tensor_copy(new.rearrange("p h e -> p (h e)"), b[:, :]).then_inc(*dv.step("read", prev))
                            eng.wait_ge(*dv.latest())
                        else:
                            old = R["S"][:, d * NB + c, :, :]
                            v.tensor_tensor(new, old, CDEC[:, d * 4:d * 4 + 4].unsqueeze(2).to_broadcast([P, NH, P]),
                                                  ALU.mult).then_inc(*dv.step())
                            eng.wait_ge(*dv.latest())
                            v.tensor_tensor(new.rearrange("p h e -> p (h e)"), new.rearrange("p h e -> p (h e)"),
                                                 b[:, :], ALU.add).then_inc(*dv.step("read", prev))
                            eng.wait_ge(*dv.latest())
                for x, c in enumerate(out_blocks(l)):
                    if x:
                        eng.wait_ge(*at("full", ("ro", l, out_blocks(l)[x - 1])))
                    eng.wait_ge(*at("full", ("rkq", l, c)))
                    b = bank_of(("rkq", l, c))
                    v.tensor_tensor(R["att"].rearrange("p h i -> p (h i)"), b[:, :],
                                         R["dec"].rearrange("p h i -> p (h i)"), ALU.mult).then_inc(*dv.step("read", ("rkq", l, c)))
                    eng.wait_ge(*dv.latest())
                    for d in range(2):
                        v.tensor_tensor(R["qd"][:, d, :, :], R["Q"][:, :, c * P:(c + 1) * P], R["qdec"][:, d, :, :],
                                              ALU.mult).then_inc(*dv.step())
                        eng.wait_ge(*dv.latest())
                    fl.mark(("ratt", l, c), dv.sem)
                    if x:
                        ret_out(out_blocks(l)[x - 1])
                ret_out(out_blocks(l)[-1])
                for t0, n in out_segs(l):
                    for g in range(NH):
                        fl.mark(("ret_mean", l, g, t0), dv.sem)
                normalise("ret", l, [[h] for h in range(NH)], lambda m, t0, n: YSb[:, BB + m, t0:t0 + n],
                          None, lambda g, t0, n: R["rs"][:, g, t0:t0 + n])
                for m in range(BB):
                    for t0, n in out_segs(l):
                        eng.wait_ge(*at("rgate", l, m, t0))
                        y = YSb[:, BB + m, t0:t0 + n]
                        v.tensor_tensor(y, y, R["g"][:, m, t0:t0 + n], ALU.mult).then_inc(*dv.step())

                dv.stage(("mlstm", l))
                M = mlstm_work()
                v.memset(M["gw"], 0.0).then_inc(*dv.step())
                eng.wait_ge(*dv.latest())
                eng.wait_ge(*at("loaded", ("mgate", l, 0)))
                src = WRr[:, SLOT[("mgate", l, 0)] % RING, 0:KD * 16].rearrange("p (k n) -> p k n", k=KD)
                for qd, kind in enumerate((0, 2, 1, 3)):
                    v.tensor_copy(M["gw"][:, :, 32 * qd:32 * qd + 4], src[:, :, 4 * kind:4 * kind + 4]).then_inc(*dv.step())
                fl.mark(("gw", l), dv.sem)
                fl.mark(("used", ("mgate", l, 0)), dv.sem)
                eng.wait_ge(*at("gate_bias", l))
                I, F_, B, A_, MM, MT, WP, EM, T = (M[x] for x in ("i", "f", "b", "a", "m", "mt", "wp", "em", "t"))
                for t0, n in ALL_SEGS:
                    eng.wait_ge(*at("full", ("mgate", l, t0)))
                    b = bank_of(("mgate", l, t0))
                    v.tensor_scalar(I[0:64, t0:t0 + n], b[0:64, 0:n], GB[0:64, 0:1], None, ALU.add).then_inc(*dv.step())
                    eng.wait_ge(*dv.latest())
                    v.tensor_scalar(F_[0:64, t0:t0 + n], b[64:128, 0:n], GB[64:128, 1:2], None, ALU.add).then_inc(*dv.step("read", ("mgate", l, t0)))
                    eng.wait_ge(*dv.latest())
                v.scalar_tensor_tensor(T[0:64, :], F_[0:64, :], -1.0, F_[0:64, :], ALU.mult, ALU.max).then_inc(*dv.step("mabs", l))
                eng.wait_ge(*dv.latest())
                v.tensor_scalar(F_[0:64, :], F_[0:64, :], 0.0, None, ALU.min).then_inc(*dv.step())
                eng.wait_ge(*dv.latest())
                eng.wait_ge(*at("mln", l))
                v.tensor_tensor(F_[0:64, :], F_[0:64, :], T[0:64, :], ALU.subtract).then_inc(*dv.step())
                eng.wait_ge(*dv.latest())
                for d in range(2):
                    q = slice(32 * d, 32 * d + 32)
                    for c in range(NB):
                        s = chunk_slice(d, c)
                        v.tensor_tensor_scan(B[q, s], const("ones")[q, :], F_[q, s], 0.0, ALU.mult, ALU.add).then_inc(*dv.step())
                        eng.wait_ge(*dv.latest())
                v.tensor_tensor(A_[0:64, :], I[0:64, :], B[0:64, :], ALU.subtract).then_inc(*dv.step())
                eng.wait_ge(*dv.latest())
                m0 = M["m0"]
                v.memset(m0, NEG).then_inc(*dv.step())
                eng.wait_ge(*dv.latest())
                for d in range(2):
                    q = slice(32 * d, 32 * d + 32)
                    for n_, c in enumerate(scan_order(d)):
                        s = chunk_slice(d, c)
                        e = (c + 1) * P - 1 if d == 0 else c * P
                        mi = m0[q, n_:n_ + 1]
                        v.tensor_tensor_scan(MM[q, s], A_[q, s], A_[q, s], mi, ALU.max, ALU.max).then_inc(*dv.step())
                        eng.wait_ge(*dv.latest())
                        if n_ < NB - 1:
                            v.tensor_tensor(m0[q, n_ + 1:n_ + 2], MM[q, e:e + 1], B[q, e:e + 1], ALU.add).then_inc(*dv.step())
                            eng.wait_ge(*dv.latest())
                        v.tensor_scalar(WP[q, s], MM[q, s], mi, -1.0, ALU.subtract, ALU.mult).then_inc(*dv.step())
                        eng.wait_ge(*dv.latest())
                        v.tensor_scalar(T[q, s], A_[q, s], MM[q, e:e + 1], None, ALU.subtract).then_inc(*dv.step())
                        eng.wait_ge(*dv.latest())
                v.tensor_tensor(MT[0:64, :], B[0:64, :], MM[0:64, :], ALU.add).then_inc(*dv.step("mrowlogs", l))
                eng.wait_ge(*dv.latest())
                order_qk = [("mq", m) for m in range(BB)] + [("mk", m) for m in range(BB)]
                v.memset(M["pad"], 0.0).then_inc(*dv.step("mpad0", l))
                eng.wait_ge(*dv.latest())
                for x, (tag, m) in enumerate(order_qk):
                    cw, cb = par("mconv_w"), par("mconv_b")
                    ch = m + (BB if tag == "mk" else 0)
                    for t0, n in (out_segs(l) if tag == "mq" else ALL_SEGS):
                        o = mpad_at(t0) - 1
                        pad = M["pad"][:, x % 2, :]
                        dst = M["Q" if tag == "mq" else "K"][:, m, t0:t0 + n]
                        eng.wait_ge(*at("mpad", l, tag, m, t0))
                        v.tensor_scalar(dst, pad[:, o:o + n], cw[:, 3 * ch:3 * ch + 1], cb[:, ch:ch + 1],
                                              ALU.mult, ALU.add).then_inc(*dv.step())
                        eng.wait_ge(*dv.latest())
                        for j in (1, 2):
                            v.scalar_tensor_tensor(dst, pad[:, o + j:o + j + n], cw[:, 3 * ch + j:3 * ch + j + 1],
                                                         dst, ALU.mult, ALU.add).then_inc(*dv.step())
                            eng.wait_ge(*dv.latest())
                        fl.mark(("mconv", l, tag, m, t0), dv.sem)
                eng.wait_ge(*at("msilu", l))
                v.tensor_scalar(M["Kf"], M["Kf"], float(P) ** -0.5, None, ALU.mult).then_inc(*dv.step("mqk_ready", l))
                eng.wait_ge(*dv.latest())
                for h in range(2):
                    for t in range(NB):
                        eng.wait_ge(*at("full", ("mv_tok", l, h, t)))
                        b = bank_of(("mv_tok", l, h, t))
                        v.tensor_copy(M["V"][:, t, h * W:(h + 1) * W], b[:, 0:W]).then_inc(*dv.step("read", ("mv_tok", l, h, t)))
                for c in range(NB):
                    eng.wait_ge(*at("full", ("mcols", l, c)))
                    b = bank_of(("mcols", l, c))
                    v.tensor_copy(M["cols"][:, c, :], b[:, 0:P]).then_inc(*dv.step("read", ("mcols", l, c)))
                    eng.wait_ge(*dv.latest())
                h4 = lambda a: a.rearrange("p (h i) -> p h i", h=NH)
                flat = lambda a: a.rearrange("p h e -> p (h e)")
                seen = set()
                for n_ in range(NB):
                    turn = [(d, scan_order(d)[n_]) for d in range(2)]
                    for d, c in turn:
                        bc = M["bc"][:, d, :]
                        eng.wait_ge(*at("mbc", l, d, c))
                        if c in out_blocks(l):
                            acol = M["cols"][:, c, 32 * d:32 * d + 4].unsqueeze(2).to_broadcast([P, NH, P])
                            v.tensor_tensor(M["e"][d], h4(bc[:, 0:512]), acol, ALU.subtract).then_inc(*dv.step("mlogw", l, d, c))
                            if n_:
                                v.tensor_tensor(M["qw"][d], M["Q"][:, :, c * P:(c + 1) * P], h4(bc[:, 512:1024]),
                                                ALU.mult).then_inc(*dv.step())
                                v.tensor_copy(M["nb"][d], M["N"][d][:, n_ % 2, :].unsqueeze(2).to_broadcast([P, NH, P]))\
                                    .then_inc(*dv.step())
                        if n_ < NB - 1:
                            wcol = M["cols"][:, c, 64 + 32 * d:64 + 32 * d + 4].unsqueeze(2).to_broadcast([P, NH, P])
                            eng.wait_ge(*at("full", ("mkT", l, d, c)))
                            b = bank_of(("mkT", l, d, c))
                            v.tensor_tensor(M["kw"][d], h4(b[:, :]), wcol, ALU.mult).then_inc(*dv.step("read", ("mkT", l, d, c)))
                            fl.mark(("mkw", l, d, c), dv.sem)
                    for d, c in turn:
                        if c in out_blocks(l):
                            eng.wait_ge(*at("mexp", l, d, c))
                            mask = const("until" if d == 0 else "since").unsqueeze(1).to_broadcast([P, NH, P])
                            v.scalar_tensor_tensor(M["e"][d], M["e"][d], 1.0, mask, ALU.min, ALU.mult).then_inc(*dv.step())
                            eng.wait_ge(*dv.latest())
                            eng.wait_ge(*at("full", ("mkq", l, d, c)))
                            b = bank_of(("mkq", l, d, c))
                            v.tensor_tensor(flat(M["s"][d]), flat(M["e"][d]), b[:, :], ALU.mult)\
                                .then_inc(*dv.step("read", ("mkq", l, d, c)))
                            fl.mark(("ms", l, d, c), dv.sem)
                    for d, c in turn:
                        if n_ < NB - 1:
                            bc = M["bc"][:, d, :]
                            new, nn = M["C"][d][:, (n_ + 1) % 2, :, :], M["N"][d][:, (n_ + 1) % 2, :]
                            if n_ == 0:
                                eng.wait_ge(*at("full", ("mC", l, d, c)))
                                b = bank_of(("mC", l, d, c))
                                v.tensor_copy(flat(new), b[:, :]).then_inc(*dv.step("read", ("mC", l, d, c)))
                                eng.wait_ge(*at("full", ("mn", l, d, c)))
                                b = bank_of(("mn", l, d, c))
                                v.tensor_copy(nn, b[:, 0:4]).then_inc(*dv.step("read", ("mn", l, d, c)))
                            else:
                                e = P - 1 if d == 0 else 0
                                dec = h4(bc[:, 512:1024])[:, :, e:e + 1]
                                old, on = M["C"][d][:, n_ % 2, :, :], M["N"][d][:, n_ % 2, :]
                                v.tensor_tensor(new, old, dec.to_broadcast([P, NH, P]), ALU.mult).then_inc(*dv.step())
                                v.tensor_tensor(nn.unsqueeze(2), on.unsqueeze(2), dec, ALU.mult).then_inc(*dv.step())
                                eng.wait_ge(*dv.latest())
                                eng.wait_ge(*at("full", ("mC", l, d, c)))
                                b = bank_of(("mC", l, d, c))
                                v.tensor_tensor(flat(new), flat(new), b[:, :], ALU.add).then_inc(*dv.step("read", ("mC", l, d, c)))
                                eng.wait_ge(*at("full", ("mn", l, d, c)))
                                b = bank_of(("mn", l, d, c))
                                v.tensor_tensor(nn, nn, b[:, 0:4], ALU.add).then_inc(*dv.step("read", ("mn", l, d, c)))
                    for d, c in turn:
                        bc, den = M["bc"][:, d, :], M["den"][d]
                        if c in out_blocks(l):
                            eng.wait_ge(*at("full", ("mden", l, d, c)))
                            b = bank_of(("mden", l, d, c))
                            v.scalar_tensor_tensor(den, b[:, :], -1.0, bc[:, 1024:1536], ALU.mult, ALU.max).then_inc(*dv.step())
                            eng.wait_ge(*dv.latest())
                            v.tensor_tensor(den, b[:, :], den, ALU.max).then_inc(*dv.step("read", ("mden", l, d, c)))
                            eng.wait_ge(*dv.latest())
                            v.reciprocal(den, den).then_inc(*dv.step())
                            eng.wait_ge(*dv.latest())
                            eng.wait_ge(*at("full", ("mnum", l, d, c)))
                            b = bank_of(("mnum", l, d, c))
                            y = YSb[:, 2 * BB:3 * BB, c * P:(c + 1) * P]
                            if c not in seen:
                                v.tensor_tensor(y, h4(b[:, :]), h4(den), ALU.mult).then_inc(*dv.step("read", ("mnum", l, d, c)))
                            else:
                                v.tensor_tensor(den, b[:, :], den, ALU.mult).then_inc(*dv.step("read", ("mnum", l, d, c)))
                                eng.wait_ge(*dv.latest())
                                v.tensor_tensor(y, y, h4(den), ALU.add).then_inc(*dv.step())
                            seen.add(c)
                        eng.wait_ge(*dv.latest())
                        fl.mark(("mbc_used", l, d, c), dv.sem)
                for t0, n in out_segs(l):
                    for g in range(NH):
                        fl.mark(("mls_mean", l, g, t0), dv.sem)
                normalise("mls", l, [[h] for h in range(NH)], lambda m, t0, n: YSb[:, 2 * BB + m, t0:t0 + n],
                          None, lambda g, t0, n: M["rs"][:, g, t0:t0 + n])
                for m in range(BB):
                    for t0, n in out_segs(l):
                        eng.wait_ge(*at("mogate", l, m, t0))
                        y = YSb[:, 2 * BB + m, t0:t0 + n]
                        v.tensor_tensor(y, y, M["g"][:, m, t0:t0 + n], ALU.mult).then_inc(*dv.step())

                dv.stage(("attn", l))
                A = attn_work()
                rope("ak", l, 1, "cosA", "sinA", lambda m: A["raw"][:, 0, :], lambda m: A["K"][:, CTX:])
                for t in range(NB):
                    eng.wait_ge(*at("full", ("akv_tok", l, 0, t)))
                    b = bank_of(("akv_tok", l, 0, t))
                    v.tensor_copy(A["V"][:, t, :], b[:, 0:P]).then_inc(*dv.step("read", ("akv_tok", l, 0, t)))
                rope("aq", l, BB, "cosA", "sinA", lambda m: A["raw"][:, m % 2, :], lambda m: A["Q"][:, m, CTX:])
                MX, NM, SE, DN, RC, SUM = AW
                seq = [(t, h) for t in out_blocks(l) for h in range(AH)]

                def scaled(x, t, h):
                    local = local_blocks(t)
                    nl = len(local) * P
                    S = A["S"][:, h % 2, :]
                    if x >= 2:
                        eng.wait_ge(*at("aexp", l, *seq[x - 2]))
                    if local:
                        eng.wait_ge(*at("full", ("aloc", l, t, h)))
                        b = bank_of(("aloc", l, t, h))
                        for y, j in enumerate(local):
                            o = slice(y * P, (y + 1) * P)
                            if j == t:
                                i = v.tensor_scalar(S[:, o], b[:, o], AD ** -0.5, None, ALU.mult)
                            else:
                                mask = const("maskprev" if j < t else "masknext")
                                i = v.scalar_tensor_tensor(S[:, o], b[:, o], AD ** -0.5, mask, ALU.mult, ALU.add)
                            i.then_inc(*dv.step())
                        fl.mark(("read", ("aloc", l, t, h)), dv.sem)
                    eng.wait_ge(*at("full", ("actx", l, t, h)))
                    b = bank_of(("actx", l, t, h))
                    v.tensor_scalar(S[:, nl:nl + CTX], b[:, 0:CTX], AD ** -0.5, None, ALU.mult)\
                        .then_inc(*dv.step("read", ("actx", l, t, h)))
                    eng.wait_ge(*dv.latest())
                    v.tensor_reduce(MX[:, h:h + 1], S[:, 0:nl + CTX], AX, ALU.max).then_inc(*dv.step())
                    eng.wait_ge(*dv.latest())
                    v.tensor_scalar(NM[:, h:h + 1], MX[:, h:h + 1], SINK[:, h:h + 1], -1.0, ALU.max, ALU.mult)\
                        .then_inc(*dv.step("anm", l, t, h))

                def moved(t, h):
                    nl = len(local_blocks(t)) * P
                    eng.wait_ge(*at("full", ("apc", l, t, h)))
                    b = bank_of(("apc", l, t, h))
                    v.tensor_copy(A["PT"][:, h % 2, nl:nl + CTX], b[:, 0:CTX]).then_inc(*dv.step("read", ("apc", l, t, h)))
                    fl.mark(("apt", l, t, h), dv.sem)

                def divided(t, h):
                    eng.wait_ge(*at("aexp", l, t, h))
                    v.tensor_tensor(DN[:, h:h + 1], SUM[:, h:h + 1], SE[:, h:h + 1], ALU.add).then_inc(*dv.step())
                    eng.wait_ge(*dv.latest())
                    v.reciprocal(RC[:, h:h + 1], DN[:, h:h + 1]).then_inc(*dv.step())
                    eng.wait_ge(*dv.latest())
                    if h == 0 and t - 2 in out_blocks(l):
                        eng.wait_ge(*at("full", ("ayT", l, t - 2)))
                    eng.wait_ge(*at("full", ("ay", l, t, h)))
                    b = bank_of(("ay", l, t, h))
                    v.tensor_scalar(A["Y"][:, t % 2, h * AD:(h + 1) * AD], b[:, 0:AD], RC[:, h:h + 1], None, ALU.mult)\
                        .then_inc(*dv.step("read", ("ay", l, t, h)))
                    if h == AH - 1:
                        fl.mark(("ayn", l, t), dv.sem)

                for x in range(len(seq) + 2):
                    if x < len(seq):
                        scaled(x, *seq[x])
                    if 1 <= x <= len(seq):
                        moved(*seq[x - 1])
                    if x >= 2:
                        divided(*seq[x - 2])

                dv.stage(("merge", l))
                ACC, GS, PRD, _, _ = merge_work()
                for j in range(D // W):
                    for i_ in range(4):
                        for m in range(2):
                            for t0, n in out_segs(l):
                                eng.wait_ge(*at("gsig", l, j, i_, m, t0))
                                eng.wait_ge(*at("full", ("branch", l, j, i_, m, t0)))
                                b = bank_of(("branch", l, j, i_, m, t0))
                                acc = ACC[:, 2 * j + m, t0:t0 + n]
                                g = GS[:, gslot(l, j, i_, m, t0), 0:n]
                                if i_ == 0:
                                    v.tensor_tensor(acc, b[:, 0:n], g, ALU.mult).then_inc(*dv.step("read", ("branch", l, j, i_, m, t0)))
                                    eng.wait_ge(*dv.latest())
                                else:
                                    v.tensor_tensor(PRD[:, 0:n], b[:, 0:n], g, ALU.mult).then_inc(*dv.step("read", ("branch", l, j, i_, m, t0)))
                                    eng.wait_ge(*dv.latest())
                                    v.tensor_tensor(acc, acc, PRD[:, 0:n], ALU.add).then_inc(*dv.step())
                                    eng.wait_ge(*dv.latest())

                dv.stage(("out", l))
                GA, TMP = merge_work()[3:]
                H2, SC2, SH2, G2, _ = out_work()

                def moved_hT(t):
                    eng.wait_ge(*at("full", ("hT", l, t, 1)))
                    b = bank_of(("hT", l, t, 1))
                    v.tensor_copy(HTk[:, 4:8, t * P:(t + 1) * P], b[:, :].rearrange("p (k i) -> p k i", k=4)).then_inc(*dv.step("read", ("hT", l, t, 1)))

                eng.wait_ge(*at("ga1", l))
                for t in out_blocks(l):
                    s = 0 if t >= CB else 1
                    for j in range(D // W):
                        eng.wait_ge(*at("full", ("out", l, j, t)))
                        b = bank_of(("out", l, j, t))
                        tmp = TMP[:, (j % 2) * W:(j % 2 + 1) * W]
                        v.tensor_tensor(tmp, b[:, 0:W], GA[:, s * D + j * W:s * D + (j + 1) * W], ALU.mult).then_inc(*dv.step("read", ("out", l, j, t)))
                        eng.wait_ge(*dv.latest())
                        x = Xb[:, t, j * W:(j + 1) * W]
                        v.tensor_tensor(x, x, tmp, ALU.add).then_inc(*dv.step("added", l, j, t))
                    if t == out_blocks(l)[0]:
                        eng.wait_ge(*at("mod2", l))
                        for s_ in range(2):
                            sc = SC2[:, s_ * D:(s_ + 1) * D]
                            v.scalar_tensor_tensor(sc, sc, 1.0, G2, ALU.add, ALU.mult).then_inc(*dv.step())
                    eng.wait_ge(*at("ssq2", l, t))
                    v.tensor_scalar(RSQ[:, t:t + 1], SSQ[:, t:t + 1], 1.0 / D, EPS, ALU.mult, ALU.add).then_inc(*dv.step())
                    eng.wait_ge(*dv.latest())
                    v.reciprocal(RSQ[:, t:t + 1], RSQ[:, t:t + 1]).then_inc(*dv.step("rsq2", l, t))
                    eng.wait_ge(*dv.latest())
                    eng.wait_ge(*at("rs2", l, t))
                    v.scalar_tensor_tensor(H2[:, t, :], Xb[:, t, :], RSB[:, t:t + 1], SC2[:, s * D:(s + 1) * D],
                                                 ALU.mult, ALU.mult).then_inc(*dv.step())
                    eng.wait_ge(*dv.latest())
                    v.tensor_tensor(H2[:, t, :], H2[:, t, :], SH2[:, s * D:(s + 1) * D], ALU.add).then_inc(*dv.step("h2", l, t))
                    eng.wait_ge(*dv.latest())
                    if t > out_blocks(l)[0]:
                        moved_hT(t - 1)
                moved_hT(NB - 1)

                dv.stage(("peerq", l))
                for h in range(HEADS):
                    t0, n = q_segs(l, 0)[0]
                    eng.wait_ge(*at("full", ("wq0", l, 2 * h + 1, t0)))
                    b = bank_of(("wq0", l, 2 * h + 1, t0))
                    v.tensor_copy(YSb[:, 2 * h + 1, t0:t0 + n], b[:, 0:n]).then_inc(*dv.step("read", ("wq0", l, 2 * h + 1, t0)))

                G = peer_work()
                S, SV, SI, SIF, CAND, CV, CI, OH = (G[x] for x in ("s", "sv", "si3", "sif", "cand", "cv", "ci", "oh"))

                def top_keys(r, h):
                    for c in (2 * h, 2 * h + 1):
                        v.max(SV[:, c, 0:8], S[:, c, :]).then_inc(*r.step())
                    eng.wait_ge(*r.latest())
                    eng.sem_inc(fl.sem("searches_allowed"), 1)
                    for c in (2 * h, 2 * h + 1):
                        v.match_replace(G["s2"][c % 2], SV[:, c, 0:8], S[:, c, :], -3e38).then_inc(*r.step())
                    for c in (2 * h, 2 * h + 1):
                        v.max_index(SI[:, c, 0:8], SV[:, c, 0:8], S[:, c, :]).then_inc(*r.step())
                    eng.wait_ge(*r.latest(2))
                    eng.sem_inc(fl.sem("searches_allowed"), 1)
                    for c in (2 * h, 2 * h + 1):
                        v.max(SV[:, c, 8:16], G["s2"][c % 2]).then_inc(*r.step())
                    eng.wait_ge(*r.latest())
                    eng.sem_inc(fl.sem("searches_allowed"), 1)
                    for c in (2 * h, 2 * h + 1):
                        v.max_index(SI[:, c, 8:16], SV[:, c, 8:16], G["s2"][c % 2]).then_inc(*r.step())

                def candidates(r, h):
                    a = SV[:, 2 * h, :].unsqueeze(2).to_broadcast([P, TOPK, TOPK])
                    b_ = SV[:, 2 * h + 1, :].unsqueeze(1).to_broadcast([P, TOPK, TOPK])
                    eng.wait_ge(*r.latest())
                    v.tensor_tensor(CAND.rearrange("p (a b) -> p a b", a=TOPK), a, b_, ALU.add).then_inc(*r.step())
                    eng.wait_ge(*r.latest())
                    eng.sem_inc(fl.sem("searches_allowed"), 1)
                    v.max(CV[:, h, 0:8], CAND).then_inc(*r.step())
                    eng.wait_ge(*r.latest())
                    eng.sem_inc(fl.sem("searches_allowed"), 1)
                    v.match_replace(G["cand2"], CV[:, h, 0:8], CAND, -3e38).then_inc(*r.step())
                    v.max_index(CI[:, h, 0:8], CV[:, h, 0:8], CAND).then_inc(*r.step())
                    eng.wait_ge(*r.latest(1))
                    eng.sem_inc(fl.sem("searches_allowed"), 1)
                    v.max(CV[:, h, 8:16], G["cand2"]).then_inc(*r.step())
                    eng.wait_ge(*r.latest())
                    eng.sem_inc(fl.sem("searches_allowed"), 1)
                    v.max_index(CI[:, h, 8:16], CV[:, h, 8:16], G["cand2"]).then_inc(*r.step())
                    eng.wait_ge(*r.latest())
                    eng.sem_inc(fl.sem("searches_allowed"), 1)

                def centre(r):
                    v.tensor_tensor(G["ce"], CV, CV[:, :, 0:1].to_broadcast([P, HEADS, TOPK]), ALU.subtract)\
                        .then_inc(fl.sem("scores_centred"), 1)
                    v.tensor_copy(G["siff"], G["si"]).then_inc(*r.step())
                    eng.wait_ge(*r.latest())

                def pick_keys(r, x):
                    op, imm = ((ALU.logical_shift_right, 4), (ALU.bitwise_and, 15))[x]
                    v.tensor_scalar(G["cu"], G["cif"], imm, None, op).then_inc(*r.step())
                    eng.wait_ge(*r.latest())
                    v.tensor_copy(G["cf"], G["cu"]).then_inc(*r.step())
                    eng.wait_ge(*r.latest())
                    v.tensor_tensor(OH, G["cf"].unsqueeze(2).to_broadcast([P, SLOTS, TOPK]),
                                    const("iota16").unsqueeze(1).to_broadcast([P, SLOTS, TOPK]), ALU.is_equal)\
                        .then_inc(*r.step())
                    eng.wait_ge(*r.latest())
                    for h in range(HEADS):
                        pick = SIF[:, 2 * h + x, :].unsqueeze(1).to_broadcast([P, TOPK, TOPK])
                        o = OH[:, h * TOPK:(h + 1) * TOPK, :]
                        v.tensor_tensor(o, o, pick, ALU.mult).then_inc(*r.step())
                    eng.wait_ge(*r.latest())
                    v.tensor_reduce(G["i1" if x == 0 else "i2"], OH, AX, ALU.add).then_inc(*r.step())
                    eng.wait_ge(*r.latest())

                def experts(r):
                    v.scalar_tensor_tensor(G["i2"], G["i1"], float(KEYS), G["i2"], ALU.mult, ALU.add).then_inc(*r.step())
                    eng.wait_ge(*r.latest())
                    v.tensor_scalar(G["idx"], G["i2"], float(l * EXPERTS), None, ALU.add).then_inc(*r.step())
                    eng.wait_ge(*r.latest())

                def gates(r, nth):
                    eng.wait_ge(fl.sem("scores_exp"), nth + 1)
                    v.tensor_reduce(G["csum"], G["ce"], AX, ALU.add).then_inc(*r.step())
                    eng.wait_ge(*r.latest())
                    v.reciprocal(G["csum"], G["csum"]).then_inc(*r.step())
                    eng.wait_ge(*r.latest())
                    v.tensor_tensor(G["gate"].rearrange("p (h k) -> p h k", h=HEADS), G["ce"],
                                    G["csum"].unsqueeze(2).to_broadcast([P, HEADS, TOPK]), ALU.mult).then_inc(*r.step())
                    eng.wait_ge(*r.latest())

                first = routed(l, peer_calls(l)[0][2])
                r = Routing(first)
                for h in range(HEADS):
                    if h % 2 == 0:
                        eng.wait_ge(*at("scored", l, out_blocks(l)[0], h // 2))
                    top_keys(r, h)
                    candidates(r, h)
                centre(r)
                pick_keys(r, 0)
                pick_keys(r, 1)
                experts(r)
                gates(r, first)
                fl.marks["route_steps"] = ("route_steps", r.n)
                v.tensor_copy(G["idxu"], G["idx"]).then_inc(fl.sem("indices_staged"), 1)

                dv.stage(("route", l))
                dv.stage(("peer", l))
                eng.wait_ge(*at("ga2", l))
                for b0, nb, base in peer_calls(l):
                    s = 0 if b0 >= CB else 1
                    with eng.Fori(0, nb) as i:
                        it = i + base
                        v.tensor_copy(G["idxv"], G["idx"]).then_inc(fl.sem("v_indices_staged"), 1)
                        v.tensor_copy(G["gateb"], G["gate"]).then_inc(fl.sem("block_staged"), 1)
                        v.tensor_copy(G["hb"], G["H2"][:, bass.ds(i * D + b0 * D, D)]).then_inc(fl.sem("block_staged"), 1)
                        nth = routed(l, it + 1)
                        r = Routing(nth)
                        first_slot = b0 - out_blocks(l)[0]
                        v.tensor_copy(G["sf"], STORE[:, bass.ds(i * NSCORE + first_slot * NSCORE, NSCORE)])\
                            .then_inc(fl.sem("scores_staged"), 1)
                        eng.wait_ge(fl.sem("scores_staged"), it + 1)
                        eng.wait_ge(fl.sem("block_staged"), (it + 1) * 2)

                        def weigh(h):
                            hs = slice(h * TOPK, (h + 1) * TOPK)
                            eng.wait_ge(fl.sem("gelu_done"), it * HEADS + h + 1)
                            v.tensor_tensor(G["w"][:, hs], G["gateb"][:, hs], G["act"][:, hs], ALU.mult)\
                                .then_inc(fl.sem("weights_ready"), 1)

                        def route_part(h, k):
                            if h < HEADS // 2 and k in (3, 11):
                                top_keys(r, 2 * h + k // 8)
                            if h < HEADS // 2 and k in (7, 15):
                                candidates(r, 2 * h + k // 8)
                            if h == HEADS // 2 and k == 0:
                                centre(r)
                            if h == HEADS // 2 and k in (4, 12):
                                pick_keys(r, k // 8)
                            if h == HEADS // 2 + 1 and k == 0:
                                experts(r)
                            if h == HEADS - 1 and k == 7:
                                gates(r, nth)

                        for h in range(HEADS):
                            for k in range(TOPK):
                                n = h * TOPK + k
                                u = G["u"][n % URING]
                                eng.wait_ge(fl.sem(f"u_landed{n % URING}"), it * (16 * SLOTS // URING) + 16 * (n // URING + 1))
                                v.tensor_tensor_reduce(u, u, G["hb"], 1.0, 0.0, ALU.mult, ALU.add, G["dots"][:, n:n + 1])\
                                    .then_inc(fl.sem("dots_done"), 1)
                                if h and k == 3:
                                    weigh(h - 1)
                                route_part(h, k)
                        v.tensor_copy(G["idxu"], G["idx"]).then_inc(fl.sem("indices_staged"), 1)
                        weigh(HEADS - 1)
                        eng.wait_ge(fl.sem("v_summed"), (it + 1) * SLOTS + 1)
                        for half in range(2):
                            v.tensor_tensor(banks[6 + half][:, :], banks[6 + half][:, :],
                                            G["ga"][:, s * D + half * 512:s * D + half * 512 + 512], ALU.mult)\
                                .then_inc(fl.sem("y_scaled"), 1)
                        eng.wait_ge(fl.sem("y_scaled"), (it + 1) * 2)
                        v.tensor_tensor(X[:, bass.ds(i * D + b0 * D, 512)], X[:, bass.ds(i * D + b0 * D, 512)],
                                        banks[6][:, :], ALU.add).then_inc(fl.sem("half_added"), 1)
                        eng.wait_ge(fl.sem("indices_staged"), routed(l, it + 1) + 1)
                        eng.wait_ge(fl.sem("half_added"), it + 1)
                        v.tensor_tensor(X[:, bass.ds(i * D + (b0 * D + 512), 512)], X[:, bass.ds(i * D + (b0 * D + 512), 512)],
                                        banks[7][:, :], ALU.add).then_inc(fl.sem("residual_added"), 1)
                        eng.wait_ge(fl.sem("residual_added"), it + 2)
            dv.stage("final")
            FG, O1, O2 = work(D, D, D)
            eng.wait_ge(*at("final_g"))
            for t in range(CB, NB):
                eng.wait_ge(*at("ssq2", DEPTH, t))
                v.tensor_scalar(RSQ[:, t:t + 1], SSQ[:, t:t + 1], 1.0 / D, EPS, ALU.mult, ALU.add).then_inc(*dv.step())
                eng.wait_ge(*dv.latest())
                v.reciprocal(RSQ[:, t:t + 1], RSQ[:, t:t + 1]).then_inc(*dv.step("rsq2", DEPTH, t))
                eng.wait_ge(*dv.latest())
                eng.wait_ge(*at("rs2", DEPTH, t))
                v.scalar_tensor_tensor(Xb[:, t, :], Xb[:, t, :], RSB[:, t:t + 1], FG, ALU.mult, ALU.mult).then_inc(*dv.step("result", t))
                eng.wait_ge(*dv.latest())
            dv.finish()

        @block.scalar
        def _(eng):
            sc = Engine(eng, "scalar")
            act = nc.scalar.activation

            def norm_side(tag, l, groups, y, sq, rs):
                for t0, n in out_segs(l):
                    for g, blocks in enumerate(groups):
                        eng.wait_ge(*at(tag + "_centred", l, g, t0))
                        for m in blocks:
                            act(sq(m, t0, n), y(m, t0, n), ACT.Square).then_inc(*sc.step())
                        fl.mark((tag + "_var", l, g, t0), sc.sem)
                for t0, n in out_segs(l):
                    for g, blocks in enumerate(groups):
                        eng.wait_ge(*at("full", (tag, "var", l, g, t0)))
                        b = bank_of((tag, "var", l, g, t0))
                        act(rs(g, t0, n), b[:, 0:n], ACT.Sqrt, bias=EPSC).then_inc(*sc.step(tag + "_root", l, g, t0))
                        fl.mark(("read", (tag, "var", l, g, t0)), sc.sem)

            EPSC = AW_EPS
            sc.stage("mod")
            eng.wait_ge(*at("eps"))
            eng.wait_ge(*at("params"))
            act(SIL, SIL, ACT.Silu).then_inc(*sc.step("silu_c"))
            eng.wait_ge(*sc.latest())

            for l in range(DEPTH):
                sc.stage(("norm", l))
                SQX = work(D, D, D)[2]
                eng.wait_ge(*at("rabs", l))
                act(T8[1], T8[0], ACT.Exp, scale=-1.0).then_inc(*sc.step())
                eng.wait_ge(*sc.latest())
                act(T8[2], T8[1], ACT.Ln, bias=1.0).then_inc(*sc.step("rln", l))
                eng.wait_ge(*sc.latest())
                eng.wait_ge(*at("lg", l))
                for d in range(2):
                    col = const("coldown" if d == 0 else "colup")
                    act(KDEC[:, 4 * d:4 * d + 4], LG[:, 4 * d:4 * d + 4], ACT.Exp, scale=col).then_inc(*sc.step())
                act(CDEC, LG, ACT.Exp, scale=float(P)).then_inc(*sc.step())
                for t in range(NB):
                    act(SQX, Xb[:, t, :], ACT.Square, accum_out=SSQ[:, t:t + 1]).then_inc(*sc.step("ssq", l, t))
                    eng.wait_ge(*sc.latest())
                for t in range(NB):
                    eng.wait_ge(*at("rsq", l, t))
                    act(RSB[:, t:t + 1], RSQ[:, t:t + 1], ACT.Sqrt).then_inc(*sc.step("rs", l, t))
                    eng.wait_ge(*sc.latest())
                    eng.wait_ge(*at("full", ("xT", l, t, 0)))
                    b = bank_of(("xT", l, t, 0))
                    s = 0 if t >= CB else 1
                    eng.wait_ge(*at("sc1", l))
                    for k in range(4):
                        act(HTk[:, k, t * P:(t + 1) * P], b[:, k * P:(k + 1) * P], ACT.Identity,
                                  bias=SH1[:, s * KD + k:s * KD + k + 1], scale=SC1[:, s * KD + k:s * KD + k + 1]).then_inc(*sc.step())
                    fl.mark(("read", ("xT", l, t, 0)), sc.sem)

                sc.stage(("ret", l))
                R = ret_work()
                CP, Y, SG, SQ, RS = conv_work()
                if l:
                    eng.wait_ge(*at("x_parked", l))
                for h in range(2):
                    for m in range(2):
                        for t0, n in out_segs(l):
                            if h:
                                eng.wait_ge(*at("conv_glu", l, 0))
                            eng.wait_ge(*at("full", ("conv_g", l, 2 * h + m, t0)))
                            b = bank_of(("conv_g", l, 2 * h + m, t0))
                            act(SG[:, m, t0:t0 + n], b[:, 0:n], ACT.Sigmoid).then_inc(*sc.step("conv_sg", l, h, m, t0))
                            fl.mark(("read", ("conv_g", l, 2 * h + m, t0)), sc.sem)
                for h in range(NH):
                    act(R["dec"][:, h, :], const("ahead"), ACT.Exp, scale=LG[:, h:h + 1]).then_inc(*sc.step())
                    act(R["dtmp"][:, h, :], const("behind"), ACT.Exp, scale=LG[:, 4 + h:5 + h]).then_inc(*sc.step("rdec", l, h))
                    for d in range(2):
                        act(R["qdec"][:, d, h, :], const("rowup" if d == 0 else "rowdown"), ACT.Exp,
                                  scale=LG[:, 4 * d + h:4 * d + h + 1]).then_inc(*sc.step())
                for tag, scale, dst in (("rk", float(P) ** -0.5, "K"), ("rq", 1.0, "Q")):
                    for m in range(BB):
                        for t0, n in (ALL_SEGS if tag == "rk" else out_segs(l)):
                            eng.wait_ge(*at("full", (tag, l, m, t0)))
                            b = bank_of((tag, l, m, t0))
                            if t0 == 0:
                                act(R[dst][:, m, 0:n], b[:, 0:n], ACT.Copy, scale=scale).then_inc(*sc.step("read", (tag, l, m, t0)))
                            else:
                                if m >= 2:
                                    eng.wait_ge(*at(tag + "_roped", l, m - 2))
                                elif tag == "rq":
                                    eng.wait_ge(*at("rk_roped", l, m + 2))
                                act(R["raw"][:, m % 2, :], b[:, 0:n], ACT.Copy, scale=scale).then_inc(*sc.step(tag + "_raw", l, m))
                                fl.mark(("read", (tag, l, m, t0)), sc.sem)
                norm_side("conv", l, [range(BB)], lambda m, t0, n: Y[:, m, t0:t0 + n],
                          lambda m, t0, n: SQ[:, m, t0:t0 + n],
                          lambda g, t0, n: RS[:, t0:t0 + n])
                for t0, n in out_segs(l):
                    eng.wait_ge(*at("conv_normed", l, 0, t0))
                    for m in range(BB):
                        act(YSb[:, m, t0:t0 + n], Y[:, m, t0:t0 + n], ACT.Silu, bias=par("ln_b")[:, m:m + 1],
                                  scale=par("ln_g")[:, m:m + 1]).then_inc(*sc.step())
                norm_side("ret", l, [[h] for h in range(NH)], lambda m, t0, n: YSb[:, BB + m, t0:t0 + n],
                          lambda m, t0, n: R["sq"][:, m, t0:t0 + n],
                          lambda g, t0, n: R["rs"][:, g, t0:t0 + n])
                for m in range(BB):
                    for t0, n in out_segs(l):
                        eng.wait_ge(*at("full", ("rg", l, m, t0)))
                        b = bank_of(("rg", l, m, t0))
                        act(R["g"][:, m, t0:t0 + n], b[:, 0:n], ACT.Silu).then_inc(*sc.step("rgate", l, m, t0))
                        fl.mark(("read", ("rg", l, m, t0)), sc.sem)

                sc.stage(("mlstm", l))
                M = mlstm_work()
                T, A_, WP, MT, MM, EM = (M[x] for x in ("t", "a", "wp", "mt", "m", "em"))
                eng.wait_ge(*at("mabs", l))
                act(T[0:64, :], T[0:64, :], ACT.Exp, scale=-1.0).then_inc(*sc.step())
                eng.wait_ge(*sc.latest())
                act(T[0:64, :], T[0:64, :], ACT.Ln, bias=1.0).then_inc(*sc.step("mln", l))
                eng.wait_ge(*sc.latest())
                eng.wait_ge(*at("mrowlogs", l))
                act(WP[0:64, :], WP[0:64, :], ACT.Exp).then_inc(*sc.step())
                act(EM[0:64, :], MT[0:64, :], ACT.Exp, scale=-1.0).then_inc(*sc.step("mwrows", l))
                act(A_[64:128, :], T[0:64, :], ACT.Exp).then_inc(*sc.step("mrows", l))
                order_qk = [("mq", m) for m in range(BB)] + [("mk", m) for m in range(BB)]
                eng.wait_ge(*at("mpad0", l))
                for x, (tag, m) in enumerate(order_qk):
                    segs = out_segs(l) if tag == "mq" else ALL_SEGS
                    if x >= 2:
                        ptag, pm = order_qk[x - 2]
                        eng.wait_ge(*at("mconv", l, ptag, pm, SEG_LAT[0]))
                    for t0, n in segs:
                        eng.wait_ge(*at("full", (tag, l, m, t0)))
                        b = bank_of((tag, l, m, t0))
                        o = mpad_at(t0)
                        act(M["pad"][:, x % 2, o:o + n], b[:, 0:n], ACT.Copy).then_inc(*sc.step("mpad", l, tag, m, t0))
                        fl.mark(("read", (tag, l, m, t0)), sc.sem)
                for tag, m in order_qk:
                    for t0, n in (out_segs(l) if tag == "mq" else ALL_SEGS):
                        eng.wait_ge(*at("mconv", l, tag, m, t0))
                        dst = M["Q" if tag == "mq" else "K"][:, m, t0:t0 + n]
                        act(dst, dst, ACT.Silu).then_inc(*sc.step())
                fl.mark(("msilu", l), sc.sem)
                for n_ in range(NB):
                    for d in range(2):
                        c = scan_order(d)[n_]
                        if c in out_blocks(l):
                            eng.wait_ge(*at("mlogw", l, d, c))
                            act(M["e"][d], M["e"][d], ACT.Exp, scale=-1.0).then_inc(*sc.step("mexp", l, d, c))
                norm_side("mls", l, [[h] for h in range(NH)], lambda m, t0, n: YSb[:, 2 * BB + m, t0:t0 + n],
                          lambda m, t0, n: M["sq"][:, m, t0:t0 + n],
                          lambda g, t0, n: M["rs"][:, g, t0:t0 + n])
                for m in range(BB):
                    for t0, n in out_segs(l):
                        eng.wait_ge(*at("full", ("mo", l, m, t0)))
                        b = bank_of(("mo", l, m, t0))
                        act(M["g"][:, m, t0:t0 + n], b[:, 0:n], ACT.Sigmoid).then_inc(*sc.step("mogate", l, m, t0))
                        fl.mark(("read", ("mo", l, m, t0)), sc.sem)

                sc.stage(("attn", l))
                A = attn_work()
                for tag, nbk in (("ak", 1), ("aq", BB)):
                    for m in range(nbk):
                        for t0, n in (ALL_SEGS if tag == "ak" else out_segs(l)):
                            eng.wait_ge(*at("full", (tag, l, m, t0)))
                            b = bank_of((tag, l, m, t0))
                            if t0 == 0:
                                dst = A["K"][:, 0:n] if tag == "ak" else A["Q"][:, m, 0:n]
                                act(dst, b[:, 0:n], ACT.Copy).then_inc(*sc.step("read", (tag, l, m, t0)))
                            else:
                                if m >= 2:
                                    eng.wait_ge(*at("aq_roped", l, m - 2))
                                elif tag == "aq":
                                    eng.wait_ge(*at("ak_roped", l, 0))
                                act(A["raw"][:, m % 2, :], b[:, 0:n], ACT.Copy).then_inc(*sc.step(tag + "_raw", l, m))
                                fl.mark(("read", (tag, l, m, t0)), sc.sem)
                seq_th = [(t, h) for t in out_blocks(l) for h in range(AH)]
                MX, NM, SE, DN, RC, SUM = AW
                for x in range(len(seq_th) + 2):
                    if x < len(seq_th):
                        t, h = seq_th[x]
                        n = len(local_blocks(t)) * P + CTX
                        eng.wait_ge(*at("anm", l, t, h))
                        if x >= 2:
                            eng.wait_ge(*at("full", ("apc", l) + seq_th[x - 2]))
                        act(A["P"][:, h % 2, 0:n], A["S"][:, h % 2, 0:n], ACT.Exp, bias=NM[:, h:h + 1],
                            accum_out=SUM[:, h:h + 1]).then_inc(*sc.step("ap", l, t, h))
                        act(SE[:, h:h + 1], SINK[:, h:h + 1], ACT.Exp, bias=NM[:, h:h + 1]).then_inc(*sc.step("aexp", l, t, h))
                    if 1 <= x <= len(seq_th):
                        t, h = seq_th[x - 1]
                        nl = len(local_blocks(t)) * P
                        if nl:
                            if x >= 3:
                                eng.wait_ge(*at("full", ("ay", l) + seq_th[x - 3]))
                            eng.wait_ge(*at("full", ("apl", l, t, h)))
                            b = bank_of(("apl", l, t, h))
                            act(A["PT"][:, h % 2, 0:nl], b[:, 0:nl], ACT.Copy).then_inc(*sc.step("apl_moved", l, t, h))
                            fl.mark(("read", ("apl", l, t, h)), sc.sem)
                    if x >= 2 and seq_th[x - 2][1] == AH - 1:
                        t = seq_th[x - 2][0]
                        eng.wait_ge(*at("full", ("ayT", l, t)))
                        b = bank_of(("ayT", l, t))
                        act(YSb[:, 3 * BB:4 * BB, t * P:(t + 1) * P], b[:, :].rearrange("p (m i) -> p m i", m=BB), ACT.Copy)\
                            .then_inc(*sc.step("read", ("ayT", l, t)))

                sc.stage(("merge", l))
                GS = merge_work()[1]
                hist = []
                for j in range(D // W):
                    for i_ in range(4):
                        for m in range(2):
                            for t0, n in out_segs(l):
                                if len(hist) >= 4:
                                    eng.wait_ge(*at("read", ("branch",) + hist[-4]))
                                hist.append((l, j, i_, m, t0))
                                eng.wait_ge(*at("full", ("gate", l, j, i_, m, t0)))
                                b = bank_of(("gate", l, j, i_, m, t0))
                                act(GS[:, gslot(l, j, i_, m, t0), 0:n], b[:, 0:n], ACT.Sigmoid).then_inc(*sc.step("gsig", l, j, i_, m, t0))
                                fl.mark(("read", ("gate", l, j, i_, m, t0)), sc.sem)

                sc.stage(("out", l))
                SQX = out_work()[4]

                def moved_hT(t):
                    eng.wait_ge(*at("full", ("hT", l, t, 0)))
                    b = bank_of(("hT", l, t, 0))
                    act(HTk[:, 0:4, t * P:(t + 1) * P], b[:, :].rearrange("p (k i) -> p k i", k=4), ACT.Copy).then_inc(*sc.step("read", ("hT", l, t, 0)))

                for t in out_blocks(l):
                    eng.wait_ge(*at("added", l, D // W - 1, t))
                    act(SQX, Xb[:, t, :], ACT.Square, accum_out=SSQ[:, t:t + 1]).then_inc(*sc.step("ssq2", l, t))
                    eng.wait_ge(*sc.latest())
                    eng.wait_ge(*at("rsq2", l, t))
                    act(RSB[:, t:t + 1], RSQ[:, t:t + 1], ACT.Sqrt).then_inc(*sc.step("rs2", l, t))
                    if t > out_blocks(l)[0]:
                        moved_hT(t - 1)
                moved_hT(NB - 1)

                G = peer_work()

                def scores_moved(t):
                    x = t - out_blocks(l)[0]
                    s = G["sf"] if x == 0 else STORE[:, (x - 1) * NSCORE:x * NSCORE]
                    for g in range(4):
                        eng.wait_ge(*at("full", ("score", l, t, g)))
                        b = bank_of(("score", l, t, g))
                        act(s[:, g * 512:(g + 1) * 512], b[:, :], ACT.Copy).then_inc(*sc.step("scored", l, t, g))
                        fl.mark(("read", ("score", l, t, g)), sc.sem)

                def query_moved(part, c):
                    for t0, n in q_segs(l, part):
                        eng.wait_ge(*at("full", (f"wq{part}", l, c, t0)))
                        b = bank_of((f"wq{part}", l, c, t0))
                        act(YSb[:, c, t0:t0 + n], b[:, 0:n], ACT.Copy).then_inc(*sc.step("read", (f"wq{part}", l, c, t0)))

                sc.stage(("peerq", l))
                for h in range(HEADS):
                    query_moved(0, 2 * h)
                scores_moved(out_blocks(l)[0])
                for c in range(2 * HEADS):
                    query_moved(1, c)
                    if c == 2 * HEADS - 3:
                        eng.wait_ge(fl.sem("scores_centred"), routed(l, peer_calls(l)[0][2]) + 1)
                        act(G["ce"], G["ce"], ACT.Exp).then_inc(fl.sem("scores_exp"), 1)
                sc.stage(("route", l))
                for t in out_blocks(l)[1:]:
                    scores_moved(t)

                sc.stage(("peer", l))
                G = peer_work()
                for b0, nb, base in peer_calls(l):
                    with eng.Fori(0, nb) as i:
                        it = i + base

                        def gelu(h):
                            hs = slice(h * TOPK, (h + 1) * TOPK)
                            eng.wait_ge(fl.sem("dots_done"), it * SLOTS + (h + 1) * TOPK + 1)
                            act(G["act"][:, hs], G["dots"][:, hs], ACT.Gelu).then_inc(fl.sem("gelu_done"), 1)

                        def diagonals(h):
                            eng.wait_ge(fl.sem("weights_ready"), it * HEADS + h + 1)
                            for k in range(TOPK):
                                n = h * TOPK + k
                                if n >= DRING:
                                    eng.wait_ge(fl.sem("v_summed"), it * SLOTS + n - DRING + 2)
                                act(G["diag"][:, n % DRING, :], ident, ACT.Copy, scale=G["w"][:, n:n + 1])\
                                    .then_inc(fl.sem("diagonal_ready"), 1)

                        gelu(0)
                        for h in range(HEADS):
                            diagonals(h)
                            if h < HEADS - 1:
                                gelu(h + 1)
                            if h == HEADS - 3:
                                eng.wait_ge(fl.sem("scores_centred"), routed(l, it + 1) + 1)
                                act(G["ce"], G["ce"], ACT.Exp).then_inc(fl.sem("scores_exp"), 1)
            sc.stage("final")
            SQX = YS[:, 0:D]
            for t in range(CB, NB):
                act(SQX, Xb[:, t, :], ACT.Square, accum_out=SSQ[:, t:t + 1]).then_inc(*sc.step("ssq2", DEPTH, t))
                eng.wait_ge(*sc.latest())
            for t in range(CB, NB):
                eng.wait_ge(*at("rsq2", DEPTH, t))
                act(RSB[:, t:t + 1], RSQ[:, t:t + 1], ACT.Sqrt).then_inc(*sc.step("rs2", DEPTH, t))
                eng.wait_ge(*sc.latest())
            sc.finish()

        @block.gpsimd
        def _(eng):
            po = Engine(eng, "gpsimd")
            po.stage("mod")
            for name in ("dots_done", "v_summed", "residual_added"):
                eng.sem_inc(fl.sem(name), 1)
            fl.done(nc.gpsimd.memset(AW_EPS, EPS), "eps_set", ("eps",))
            fl.done(nc.gpsimd.memset(GB, 0.0), "gb_zero", ("gb_zero",))
            MR, MB = work(6 * D, 6 * D)

            def dma(dst, src, sem, step=None):
                fl.done(eng.dma_start(dst, src), sem, step, by=16)

            for l in range(DEPTH):
                if l:
                    eng.wait_ge(*at("mod_rows", l - 1))
                dma(MB[0:2, :], ins["mod_b"][l:l + 1, :].to_broadcast([2, 6 * D]), "mod_bias_loaded", ("mod_b", l))
                eng.wait_ge(*at("mod_rows", l))
                dma(modr[l], MR[0:2, :], "mod_rows_stored", ("mod_stored", l))
            eng.wait_ge(*at("mod_stored", DEPTH - 1))
            eng.sem_inc(*po.step())
            for l in range(DEPTH):
                po.stage(("norm", l))
                po.stage(("ret", l))
                if l:
                    dma(ins["parked"].rearrange("b p d -> p b d"), Xb[:, CB:NB, :], "x_parked", ("x_parked", l))
                po.stage(("mlstm", l))
                M = mlstm_work()
                if l == 0:
                    eng.wait_ge(*at("gb_zero"))
                for x, (kind, p0) in enumerate(((0, 0), (2, 32))):
                    dma(GB[p0:p0 + 4, 0:1], ins["mlstm_gate_b"][l, kind].rearrange("(h o) -> h o", o=1), "gate_bias_loaded")
                    dma(GB[64 + p0:64 + p0 + 4, 1:2], ins["mlstm_gate_b"][l, kind + 1].rearrange("(h o) -> h o", o=1),
                        "gate_bias_loaded")
                fl.mark(("gate_bias", l), "gate_bias_loaded")
                eng.wait_ge(*at("mwrows", l))
                for d in range(2):
                    for kind, rows in enumerate((M["m"], M["wp"], M["em"])):
                        dma(rowsd[d, :, kind].rearrange("c (h i) -> h c i", h=NH),
                            rows[32 * d:32 * d + 4, :].rearrange("h (c i) -> h c i", c=NB), "rows_stored")
                fl.mark(("rows_stored", l), "rows_stored")
                eng.wait_ge(*at("rows_stored", l))
                for n_ in range(NB):
                    for d in range(2):
                        c = scan_order(d)[n_]
                        if n_:
                            eng.wait_ge(*at("mbc_used", l, d, scan_order(d)[n_ - 1]))
                        else:
                            eng.wait_ge(*at("full", ("mcols", l, NB - 1)))
                        dma(M["bc"][:, d, :], rowsd[d:d + 1, c].rearrange("o k n -> o (k n)").partition_broadcast(P)
                            .rearrange("p o n -> p (o n)"), f"row_copies_loaded{d}", ("mbc", l, d, c))
                po.stage(("attn", l))
                po.stage(("merge", l))
                po.stage(("out", l))
                po.stage(("peerq", l))
                po.stage(("route", l))
                po.stage(("peer", l))
                G = peer_work()
                utab = ins["peer_u"]
                vtab = ins["peer_v"]
                for b0, nb, base in peer_calls(l):
                    with eng.Fori(0, nb) as i:
                        it = i + base
                        eng.wait_ge(fl.sem("indices_staged"), routed(l, it) + 1)
                        eng.wait_ge(fl.sem("dots_done"), it * SLOTS + 1)
                        eng.sem_inc(fl.sem("gathers_allowed"), 1)
                        for h in range(HEADS + 1):
                            if h == 1:
                                eng.wait_ge(fl.sem("v_indices_staged"), it + 1)
                                eng.wait_ge(fl.sem("v_summed"), it * SLOTS + 1)
                                eng.sem_inc(fl.sem("gathers_allowed"), 1)
                            for k in range(TOPK):
                                n = h * TOPK + k
                                if h < HEADS:
                                    if n >= URING:
                                        eng.wait_ge(fl.sem("dots_done"), it * SLOTS + n - URING + 2)
                                        eng.sem_inc(fl.sem("gathers_allowed"), 1)
                                    eng.indirect_dma_start(G["u"][n % URING], None, utab,
                                                           bass.IndirectOffsetOnAxis(G["idxu"][:, n:n + 1], 0))\
                                        .then_inc(fl.sem(f"u_landed{n % URING}"), 16)
                                if h:
                                    n -= TOPK
                                    if n >= VRING:
                                        eng.wait_ge(fl.sem("v_summed"), it * SLOTS + n - VRING + 2)
                                        eng.sem_inc(fl.sem("gathers_allowed"), 1)
                                    eng.indirect_dma_start(G["v"][n % VRING], None, vtab,
                                                           bass.IndirectOffsetOnAxis(G["idxv"][:, n:n + 1], 0))\
                                        .then_inc(fl.sem(f"v_landed{n % VRING}"), 16)
            po.stage("final")
            po.finish()

        @block.sync
        def _(eng):
            def dma(dst, src, sem, step=None, slow=False):
                fl.done(eng.dma_start(dst, src, allow_slow_non_contiguous=slow), sem, step, by=16)

            dma(CT, ins["consts"], "params_loaded")
            dma(Xb[:, 0:CB, :], ins["ctx"][0].rearrange("(b p) d -> p b d", p=P), "params_loaded")
            dma(Xb[:, CB:NB, :], ins["x"][0].rearrange("(b p) d -> p b d", p=P), "params_loaded")
            dma(SIL, ins["cvec"], "params_loaded")
            fl.mark(("params",), "params_loaded")

            def layer_vectors(l):
                if l:
                    for e in ENG:
                        eng.wait_ge(*at("end", e, ("route", l - 1)))
                eng.wait_ge(*at("mod_stored", l))
                if l == 0:
                    eng.wait_ge(*at("mod_stored", 0))
                dma(PR, ins["params"][l], "layer_loaded")
                dma(LG, ins["ret_decay"][l].rearrange("(o d) h -> o (d h)", o=1).to_broadcast([P, 8]), "layer_loaded")
                dma(SINK, ins["attn_sink"][l:l + 1, :].to_broadcast([P, AH]), "layer_loaded")
                dma(KEYT, ins["keysT"][l], "layer_loaded")
                for s in range(2):
                    for dst, part in ((SH1, 0), (SC1, 1)):
                        dma(dst[:, s * KD:(s + 1) * KD], modr[l, s, part * D:(part + 1) * D].rearrange("(k p) -> p k", p=P),
                            "layer_loaded", slow=True)
                fl.mark(("layer", l), "layer_loaded")

            for n, (name, parts) in enumerate(PLAN):
                if n >= RING:
                    eng.wait_ge(*at("used", PLAN[n - RING][0]))
                for dst, src in parts:
                    dma(dst(WRr[:, n % RING, :]), src, f"weights_loaded{n % RING}")
                fl.mark(("loaded", name), f"weights_loaded{n % RING}")
                l = name[1]
                if name[0] == "mod" and l == DEPTH - 1 and name[2] == 6 * D // W - 1:
                    layer_vectors(0)
                if name == ("branch", l, 0, 3):
                    for e in ENG:
                        eng.wait_ge(*at("end", e, ("attn", l)))
                    GA = merge_work()[3]
                    for s in range(2):
                        dma(GA[:, s * D:(s + 1) * D], modr[l, s:s + 1, 2 * D:3 * D].to_broadcast([P, D]), "ga1_loaded")
                    if l == 0:
                        dma(Xb[:, 0:CB, :], ins["ctx"][0].rearrange("(b p) d -> p b d", p=P), "ga1_loaded")
                        dma(Xb[:, CB:NB, :], ins["x"][0].rearrange("(b p) d -> p b d", p=P), "ga1_loaded")
                    else:
                        dma(Xb[:, CB:NB, :], ins["parked"].rearrange("b p d -> p b d"), "ga1_loaded")
                    fl.mark(("ga1", l), "ga1_loaded")
                if name == ("out", l, D // W - 1):
                    for e in ENG:
                        eng.wait_ge(*at("end", e, ("merge", l)))
                    _, SC2, SH2, G2, _ = out_work()
                    for s in range(2):
                        dma(SC2[:, s * D:(s + 1) * D], modr[l, s:s + 1, 4 * D:5 * D].to_broadcast([P, D]), "mod2_loaded")
                        dma(SH2[:, s * D:(s + 1) * D], modr[l, s:s + 1, 3 * D:4 * D].to_broadcast([P, D]), "mod2_loaded")
                    dma(G2, ins["norm2_g"][l:l + 1, :].to_broadcast([P, D]), "mod2_loaded")
                    fl.mark(("mod2", l), "mod2_loaded")
                if name == ("wq1", l, HEADS * 256 // W - 1):
                    for e in ENG:
                        eng.wait_ge(*at("end", e, ("peerq", l)))
                    G = peer_work()
                    for s in range(2):
                        dma(G["ga"][:, s * D:(s + 1) * D], modr[l, s:s + 1, 5 * D:6 * D].to_broadcast([P, D]), "ga2_loaded")
                    fl.mark(("ga2", l), "ga2_loaded")
                    if l + 1 < DEPTH:
                        layer_vectors(l + 1)
                        for e in ENG:
                            eng.wait_ge(*at("end", e, ("peer", l)))
            for e in ENG:
                eng.wait_ge(*at("end", e, ("peer", DEPTH - 1)))
            dma(work(D)[0], ins["final_g"].rearrange("(o d) -> o d", o=1).to_broadcast([P, D]), "final_g_loaded", ("final_g",))
            for t in range(CB, NB):
                eng.wait_ge(*at("result", t))
                dma(out[0, (t - CB) * P:(t - CB + 1) * P, :], Xb[:, t, :], "result_stored")
            fl.mark(("stored",), "result_stored")
            if known is not None:
                eng.wait_ge(fl.sem("result_stored"), fl.count["result_stored"])
        fl.marks["banks"] = dict(banks_of)
        return fl.marks


def program(nc, ins, out, known):
    scratch = {"parked": nc.dram_tensor("parked", (NB - CB, P, D), F32).ap(),
               "mod_rows": nc.dram_tensor("mod_rows", (DEPTH, 2, 6 * D), F32).ap(),
               "mlstm_rows": nc.dram_tensor("mlstm_rows", (2, NB, 3, BR), F32).ap()}
    return build(nc, {**ins, **scratch}, out, known)


def _arrays(i):
    def chan(a):
        a = np.atleast_2d(a)
        return a.T.reshape(-1, P, a.shape[0]).transpose(1, 0, 2).reshape(P, -1)

    f = {k: np.ascontiguousarray(v) for k, v in i.items()}
    params = np.stack([np.concatenate([chan(f["norm1_g"][l]), chan(f["conv_w"][l]), chan(f["conv_b"][l]),
                                       chan(f["conv_ln_g"][l]), chan(f["conv_ln_b"][l]), chan(f["mlstm_conv_w"][l]),
                                       chan(f["mlstm_conv_b"][l])], axis=1) for l in range(DEPTH)])
    a = {k: f[k] for k in ("x", "ctx", "mod_w", "mod_b", "w_in", "ret_decay", "mlstm_gate_b", "attn_sink", "w_branch",
                           "w_out", "peer_wq", "norm2_g", "final_g")}
    a["cvec"] = chan(np.stack([f["c"][0], f["c_ctx"]]))
    a["params"] = params
    a["keysT"] = f["peer_keys"].transpose(0, 3, 1, 2).reshape(DEPTH, P, 2 * KEYS)
    a["peer_u"] = f["peer_u"].reshape(DEPTH * EXPERTS, D)
    a["peer_v"] = f["peer_v"].reshape(DEPTH * EXPERTS, D)
    a["consts"] = const_table()
    return {k: np.ascontiguousarray(v) for k, v in a.items()}


def kernel(**inputs):
    import concourse.bacc as bacc
    from concourse.bass_utils import run_bass_kernel_spmd as run

    arrays = _arrays(inputs)
    known = None
    for _ in range(2):
        nc = bacc.Bacc("TRN2", target_bir_lowering=False, num_devices=1)
        ins = {k: nc.dram_tensor(f"in_{k}", a.shape, F32, kind="ExternalInput").ap() for k, a in arrays.items()}
        out = nc.dram_tensor("out_0", (1, LAT, D), F32, kind="ExternalOutput").ap()
        known = program(nc, ins, out, known)
    r = run(nc, [{f"in_{k}": a for k, a in arrays.items()}], core_ids=[0])
    return r.results[0]["out_0"]
```
